# Optimizing a Trainium2 kernel written in Bass

```python
import math
import jax, jax.numpy as jnp
from jax import lax
import numpy as np

D_MODEL = 1024
BATCH = 1
SEQ = 256
DEPTH = 2

N_MIXERS = 2
N_ATTN_LAYERS = (DEPTH + 1) // 2
N_HGRN_LAYERS = DEPTH // 2

ATT_HEADS = 16
ATT_HEAD_DIM = 64
ATT_KV_HEADS = 2
Q_LORA_RANK = 256
IDX_HEADS = 8
IDX_DIM = 128
INDEX_TOPK = 256
Q_BLOCK = 128
ATT_KV_DIM = ATT_KV_HEADS * ATT_HEAD_DIM
ATT_IN_DIM = Q_LORA_RANK + 2 * ATT_KV_DIM + IDX_DIM + IDX_HEADS

HGRN_EXPAND = 128
HGRN_HEADS = D_MODEL // HGRN_EXPAND
HGRN_F_DIM = HGRN_HEADS * HGRN_EXPAND
HGRN_V_DIM = D_MODEL // HGRN_HEADS
HGRN_CHUNK = 64
HGRN_IN_DIM = 2 * HGRN_F_DIM + D_MODEL + D_MODEL

D_FF = -(-8 * D_MODEL // (3 * 256)) * 256

ROPE_THETA = 500000.0
ATT_ROT_DIM = ATT_HEAD_DIM // 4
IDX_ROT_DIM = IDX_DIM // 4
DEEPNORM_ALPHA = (2 * DEPTH) ** 0.25
DEEPNORM_BETA = (8 * DEPTH) ** -0.25
LN_EPS = 1e-5
RMS_EPS = 1e-6


def layer_norm(x, g, b):
    xf = x.astype(jnp.float32)
    mu = jnp.mean(xf, axis=-1, keepdims=True)
    var = jnp.mean(jnp.square(xf - mu), axis=-1, keepdims=True)
    return ((xf - mu) * lax.rsqrt(var + LN_EPS) * g.astype(jnp.float32) + b.astype(jnp.float32)).astype(x.dtype)

def rms_norm(x, g):
    xf = x.astype(jnp.float32)
    ms = jnp.mean(jnp.square(xf), axis=-1, keepdims=True)
    return (xf * lax.rsqrt(ms + RMS_EPS) * g.astype(jnp.float32)).astype(x.dtype)

def rope_tables(positions, rot_dim):
    inv = ROPE_THETA ** (-jnp.arange(0, rot_dim, 2, dtype=jnp.float32) / rot_dim)
    ang = positions.astype(jnp.float32)[..., None] * inv
    return jnp.cos(ang), jnp.sin(ang)

def apply_rope(x, cos, sin):
    half = cos.shape[-1]
    cos = cos.astype(x.dtype)
    sin = sin.astype(x.dtype)
    x1 = x[..., :half]
    x2 = x[..., half:2 * half]
    return jnp.concatenate([x1 * cos - x2 * sin, x2 * cos + x1 * sin, x[..., 2 * half:]], axis=-1)

def dsa_mixer(x, cos_q, sin_q, cos_i, sin_i, w_in, g_cq, w_uq, w_iq, g_ik, b_ik, w_o):
    B, T, _ = x.shape
    dt = x.dtype
    h = x @ w_in
    c_q, k, v, k_idx, w_idx = jnp.split(
        h, [Q_LORA_RANK, Q_LORA_RANK + ATT_KV_DIM, Q_LORA_RANK + 2 * ATT_KV_DIM,
            Q_LORA_RANK + 2 * ATT_KV_DIM + IDX_DIM], axis=-1)
    c_q = rms_norm(c_q, g_cq)
    q = (c_q @ w_uq).reshape(B, T, ATT_HEADS, ATT_HEAD_DIM)
    q_idx = (c_q @ w_iq).reshape(B, T, IDX_HEADS, IDX_DIM)
    k = k.reshape(B, T, ATT_KV_HEADS, ATT_HEAD_DIM)
    v = v.reshape(B, T, ATT_KV_HEADS, ATT_HEAD_DIM)
    k_idx = layer_norm(k_idx, g_ik, b_ik)
    q = apply_rope(q, cos_q[:, :, None], sin_q[:, :, None])
    k = apply_rope(k, cos_q[:, :, None], sin_q[:, :, None])
    q_idx = apply_rope(q_idx, cos_i[:, :, None], sin_i[:, :, None])
    k_idx = apply_rope(k_idx, cos_i, sin_i)
    w_idx = w_idx * (IDX_HEADS ** -0.5 * IDX_DIM ** -0.5)

    topk = min(INDEX_TOPK, T // 4)
    nb = T // Q_BLOCK
    group = ATT_HEADS // ATT_KV_HEADS
    key_pos = jnp.arange(T)

    def blocks(a):
        return jnp.moveaxis(a.reshape(B, nb, Q_BLOCK, *a.shape[2:]), 1, 0)

    def attend_block(args):
        qb, qib, wb, start = args
        t_pos = start + jnp.arange(Q_BLOCK)
        causal = key_pos[None, :] <= t_pos[:, None]
        rel = jax.nn.relu(jnp.einsum('bqhd,bsd->bhqs', qib, k_idx))
        score = jnp.einsum('bqh,bhqs->bqs', wb, rel).astype(jnp.float32)
        score = jnp.where(causal[None], score, -jnp.inf)
        _, sel = lax.top_k(score, topk)
        valid = sel <= t_pos[None, :, None]
        k_sel = jax.vmap(lambda kk, ii: kk[ii])(k, sel)
        v_sel = jax.vmap(lambda vv, ii: vv[ii])(v, sel)
        qg = qb.reshape(B, Q_BLOCK, ATT_KV_HEADS, group, ATT_HEAD_DIM)
        logits = jnp.einsum('bqgrd,bqkgd->bqgrk', qg, k_sel).astype(jnp.float32) * (ATT_HEAD_DIM ** -0.5)
        logits = jnp.where(valid[:, :, None, None, :], logits, -jnp.inf)
        p = jax.nn.softmax(logits, axis=-1).astype(dt)
        o = jnp.einsum('bqgrk,bqkgd->bqgrd', p, v_sel)
        return o.reshape(B, Q_BLOCK, ATT_HEADS * ATT_HEAD_DIM)

    out = lax.map(attend_block, (blocks(q), blocks(q_idx), blocks(w_idx), jnp.arange(nb) * Q_BLOCK))
    out = jnp.moveaxis(out, 0, 1).reshape(B, T, ATT_HEADS * ATT_HEAD_DIM)
    return out @ w_o

def chunk_gated_linear(q, k, v, logf):
    B, H, T, K = q.shape
    V = v.shape[-1]
    C = HGRN_CHUNK
    nc = T // C
    mask = jnp.tril(jnp.ones((C, C), dtype=bool))

    def to_chunks(a):
        return jnp.moveaxis(a.reshape(B, H, nc, C, a.shape[-1]), 2, 0)

    def step(S, inp):
        qc, kc, vc, gc = inp
        b = jnp.cumsum(gc, axis=-2)
        diff = b[..., :, None, :] - b[..., None, :, :]
        decay = jnp.exp(jnp.where(mask[:, :, None], diff, -jnp.inf))
        attn = jnp.einsum('bhtsk,bhsk->bhts', decay * qc[..., :, None, :], kc)
        o = jnp.einsum('bhts,bhsv->bhtv', attn, vc) + jnp.einsum('bhtk,bhkv->bhtv', qc * jnp.exp(b), S)
        b_last = b[..., -1:, :]
        S = jnp.exp(b_last[..., 0, :])[..., None] * S + jnp.einsum('bhsk,bhsv->bhkv', kc * jnp.exp(b_last - b), vc)
        return S, o

    S0 = jnp.zeros((B, H, K, V), jnp.float32)
    _, o = lax.scan(step, S0, (to_chunks(q), to_chunks(k), to_chunks(v), to_chunks(logf)))
    return jnp.moveaxis(o, 0, 2).reshape(B, H, T, V)

def hgrn2_mixer(x, lb, w_in, g_norm, w_o):
    B, T, _ = x.shape
    dt = x.dtype
    h = x @ w_in
    q, f, i, g = jnp.split(h, [HGRN_F_DIM, 2 * HGRN_F_DIM, 2 * HGRN_F_DIM + D_MODEL], axis=-1)
    q = jax.nn.silu(q.astype(jnp.float32))
    fg = lb + (1.0 - lb) * jax.nn.sigmoid(f.astype(jnp.float32))
    k = 1.0 - fg
    logf = jnp.log(fg)

    def heads(a, d):
        return jnp.transpose(a.reshape(B, T, HGRN_HEADS, d), (0, 2, 1, 3))

    o = chunk_gated_linear(heads(q, HGRN_EXPAND), heads(k, HGRN_EXPAND),
                           heads(i.astype(jnp.float32), HGRN_V_DIM), heads(logf, HGRN_EXPAND))
    o = jnp.transpose(o, (0, 2, 1, 3))
    o = rms_norm(o, g_norm) * jax.nn.silu(g.astype(jnp.float32).reshape(B, T, HGRN_HEADS, HGRN_V_DIM))
    return o.reshape(B, T, D_MODEL).astype(dt) @ w_o

def swiglu(x, w_gate, w_up, w_down):
    return (jax.nn.silu(x @ w_gate) * (x @ w_up)) @ w_down

def first_inputs(seed: int = 0) -> dict:
    key = jax.random.key(seed)
    ks = jax.random.split(key, 32)
    f32 = jnp.float32
    nA, nB, D = N_ATTN_LAYERS, N_HGRN_LAYERS, D_MODEL

    def nrm(k, shape, fan_in, scale=1.0):
        return jax.random.normal(k, shape, f32) * (fan_in ** -0.5) * scale

    x = jax.random.normal(ks[0], (BATCH, SEQ, D), f32)
    offset = jax.random.randint(ks[1], (BATCH, 1), 0, 1024, dtype=jnp.int32)
    positions = offset + jnp.arange(SEQ, dtype=jnp.int32)[None, :]

    att_w_in = jnp.concatenate([
        nrm(ks[2], (nA, D, Q_LORA_RANK), D),
        nrm(ks[3], (nA, D, ATT_KV_DIM), D),
        nrm(ks[4], (nA, D, ATT_KV_DIM), D, DEEPNORM_BETA),
        nrm(ks[5], (nA, D, IDX_DIM), D),
        nrm(ks[6], (nA, D, IDX_HEADS), D)], axis=-1)
    att_g_cq = 1.0 + 0.02 * jax.random.normal(ks[7], (nA, Q_LORA_RANK), f32)
    att_w_uq = nrm(ks[8], (nA, Q_LORA_RANK, ATT_HEADS * ATT_HEAD_DIM), Q_LORA_RANK)
    att_w_iq = nrm(ks[9], (nA, Q_LORA_RANK, IDX_HEADS * IDX_DIM), Q_LORA_RANK)
    att_g_ik = 1.0 + 0.02 * jax.random.normal(ks[10], (nA, IDX_DIM), f32)
    att_b_ik = 0.02 * jax.random.normal(ks[11], (nA, IDX_DIM), f32)
    att_w_o = nrm(ks[12], (nA, ATT_HEADS * ATT_HEAD_DIM, D), ATT_HEADS * ATT_HEAD_DIM, DEEPNORM_BETA)

    hgrn_lb_logits = 0.5 * jax.random.normal(ks[13], (DEPTH, HGRN_F_DIM), f32)
    hgrn_w_in = jnp.concatenate([
        nrm(ks[14], (nB, D, HGRN_F_DIM), D),
        nrm(ks[15], (nB, D, HGRN_F_DIM), D),
        nrm(ks[16], (nB, D, D), D, DEEPNORM_BETA),
        nrm(ks[17], (nB, D, D), D)], axis=-1)
    hgrn_g_norm = 1.0 + 0.02 * jax.random.normal(ks[18], (nB, HGRN_V_DIM), f32)
    hgrn_w_o = nrm(ks[19], (nB, D, D), D, DEEPNORM_BETA)

    ffn_w_gate = nrm(ks[20], (DEPTH, D, D_FF), D, DEEPNORM_BETA)
    ffn_w_up = nrm(ks[21], (DEPTH, D, D_FF), D, DEEPNORM_BETA)
    ffn_w_down = nrm(ks[22], (DEPTH, D_FF, D), D_FF, DEEPNORM_BETA)

    ln_g = 1.0 + 0.02 * jax.random.normal(ks[23], (DEPTH, 2, D), f32)
    ln_b = 0.02 * jax.random.normal(ks[24], (DEPTH, 2, D), f32)

    return {"x": x, "positions": positions,
            "att_w_in": att_w_in, "att_g_cq": att_g_cq, "att_w_uq": att_w_uq, "att_w_iq": att_w_iq,
            "att_g_ik": att_g_ik, "att_b_ik": att_b_ik, "att_w_o": att_w_o,
            "hgrn_lb_logits": hgrn_lb_logits, "hgrn_w_in": hgrn_w_in, "hgrn_g_norm": hgrn_g_norm,
            "hgrn_w_o": hgrn_w_o,
            "ffn_w_gate": ffn_w_gate, "ffn_w_up": ffn_w_up, "ffn_w_down": ffn_w_down,
            "ln_g": ln_g, "ln_b": ln_b}

def first_block(x, positions, att_w_in, att_g_cq, att_w_uq, att_w_iq, att_g_ik, att_b_ik, att_w_o,
              hgrn_lb_logits, hgrn_w_in, hgrn_g_norm, hgrn_w_o,
              ffn_w_gate, ffn_w_up, ffn_w_down, ln_g, ln_b):
    cos_q, sin_q = rope_tables(positions, ATT_ROT_DIM)
    cos_i, sin_i = rope_tables(positions, IDX_ROT_DIM)
    lb_all = jnp.cumsum(jax.nn.softmax(hgrn_lb_logits.astype(jnp.float32), axis=0), axis=0)
    lb_all = lb_all - lb_all[0]
    h = x
    for layer in range(DEPTH):
        j = layer // N_MIXERS
        if layer % N_MIXERS == 0:
            mix = dsa_mixer(h, cos_q, sin_q, cos_i, sin_i, att_w_in[j], att_g_cq[j], att_w_uq[j],
                            att_w_iq[j], att_g_ik[j], att_b_ik[j], att_w_o[j])
        else:
            mix = hgrn2_mixer(h, lb_all[layer], hgrn_w_in[j], hgrn_g_norm[j], hgrn_w_o[j])
        h = layer_norm(DEEPNORM_ALPHA * h + mix, ln_g[layer, 0], ln_b[layer, 0])
        ffn = swiglu(h, ffn_w_gate[layer], ffn_w_up[layer], ffn_w_down[layer])
        h = layer_norm(DEEPNORM_ALPHA * h + ffn, ln_g[layer, 1], ln_b[layer, 1])
    return h


DEPTH_2 = 1

CHUNK = 64

GLA_HEADS = 4
GLA_DK = 128
GLA_DV = 256
GLA_LOWRANK = 16
GLA_GATE_TEMP = 16.0

MLA_HEADS = 8
MLA_Q_LORA = 384
MLA_KV_LORA = 256
MLA_NOPE = 128
MLA_ROPE = 64
MLA_V = 128
ROPE_THETA_2 = 10000.0

D_FF_2 = ((8 * D_MODEL // 3 + 255) // 256) * 256

NORM_EPS = 1e-6

IN_SPLITS = (
    GLA_HEADS * GLA_DK,
    GLA_HEADS * GLA_DK,
    GLA_HEADS * GLA_DV,
    GLA_HEADS * GLA_DV,
    GLA_LOWRANK,
    MLA_Q_LORA,
    MLA_KV_LORA,
    MLA_ROPE,
)
D_IN = sum(IN_SPLITS)
GLA_WIDTH = GLA_HEADS * GLA_DV
MLA_WIDTH = MLA_HEADS * MLA_V


def rms_norm_2(x, g):
    xf = x.astype(jnp.float32)
    y = xf * lax.rsqrt(jnp.mean(xf * xf, axis=-1, keepdims=True) + NORM_EPS)
    return (y * g.astype(jnp.float32)).astype(x.dtype)

def rope_tables_2(positions):
    inv_freq = 1.0 / (ROPE_THETA_2 ** (jnp.arange(0, MLA_ROPE, 2, dtype=jnp.float32) / MLA_ROPE))
    ang = positions.astype(jnp.float32)[..., None] * inv_freq
    return jnp.cos(ang), jnp.sin(ang)

def apply_rope_2(x, cos, sin):
    half = x.shape[-1] // 2
    x1 = x[..., :half].astype(jnp.float32)
    x2 = x[..., half:].astype(jnp.float32)
    out = jnp.concatenate([x1 * cos - x2 * sin, x2 * cos + x1 * sin], axis=-1)
    return out.astype(x.dtype)

def gla_branch(h_q, h_k, h_v, h_g, h_a, w_a2, b_a2, gla_norm):
    B, S, _ = h_q.shape
    n_chunks = S // CHUNK
    f32 = jnp.float32
    q = h_q.reshape(B, S, GLA_HEADS, GLA_DK).astype(f32) * (GLA_DK ** -0.5)
    k = h_k.reshape(B, S, GLA_HEADS, GLA_DK).astype(f32)
    v = h_v.reshape(B, S, GLA_HEADS, GLA_DV).astype(f32)
    log_a = jax.nn.log_sigmoid((h_a @ w_a2 + b_a2).astype(f32)) / GLA_GATE_TEMP
    log_a = log_a.reshape(B, S, GLA_HEADS, GLA_DK)

    def to_chunks(t):
        return t.reshape(B, n_chunks, CHUNK, GLA_HEADS, t.shape[-1]).transpose(1, 0, 3, 2, 4)

    q, k, v, log_a = to_chunks(q), to_chunks(k), to_chunks(v), to_chunks(log_a)
    b = jnp.cumsum(log_a, axis=3)
    b_end = b[:, :, :, -1:, :]
    k_dec = k * jnp.exp(b_end - b)
    chunk_decay = jnp.exp(b_end[:, :, :, 0, :])

    def step(state, inp):
        qc, kc, vc, dc = inp
        state = dc[..., None] * state + jnp.einsum('bhck,bhcv->bhkv', kc, vc)
        out = jnp.einsum('bhck,bhkv->bhcv', qc, state)
        return state, out

    state0 = jnp.zeros((B, GLA_HEADS, GLA_DK, GLA_DV), f32)
    _, o = lax.scan(step, state0, (q, k_dec, v, chunk_decay))
    o = o.transpose(1, 0, 3, 2, 4).reshape(B, S, GLA_HEADS, GLA_DV)
    o = rms_norm_2(o, gla_norm)
    g = h_g.reshape(B, S, GLA_HEADS, GLA_DV).astype(f32)
    o = o * jax.nn.silu(g)
    return o.reshape(B, S, GLA_WIDTH).astype(h_q.dtype)

def mla_branch(c_q, c_kv, k_pe, cos, sin, q_norm, w_uq, kv_norm, w_ukv):
    B, S, _ = c_q.shape
    q = (rms_norm_2(c_q, q_norm) @ w_uq).reshape(B, S, MLA_HEADS, MLA_NOPE + MLA_ROPE)
    q_nope = q[..., :MLA_NOPE]
    q_pe = apply_rope_2(q[..., MLA_NOPE:], cos[:, :, None, :], sin[:, :, None, :])
    kv = (rms_norm_2(c_kv, kv_norm) @ w_ukv).reshape(B, S, MLA_HEADS, MLA_NOPE + MLA_V)
    k_nope = kv[..., :MLA_NOPE]
    v = kv[..., MLA_NOPE:]
    k_pe = apply_rope_2(k_pe, cos, sin)
    scale = (MLA_NOPE + MLA_ROPE) ** -0.5
    n_blocks = S // Q_BLOCK

    def blocks(t):
        return t.reshape(B, n_blocks, Q_BLOCK, MLA_HEADS, t.shape[-1]).transpose(1, 0, 2, 3, 4)

    key_chunk = jnp.arange(S) // CHUNK

    def attend(args):
        qn_b, qp_b, blk = args
        s = (jnp.einsum('bqhd,bkhd->bhqk', qn_b, k_nope)
             + jnp.einsum('bqhr,bkr->bhqk', qp_b, k_pe)).astype(jnp.float32) * scale
        q_chunk = (blk * Q_BLOCK + jnp.arange(Q_BLOCK)) // CHUNK
        mask = key_chunk[None, :] <= q_chunk[:, None]
        s = jnp.where(mask[None, None], s, -jnp.inf)
        p = jax.nn.softmax(s, axis=-1).astype(v.dtype)
        return jnp.einsum('bhqk,bkhd->bqhd', p, v)

    o = lax.map(attend, (blocks(q_nope), blocks(q_pe), jnp.arange(n_blocks)))
    return o.transpose(1, 0, 2, 3, 4).reshape(B, S, MLA_WIDTH)

def second_inputs(seed: int = 0) -> dict:
    key = jax.random.key(seed)
    ks = jax.random.split(key, 24)
    f32 = jnp.float32

    def w(k, shape, fan_in):
        return jax.random.normal(k, shape, f32) * (fan_in ** -0.5)

    def gain(k, dim):
        return 1.0 + 0.02 * jax.random.normal(k, (DEPTH_2, dim), f32)

    x = jax.random.normal(ks[0], (BATCH, SEQ, D_MODEL), f32)
    offsets = jax.random.randint(ks[1], (BATCH, 1), 0, 4096, dtype=jnp.int32)
    positions = offsets + jnp.arange(SEQ, dtype=jnp.int32)[None, :]
    return {
        "x": x,
        "positions": positions,
        "pre_mix_norm": gain(ks[2], D_MODEL),
        "w_in": w(ks[3], (DEPTH_2, D_MODEL, D_IN), D_MODEL),
        "w_a2": w(ks[4], (DEPTH_2, GLA_LOWRANK, GLA_HEADS * GLA_DK), GLA_LOWRANK),
        "b_a2": 0.1 * jax.random.normal(ks[5], (DEPTH_2, GLA_HEADS * GLA_DK), f32),
        "gla_norm": gain(ks[6], GLA_DV),
        "w_o_gla": w(ks[7], (DEPTH_2, GLA_WIDTH, D_MODEL), GLA_WIDTH),
        "q_norm": gain(ks[8], MLA_Q_LORA),
        "w_uq": w(ks[9], (DEPTH_2, MLA_Q_LORA, MLA_HEADS * (MLA_NOPE + MLA_ROPE)), MLA_Q_LORA),
        "kv_norm": gain(ks[10], MLA_KV_LORA),
        "w_ukv": w(ks[11], (DEPTH_2, MLA_KV_LORA, MLA_HEADS * (MLA_NOPE + MLA_V)), MLA_KV_LORA),
        "w_o_mla": w(ks[12], (DEPTH_2, MLA_WIDTH, D_MODEL), MLA_WIDTH),
        "w_gate": w(ks[13], (DEPTH_2, D_MODEL, 2 * D_MODEL), D_MODEL),
        "b_gate": 0.02 * jax.random.normal(ks[14], (DEPTH_2, 2 * D_MODEL), f32),
        "w_out": w(ks[15], (DEPTH_2, D_MODEL, D_MODEL), D_MODEL),
        "post_mix_norm": gain(ks[16], D_MODEL),
        "pre_ffn_norm": gain(ks[17], D_MODEL),
        "w_ffn_gate": w(ks[18], (DEPTH_2, D_MODEL, D_FF_2), D_MODEL),
        "w_ffn_up": w(ks[19], (DEPTH_2, D_MODEL, D_FF_2), D_MODEL),
        "w_ffn_down": w(ks[20], (DEPTH_2, D_FF_2, D_MODEL), D_FF_2),
        "post_ffn_norm": gain(ks[21], D_MODEL),
    }

def second_block(x, positions, pre_mix_norm, w_in, w_a2, b_a2, gla_norm, w_o_gla,
              q_norm, w_uq, kv_norm, w_ukv, w_o_mla, w_gate, b_gate, w_out,
              post_mix_norm, pre_ffn_norm, w_ffn_gate, w_ffn_up, w_ffn_down,
              post_ffn_norm):
    cos, sin = rope_tables_2(positions)
    split_points = list(np.cumsum(IN_SPLITS)[:-1])
    for l in range(DEPTH_2):
        h = rms_norm_2(x, pre_mix_norm[l])
        proj = h @ w_in[l]
        h_q, h_k, h_v, h_g, h_a, c_q, c_kv, k_pe = jnp.split(proj, split_points, axis=-1)
        y_a = gla_branch(h_q, h_k, h_v, h_g, h_a, w_a2[l], b_a2[l], gla_norm[l]) @ w_o_gla[l]
        y_b = mla_branch(c_q, c_kv, k_pe, cos, sin, q_norm[l], w_uq[l], kv_norm[l], w_ukv[l]) @ w_o_mla[l]
        gates = jax.nn.sigmoid(h @ w_gate[l] + b_gate[l])
        g_a, g_b = jnp.split(gates, 2, axis=-1)
        mixed = (g_a * y_a + g_b * y_b) @ w_out[l]
        x = x + rms_norm_2(mixed, post_mix_norm[l])
        h = rms_norm_2(x, pre_ffn_norm[l])
        f = (jax.nn.silu(h @ w_ffn_gate[l]) * (h @ w_ffn_up[l])) @ w_ffn_down[l]
        x = x + rms_norm_2(f, post_ffn_norm[l])
    return x


def setup_inputs(seed=0):
    out = dict(first_inputs(seed))
    for name, value in second_inputs(seed + 1).items():
        if name != "x":
            out[name + "_2"] = value
    return out


def reference(
    x, positions, att_w_in, att_g_cq, att_w_uq, att_w_iq, att_g_ik, att_b_ik, att_w_o,
    hgrn_lb_logits, hgrn_w_in, hgrn_g_norm, hgrn_w_o, ffn_w_gate, ffn_w_up, ffn_w_down, ln_g,
    ln_b, positions_2, pre_mix_norm_2, w_in_2, w_a2_2, b_a2_2, gla_norm_2, w_o_gla_2, q_norm_2,
    w_uq_2, kv_norm_2, w_ukv_2, w_o_mla_2, w_gate_2, b_gate_2, w_out_2, post_mix_norm_2,
    pre_ffn_norm_2, w_ffn_gate_2, w_ffn_up_2, w_ffn_down_2, post_ffn_norm_2,
):
    x = first_block(
        x, positions, att_w_in, att_g_cq, att_w_uq, att_w_iq, att_g_ik, att_b_ik, att_w_o,
        hgrn_lb_logits, hgrn_w_in, hgrn_g_norm, hgrn_w_o, ffn_w_gate, ffn_w_up, ffn_w_down,
        ln_g, ln_b,
    )
    return second_block(
        x, positions_2, pre_mix_norm_2, w_in_2, w_a2_2, b_a2_2, gla_norm_2, w_o_gla_2, q_norm_2,
        w_uq_2, kv_norm_2, w_ukv_2, w_o_mla_2, w_gate_2, b_gate_2, w_out_2, post_mix_norm_2,
        pre_ffn_norm_2, w_ffn_gate_2, w_ffn_up_2, w_ffn_down_2, post_ffn_norm_2,
    )


_drawn_inputs = setup_inputs


def setup_inputs(seed=0):
    import zlib

    import numpy as np

    out = dict(_drawn_inputs(seed))
    spreads = {}
    factors = {'att_g_cq': 7.5,
     'att_g_ik': 7.673,
     'att_b_ik': 8.0,
     'hgrn_g_norm': 7.647,
     'gla_norm_2': 27.536,
     'q_norm_2': 8.0,
     'kv_norm_2': 8.0,
     'b_gate_2': 8.0,
     'post_mix_norm_2': 3.307,
     'pre_ffn_norm_2': 3.423,
     'post_ffn_norm_2': 17.106,
     'b_a2_2': 3.976}
    for name, (base, spread) in spreads.items():
        noise = np.random.default_rng([zlib.crc32(name.encode()), seed]).standard_normal(out[name].shape)
        drawn = base * np.exp(spread * noise) if base else spread * noise
        out[name] = __import__('jax').numpy.asarray(drawn.astype(out[name].dtype))
    for name, factor in factors.items():
        out[name] = (out[name] * factor).astype(out[name].dtype)
    return out
```

```python
import math

import numpy as np
import concourse.bass as bass
from concourse import mybir
from contextlib import ExitStack

F32 = mybir.dt.float32
F32R = mybir.dt.float32r
BF16 = mybir.dt.bfloat16
I32 = mybir.dt.int32
ALU = mybir.AluOpType
ACT = mybir.ActivationFunctionType
AX = mybir.AxisListType

T = 256
D = 1024
P = 128
KD = D // P
DFF = -(-8 * D // (3 * 256)) * 256
NF = DFF // P
ALPHA = float((2 * 2) ** 0.25)
LN_EPS, RMS_EPS = 1e-5, 1e-6
HEADS, HD, KVH = 16, 64, 2
IH, ID = 8, 128
TOPK = min(256, T // 4)
ROT, IROT = HD // 4 // 2, ID // 4 // 2
GH, GK, GV, GLR = 4, 128, 256, 16
MH, MN, MR, MV = 8, 128, 64, 128
QL2, KVL2 = 384, 256
CH = 64
NCH = T // CH
LEVELS = [128, 64, 32, 16, 8, 4, 2, 1]
MASKED = [0] + LEVELS[1:]
BIG = 1e30
NOT_CAUSAL, TAKEN = -3.0e38, -3.3e38
MAGIC = 1.5 * 2.0 ** 23

RING = 4
TW = 2048


class Signal:

    def __init__(self, sem):
        self.sem, self.n, self.read = sem, 0, {}

    def up(self):
        self.n += 1
        return 1

    def now(self):
        return self.n

    def due(self, engine, k=1):
        self.read[id(engine)] = self.read.get(id(engine), 0) + k
        return self.read[id(engine)]

    def seen(self, engine):
        return self.read.get(id(engine), 0)

    def skip(self, engine, k):
        self.read[id(engine)] = self.read.get(id(engine), 0) + k


def build(nc, A, out):
    ctx = ExitStack()
    with ctx:
        def sb(name, shape, dt=F32):
            return ctx.enter_context(nc.sbuf_tensor(name, shape, dt))

        def sem(name):
            return ctx.enter_context(nc.semaphore(name))

        stage = sb("stage", [P, RING, TW])
        wh = sb("wh", [P, RING, TW], F32R)
        wl = sb("wl", [P, RING, TW], F32R)
        xt = sb("xt", [P, KD, T])
        xh = sb("xh", [P, KD, T], F32R)
        xl = sb("xl", [P, KD, T], F32R)
        ident = sb("ident", [P, P])
        mean_d = sb("mean_d", [P, P])
        mean_hd = sb("mean_hd", [P, P])
        vec = sb("vec", [P, P])
        vec2 = sb("vec2", [14, P])
        gt = sb("gt", [P, 142])
        restart = sb("restart", [P, T])
        lmask = sb("lmask", [P, len(MASKED), P], BF16)
        mbias = sb("mbias", [P, 3 * P])
        sbias = sb("sbias", [P, 3 * P])
        trig = sb("trig", [P, 2, 2, 24])
        trig_t = sb("trig_t", [P, 2, T])
        inv24 = sb("inv24", [P, 24])
        inv_t = sb("inv_t", [P, 1])
        kg = sb("kg", [P, 2, P])
        wa = sb("wa", [GLR, GH * GK])
        small = sb("small", [P, 128])
        eps = sb("eps", [P, 2])

        ARENA = 18000
        with nc.sbuf_tensor("arena", [P, ARENA], F32) as arena:
            pass
        hh = sb("hh", [P, NF, T], F32R)
        hl = sb("hl", [P, NF, T], F32R)

        def cut(at, *shape):
            n = math.prod(shape)
            assert at + n <= ARENA
            ap = arena[:, at:at + n]
            if len(shape) == 2:
                ap = ap.rearrange("p (a b) -> p a b", a=shape[0])
            if len(shape) == 3:
                ap = ap.rearrange("p (a b c) -> p a b c", a=shape[0], b=shape[1])
            if len(shape) == 4:
                ap = ap.rearrange("p (a b c d) -> p a b c d", a=shape[0], b=shape[1], c=shape[2])
            return ap

        NREST = GLR + QL2 + KVL2 + MR
        above = 2 * NF * T
        r = cut(above, KD, T)
        sq = cut(above + 2048, 4, T)
        rs = cut(above + 3072, T)
        silu_g = cut(above + 3328, 2, 512)
        hf = cut(above, 2, 512)
        q, iq = cut(0, 2, D), cut(2048, 2, D)
        qt, iqt = cut(4096, KD, T), cut(6144, KD, T)
        x_tok = cut(4096, 2, D)
        kr = cut(8192, 2, 256)
        kd = cut(8704, 2, KVH, 2, HD)
        kpad = cut(9216, KVH, 2, T)
        cq, cqt = cut(10240, 2, 256), cut(10752, 2, T)
        relu = cut(11264, 2, 2, 3 * P)
        score = cut(12800, 3 * P)
        top8 = cut(13184, 2, 8)
        wi = cut(13200, 2, IH)
        lg = cut(13216, 2, 2, 3 * P)
        pts = cut(14752, 2, 2, 3 * P)
        kit, kis = cut(16288, T), cut(16544, 2, P)
        tmp = cut(16800, 4, 256)
        pos_i, pos_t = small[:, 126:128].bitcast(I32), cut(11264, T).bitcast(I32)
        ang, turn = cut(11520, 2, T), cut(12032, 2, T)
        ang24, turn24 = cut(12544, 2, 48), cut(12640, 2, 48)
        row_i, col_i = cut(13216, P).bitcast(I32), cut(13344, P).bitcast(I32)
        apart, ge = cut(13472, P), cut(13600, 8, P)

        hv, hq, hgate = cut(0, 2, D), cut(2048, KD, T), cut(4096, KD, T)
        hk, hb = cut(6144, KD, T), cut(8192, KD, T)
        lev = cut(10240, 8, 2, T)
        dec = cut(14336, 2, 2 * T)
        masked_a = cut(15360, 8, P)
        at_h = cut(16384, 2, 3, P)
        o_tmp = cut(17152, 512)
        lb, one_lb, lb_x = small[:, 84:92], small[:, 92:100], small[:, 100:124]
        gates, sg, gv = cut(0, 16, T), cut(4096, KD, T), cut(6144, 2, D)
        gq, gk, gb = cut(8192, GH, T), cut(9216, GH, T), cut(10240, GH, T)
        kdec, tk = cut(11264, GH, T), cut(12288, 2, NREST)
        gqh = cut(13728, 3, GH, T)
        z, nz = cut(11264, GH * T), cut(13728, GH * T)
        at_g = cut(16800, 2, 3 * P)
        ha = cut(17568, T)[0:GLR, :]
        fl = cut(17824, GH, 6)
        g_sq, g_rs, g_tmp = cut(9216, 2, 512), cut(10240, 2, T), cut(10752, 512)
        qn, rr, ya = cut(0, KD, T), cut(4096, 2, 2, T), cut(6144, KD, T)
        kn, vm = cut(8192, KD, T), cut(10240, 2, D)
        kp = [cut(5120, 4, T), cut(16288, 4, T)]
        lat, kx = cut(14752, 5, T), cut(17312, 2, 2, P)
        tmp2 = cut(13728, 4, T)
        rp = cut(14752, 4, 2 * T)
        out_sb = cut(0, 2, D)

        ps = ctx.enter_context(nc.psum_tensor("ps", [P, 8, 512], F32))

        x_in, c_in, c_in2, stored = sem("x_in"), sem("c_in"), sem("c_in2"), sem("stored")
        stage_in = [sem(f"stage_in{s}") for s in range(RING)]
        hi_done, lo_done, used = sem("hi_done"), sem("lo_done"), sem("used")
        act_step, dve_step, pool_step = Signal(sem("act_step")), Signal(sem("dve_step")), Signal(sem("pool_step"))

        def signals(names):
            return [Signal(sem(n)) for n in names.split()]

        consts, vt_ps, gt_done, reduced, xt_ps, xt_done, xh_done, x_ready = signals(
            "consts vt_ps gt_done reduced xt_ps xt_done xh_done x_ready")
        lmask_raw, lmask_done, trig_done = signals("lmask_raw lmask_done trig_done")
        ki_var, ki_rstd, cq_ready, cqt_ps, kd_ready, kt_ps, kt_ready = signals(
            "ki_var ki_rstd cq_ready cqt_ps kd_ready kt_ps kt_ready")
        iq_copied, iq_rot, iqt_ps, iqt_done, ix_ps, relu_done, relu_used, score_done, score_cut = signals(
            "iq_copied iq_rot iqt_ps iqt_done ix_ps relu_done relu_used score_done score_cut")
        q_rot, qt_ps, qt_done, sel_done, bias_ready = signals("q_rot qt_ps qt_done sel_done bias_ready")
        lg_ps, lg_free, nmx_ready, p_ready, pn_ready, pt_ps, pts_done, ot_ps, oh_done = signals(
            "lg_ps lg_free nmx_ready p_ready pn_ready pt_ps pts_done ot_ps oh_done")
        r_ready, mean_ps, d_ready, sq_ready, sq_used, rs_ready = signals(
            "r_ready mean_ps d_ready sq_ready sq_used rs_ready")
        s_done, h_mul, h_hi, h_ready, y_done = signals("s_done h_mul h_hi h_ready y_done")

        lb_in, lb_exp, hg_v, hg_a, hg_ln, hg_b, hg_d, hg_e, hg_p, hg_ps = signals(
            "lb_in lb_exp hg_v hg_a hg_ln hg_b hg_d hg_e hg_p hg_ps")
        hg_free, hg_at, hg_o, hg_sq, hg_mean, hg_rs, hg_g = signals("hg_free hg_at hg_o hg_sq hg_mean hg_rs hg_g")
        b2_d, b2_a, ha_ps, ha_done, z_ps, z_done, nz_done, sp_done, gb_done, kdec_e, gqh_done = signals(
            "b2_d b2_a ha_ps ha_done z_ps z_done nz_done sp_done gb_done kdec_e gqh_done")
        ga_ps, ga_at, go_ps, go_sq, go_mean, go_rs, go_g, ya_done = signals(
            "ga_ps ga_at go_ps go_sq go_mean go_rs go_g ya_done")
        lat_scaled, kx_done, lat_ps, lat_done, m_a, m_d = signals("lat_scaled kx_done lat_ps lat_done m_a m_d")
        out_ps, out_done, stream = signals("out_ps out_done stream")

        tiles = []
        runs = {}

        def rows(w, a, b):
            return w[a * P:b * P, :].rearrange("(k p) n -> p k n", p=P)

        def columns(w, a, n):
            tiles.append([(None, w.rearrange("(k p) n -> p k n", p=P)[:, :, a:a + n])])

        def tile_range(count):
            return range(len(tiles), len(tiles) + count)

        FFNS = [(A["ffn_w_gate"][0], A["ffn_w_up"][0], A["ffn_w_down"][0]),
                (A["ffn_w_gate"][1], A["ffn_w_up"][1], A["ffn_w_down"][1]),
                (A["w_ffn_gate_2"][0], A["w_ffn_up_2"][0], A["w_ffn_down_2"][0])]

        def plan_ffn(f):
            gate, up, down = FFNS[f]
            base = len(tiles)
            gates, ups = (w.rearrange("(k p) n -> p k n", p=P) for w in (gate, up))
            pair = [lambda i, w=w, p=p: w[:, :, bass.ds(i * 512 + 256 * p, 256)] for p in range(2) for w in (gates, ups)]
            downs = down.rearrange("(j k p) n -> p j k n", p=P, k=2)
            runs[base] = (NF // 4, 4, pair)
            runs[base + NF] = (2, 4, [lambda i, j=j: downs[:, bass.ds(i * 4 + j, 1), :, :].rearrange(
                "p a k n -> p (a k) n") for j in range(4)])
            for p in range(NF // 2):
                columns(gate, 256 * p, 256)
                columns(up, 256 * p, 256)
            for j in range(NF // 2):
                tiles.append([(None, rows(down, 2 * j, 2 * j + 2))])
            return base

        w_att = A["att_w_in"][0]
        for a in (0, 256, 648 - 256):
            columns(w_att, a, 256)
        tiles.append([(None, rows(A["att_w_iq"][0], 0, 2))])
        tiles.append([(None, rows(A["att_w_uq"][0], 0, 2))])
        t_wo = len(tiles)
        for m in range(4):
            columns(A["att_w_o"][0], 256 * m, 256)
        t_ffn0 = plan_ffn(0)
        def column_blocks(w, a, count):
            at = len(tiles)
            for j in range(count):
                columns(w, a + 256 * j, 256)
            return at

        w_h = A["hgrn_w_in"][0]
        t_hi, t_hq, t_hf, t_hg = (column_blocks(w_h, a, 4) for a in (2 * D, 0, D, 3 * D))
        t_hwo = column_blocks(A["hgrn_w_o"][0], 0, 4)
        t_ffn1 = plan_ffn(1)
        w_2 = A["w_in_2"][0]
        GQ = GH * GK
        REST = 2 * GQ + 2 * GH * GV
        t_rest = len(tiles)
        for a in (REST, REST + 256, REST + NREST - 256):
            columns(w_2, a, 256)
        t_gv = column_blocks(w_2, 2 * GQ, 4)
        t_gq = column_blocks(w_2, 0, 2)
        t_gk = column_blocks(w_2, GQ, 2)
        t_gg = column_blocks(w_2, 2 * GQ + GH * GV, 4)
        t_gate = column_blocks(A["w_gate_2"][0], 0, 8)
        t_gwo = column_blocks(A["w_o_gla_2"][0], 0, 4)
        t_uq = len(tiles)
        uq = A["w_uq_2"][0].rearrange("(k p) (h c) -> p k h c", p=P, c=MN + MR)
        KQ = QL2 // P
        HR = MR // 2
        tiles.append([((k * 512 + x * 256, 8 * HR, 8), uq[:, k, :, MN + x * HR:MN + (x + 1) * HR])
                      for k in range(KQ) for x in range(2)])
        for j in range(2):
            tiles.append([((k * 512, 512, 4), uq[:, k, 4 * j:4 * j + 4, 0:MN]) for k in range(KQ)])
        t_ukv = len(tiles)
        for j in range(2):
            tiles.append([(None, rows(A["w_ukv_2"][0], 0, 2)[:, :, j * 1024:(j + 1) * 1024])])
        t_mwo = column_blocks(A["w_o_mla_2"][0], 0, 4)
        t_out = column_blocks(A["w_out_2"][0], 0, 4)
        t_ffn2 = plan_ffn(2)

        come, total = [], [0] * RING
        for n, parts in enumerate(tiles):
            total[n % RING] += 16 * len(parts)
            come.append(total[n % RING])

        def load(sp, n, i=None, source=None):
            if n >= RING:
                sp.wait_ge(lo_done, (n - RING + 1) if i is None else i * RING + (n - RING + 1))
            for place, src in ([(None, source(i))] if source else tiles[n]):
                if place is None:
                    to = stage[:, ring(n), :].rearrange("p (k n) -> p k n", k=src.shape[1])
                else:
                    at, words, k = place
                    to = stage[:, ring(n), at:at + words].rearrange("p (k n) -> p k n", k=k)
                sp.dma_start(to, src).then_inc(stage_in[ring(n)], 16)

        def ring(n):
            return n % RING

        def hi(act, n, i=None, base=None):
            off = 0 if i is None else i
            act.wait_ge(stage_in[ring(n)], off * 16 + come[n])
            if n >= RING:
                act.wait_ge(used, off * RING + (n - RING + 1))
            nc.scalar.activation(wh[:, ring(n), :], stage[:, ring(n), :], ACT.Copy).then_inc(hi_done, 1)

        def lo(pool, n, i=None):
            off = 0 if i is None else i
            pool.wait_ge(hi_done, off * RING + (n + 1))
            nc.gpsimd.tensor_tensor(wl[:, ring(n), :], stage[:, ring(n), :], wh[:, ring(n), :].bitcast(F32),
                                    ALU.subtract).then_inc(lo_done, 1)

        his = [0]

        def hi_until(act, n):
            while his[0] <= min(n, len(tiles) - 1):
                hi(act, his[0])
                his[0] += 1




        V = nc.vector
        mm = nc.tensor.matmul

        def mm3(out_, lhs, rhs, start, stop, skip=False):
            (lh, ll), (rh, rl) = lhs, rhs
            mm(out_, lh, rh, start=start, stop=False, skip_group_check=skip)
            mm(out_, lh, rl, start=False, stop=False, skip_group_check=skip)
            return mm(out_, ll, rh, start=False, stop=stop, skip_group_check=skip)

        def tile_a(pe, n, b, kt=KD, width=256, i=None, m_cols=(0, 128), x0=0, done=True):
            pe.wait_ge(lo_done, (n + 1) if i is None else i * RING + (n + 1))
            s = ring(n)
            for m, c in enumerate(m_cols):
                for k in range(kt):
                    o = k * width + c
                    last = mm3(ps[:, b + m // 2, m % 2 * T:(m % 2 + 1) * T],
                               (wh[:, s, o:o + P], wl[:, s, o:o + P]), (xh[:, x0 + k, :], xl[:, x0 + k, :]),
                               k == 0, k == kt - 1)
            if done:
                last.then_inc(used, 1)
            return last

        def tile_b(pe, n, outs, kt=KD, width=256, cols=256):
            pe.wait_ge(lo_done, n + 1)
            s = ring(n)
            for t, c, out_ in outs:
                for k in range(kt):
                    o = k * width + c
                    x = slice(t * P, (t + 1) * P)
                    last = mm3(out_, (xh[:, k, x], xl[:, k, x]),
                               (wh[:, s, o:o + cols], wl[:, s, o:o + cols]), k == 0, k == kt - 1)
            last.then_inc(used, 1)

        def setup_pool(pool):
            nc.gpsimd.memset(ident[:], 0.0).then_inc(pool_step.sem, pool_step.up())
            pool.wait_ge(pool_step.sem, pool_step.now())
            nc.gpsimd.affine_select(out=ident[:], in_=ident[:], compare_op=ALU.not_equal, fill=1.0, base=0,
                                    pattern=[[-1, P]], channel_multiplier=1).then_inc(pool_step.sem, pool_step.up())
            pool.wait_ge(pool_step.sem, pool_step.now())
            nc.gpsimd.iota(row_i, [[0, P]], base=0, channel_multiplier=1
            ).then_inc(pool_step.sem, pool_step.up())
            pool.wait_ge(pool_step.sem, pool_step.now())
            nc.gpsimd.iota(col_i, [[1, P]], base=0, channel_multiplier=0
            ).then_inc(pool_step.sem, pool_step.up())
            pool.wait_ge(pool_step.sem, pool_step.now())
            nc.gpsimd.memset(mean_d[:], 1.0 / D).then_inc(pool_step.sem, pool_step.up())
            pool.wait_ge(pool_step.sem, pool_step.now())
            nc.gpsimd.memset(mean_hd[:], 1.0 / P).then_inc(pool_step.sem, pool_step.up())
            pool.wait_ge(pool_step.sem, pool_step.now())
            nc.gpsimd.memset(restart[:], 1.0).then_inc(pool_step.sem, pool_step.up())
            pool.wait_ge(pool_step.sem, pool_step.now())
            nc.gpsimd.memset(restart[:, 0:T:CH], 0.0).then_inc(pool_step.sem, pool_step.up())
            pool.wait_ge(pool_step.sem, pool_step.now())
            nc.gpsimd.memset(mbias[:], 0.0).then_inc(pool_step.sem, pool_step.up())
            pool.wait_ge(pool_step.sem, pool_step.now())
            nc.gpsimd.memset(mbias[0:CH, CH:P], -BIG).then_inc(pool_step.sem, pool_step.up())
            pool.wait_ge(pool_step.sem, pool_step.now())
            nc.gpsimd.memset(mbias[0:CH, 2 * P + CH:3 * P], -BIG).then_inc(pool_step.sem, pool_step.up())
            pool.wait_ge(pool_step.sem, pool_step.now())
            nc.gpsimd.memset(eps[:, 0:1], LN_EPS).then_inc(pool_step.sem, pool_step.up())
            pool.wait_ge(pool_step.sem, pool_step.now())
            nc.gpsimd.memset(kpad, 0.0).then_inc(pool_step.sem, pool_step.up())
            pool.wait_ge(pool_step.sem, pool_step.now())
            nc.gpsimd.memset(eps[:, 1:2], RMS_EPS).then_inc(consts.sem, consts.up())
            pool.wait_ge(consts.sem, consts.now())

        def setup_act(act):
            def load(to, src):
                act.dma_start(to, src, allow_slow_non_contiguous=True).then_inc(c_in, 16)

            def blocks(x):
                return x.rearrange("a (k p) -> (a k) p", p=P)

            load(pos_i, A["positions"][0].rearrange("(t p) -> p t", p=P))
            load(pos_t, A["positions_2"][0, :].partition_broadcast(P))
            load(inv24[:], A["inv24"][0, :].partition_broadcast(P))
            load(inv_t[:], A["inv_t"])
            load(vec[0:32, :], A["ln_g"].rearrange("l j (k p) -> (l j k) p", p=P))
            load(vec[32:64, :], A["ln_b"].rearrange("l j (k p) -> (l j k) p", p=P))
            for at, name in ((64, "pre_mix_norm_2"), (72, "post_mix_norm_2"), (80, "pre_ffn_norm_2"),
                             (88, "post_ffn_norm_2"), (96, "b_gate_2"), (112, "hgrn_lb_logits")):
                n = math.prod(A[name].shape) // P
                load(vec[at:at + n, :], blocks(A[name]))
            for at, name in ((0, "b_a2_2"), (4, "gla_norm_2"), (6, "q_norm_2"), (9, "kv_norm_2"),
                             (11, "hgrn_g_norm"), (12, "att_g_cq")):
                n = math.prod(A[name].shape) // P
                load(vec2[at:at + n, :], blocks(A[name]))
            load(kg[:, 0, :], A["att_g_ik"][0, :].partition_broadcast(P))
            load(kg[:, 1, :], A["att_b_ik"][0, :].partition_broadcast(P))
            load(wa[:], A["w_a2_2"][0])
        N_CONST = 21

        def setup_act2(act):
            act.wait_ge(reduced.sem, reduced.due(act))
            nc.scalar.activation(trig[:, :, :, :].rearrange("p c t f -> p (c t f)"),
                                 ang24.rearrange("p c f -> p (c f)"), ACT.Sin).then_inc(act_step.sem, act_step.up())
            act.wait_ge(act_step.sem, act_step.now())
            nc.scalar.activation(trig_t[:, :, :].rearrange("p c t -> p (c t)"),
                                 ang.rearrange("p c t -> p (c t)"), ACT.Sin).then_inc(trig_done.sem, trig_done.up())
            act.wait_ge(trig_done.sem, trig_done.now())
            act.wait_ge(lb_in.sem, lb_in.due(act))
            nc.scalar.preload_act_table_set("natural_log_exp_and_others")
            nc.scalar.activation(lb_x[:, 0:16], lb_x[:, 0:16], ACT.Exp).then_inc(lb_exp.sem, lb_exp.up())
            act.wait_ge(lb_exp.sem, lb_exp.now())

        def reduce_angle(dve, x, n, quarter):
            parts, left = [], 2 * math.pi
            for bits in (8, 8, 8):
                unit = 2.0 ** (math.floor(math.log2(left)) - bits + 1)
                parts.append(math.floor(left / unit) * unit)
                left -= parts[-1]
            parts.append(left)
            V.tensor_scalar(n, x, 1 / (2 * math.pi), 0.25 if quarter else 0.0, ALU.mult, ALU.add
            ).then_inc(dve_step.sem, dve_step.up())
            dve.wait_ge(dve_step.sem, dve_step.now())
            V.tensor_scalar(n, n, MAGIC, MAGIC, ALU.add, ALU.subtract).then_inc(dve_step.sem, dve_step.up())
            dve.wait_ge(dve_step.sem, dve_step.now())
            for part in parts:
                V.scalar_tensor_tensor(out=x, in0=n, scalar=-part, in1=x, op0=ALU.mult, op1=ALU.add
                ).then_inc(dve_step.sem, dve_step.up())
                dve.wait_ge(dve_step.sem, dve_step.now())
            if quarter:
                V.tensor_scalar(x, x, math.pi / 2, None, ALU.add).then_inc(dve_step.sem, dve_step.up())
                dve.wait_ge(dve_step.sem, dve_step.now())
            V.tensor_scalar(x, x, 3.1415925, -3.1415925, ALU.min, ALU.max).then_inc(dve_step.sem, dve_step.up())
            dve.wait_ge(dve_step.sem, dve_step.now())

        def setup_dve(dve):
            dve.wait_ge(c_in, 16 * N_CONST)
            f24 = tmp[:, 0, 0:2]
            V.tensor_copy(f24, pos_i).then_inc(dve_step.sem, dve_step.up())
            dve.wait_ge(dve_step.sem, dve_step.now())
            for t in range(2):
                V.tensor_scalar(ang24[:, 0, t * 24:(t + 1) * 24], inv24[:], f24[:, t:t + 1], None, ALU.mult
                ).then_inc(dve_step.sem, dve_step.up())
                dve.wait_ge(dve_step.sem, dve_step.now())
            V.tensor_copy(ang24[:, 1, :], ang24[:, 0, :]).then_inc(dve_step.sem, dve_step.up())
            dve.wait_ge(dve_step.sem, dve_step.now())
            V.tensor_copy(ang[:, 1, :], pos_t).then_inc(dve_step.sem, dve_step.up())
            dve.wait_ge(dve_step.sem, dve_step.now())
            V.tensor_scalar(ang[:, 0, :], ang[:, 1, :], inv_t[:, 0:1], None, ALU.mult
            ).then_inc(dve_step.sem, dve_step.up())
            dve.wait_ge(dve_step.sem, dve_step.now())
            V.tensor_copy(ang[:, 1, :], ang[:, 0, :]).then_inc(dve_step.sem, dve_step.up())
            dve.wait_ge(dve_step.sem, dve_step.now())
            for c in range(2):
                reduce_angle(dve, ang24[:, c, :], turn24[:, c, :], c == 0)
                reduce_angle(dve, ang[:, c, :], turn[:, c, :], c == 0)
            V.tensor_copy(f24, f24).then_inc(reduced.sem, reduced.up())
            dve.wait_ge(reduced.sem, reduced.now())

        def setup_dve2(dve):
            dve.wait_ge(consts.sem, consts.due(dve))
            V.tensor_tensor(row_i, row_i, col_i, ALU.bitwise_xor).then_inc(dve_step.sem, dve_step.up())
            dve.wait_ge(dve_step.sem, dve_step.now())
            V.tensor_copy(apart, row_i).then_inc(dve_step.sem, dve_step.up())
            dve.wait_ge(dve_step.sem, dve_step.now())
            V.tensor_scalar(lmask[:, 0, :], apart, 0.0, None, ALU.is_equal
            ).then_inc(dve_step.sem, dve_step.up())
            dve.wait_ge(dve_step.sem, dve_step.now())
            for l, d in enumerate(MASKED[1:]):
                V.tensor_scalar(ge[:, l, :], apart, float(d), None, ALU.is_ge
                ).then_inc(dve_step.sem, dve_step.up())
                dve.wait_ge(dve_step.sem, dve_step.now())
            V.tensor_copy(lmask[:, 1, :], ge[:, 0, :]).then_inc(dve_step.sem, dve_step.up())
            dve.wait_ge(dve_step.sem, dve_step.now())
            for l in range(1, 7):
                V.tensor_tensor(lmask[:, l + 1, :], ge[:, l, :], ge[:, l - 1, :], ALU.subtract
                ).then_inc(dve_step.sem, dve_step.up())
                dve.wait_ge(dve_step.sem, dve_step.now())
            V.tensor_copy(apart, apart).then_inc(lmask_raw.sem, lmask_raw.up())
            dve.wait_ge(lmask_raw.sem, lmask_raw.now())
            dve.wait_ge(vt_ps.sem, vt_ps.due(dve))
            V.tensor_copy(gt[:, 0:142], ps[:, 0, 0:142]).then_inc(gt_done.sem, gt_done.up())
            dve.wait_ge(gt_done.sem, gt_done.now())
            l0, l1, top = gt[:, 112:120], gt[:, 120:128], lb_x[:, 16:24]
            V.tensor_tensor(top, l0, l1, ALU.max).then_inc(dve_step.sem, dve_step.up())
            dve.wait_ge(dve_step.sem, dve_step.now())
            V.tensor_tensor(lb_x[:, 0:8], l0, top, ALU.subtract).then_inc(dve_step.sem, dve_step.up())
            dve.wait_ge(dve_step.sem, dve_step.now())
            V.tensor_tensor(lb_x[:, 8:16], l1, top, ALU.subtract).then_inc(lb_in.sem, lb_in.up())
            dve.wait_ge(lb_in.sem, lb_in.now())
            dve.wait_ge(lb_exp.sem, lb_exp.due(dve))
            V.tensor_tensor(top, lb_x[:, 0:8], lb_x[:, 8:16], ALU.add).then_inc(dve_step.sem, dve_step.up())
            dve.wait_ge(dve_step.sem, dve_step.now())
            V.reciprocal(top, top).then_inc(dve_step.sem, dve_step.up())
            dve.wait_ge(dve_step.sem, dve_step.now())
            V.tensor_tensor(lb_x[:, 0:8], lb_x[:, 0:8], top, ALU.mult).then_inc(dve_step.sem, dve_step.up())
            dve.wait_ge(dve_step.sem, dve_step.now())
            V.tensor_tensor(lb_x[:, 8:16], lb_x[:, 8:16], top, ALU.mult).then_inc(dve_step.sem, dve_step.up())
            dve.wait_ge(dve_step.sem, dve_step.now())
            V.tensor_tensor(lb, lb_x[:, 0:8], lb_x[:, 8:16], ALU.add).then_inc(dve_step.sem, dve_step.up())
            dve.wait_ge(dve_step.sem, dve_step.now())
            V.tensor_tensor(lb, lb, lb_x[:, 0:8], ALU.subtract).then_inc(dve_step.sem, dve_step.up())
            dve.wait_ge(dve_step.sem, dve_step.now())
            V.tensor_scalar(one_lb, lb, -1.0, 1.0, ALU.mult, ALU.add).then_inc(dve_step.sem, dve_step.up())
            dve.wait_ge(dve_step.sem, dve_step.now())

        def setup_pool2(pool):
            pool.wait_ge(lmask_raw.sem, lmask_raw.due(pool))
            nc.gpsimd.affine_select(out=lmask[:, 1:8, :], in_=lmask[:, 1:8, :], compare_op=ALU.is_gt, fill=0.0,
                                    base=0, pattern=[[0, 7], [1, P]], channel_multiplier=-1
            ).then_inc(lmask_done.sem, lmask_done.up())
            pool.wait_ge(lmask_done.sem, lmask_done.now())

        def setup_pe(pe):
            pe.wait_ge(consts.sem, consts.due(pe))
            pe.wait_ge(c_in, 16 * N_CONST)
            nc.tensor.transpose(ps[:, 0, 0:P], vec[:], ident[:])
            nc.tensor.transpose(ps[:, 0, P:P + 14], vec2[:], ident[0:14, 0:14]).then_inc(vt_ps.sem, vt_ps.up())
            pe.wait_ge(x_in, 16)
            for c in range(4):
                for k in range(2):
                    for t in range(2):
                        last = nc.tensor.transpose(ps[:, 4 + c, k * T + t * P:k * T + (t + 1) * P],
                                                   x_tok[:, t, (2 * c + k) * P:(2 * c + k + 1) * P], ident[:])
                last.then_inc(xt_ps.sem, xt_ps.up())

        def two(x, c):
            return x[:, 2 * c:2 * c + 2, :]

        def x_act(act, src=None):
            for c in range(4):
                act.wait_ge(xt_done.sem, xt_done.due(act))
                nc.scalar.activation(two(xh, c), two(src if src is not None else xt, c), ACT.Copy
                ).then_inc(xh_done.sem, xh_done.up())
                act.wait_ge(xh_done.sem, xh_done.now())

        def bank2(b):
            return ps[:, b, :].rearrange("p (k t) -> p k t", k=2)

        def setup_x_dve(dve):
            for c in range(4):
                dve.wait_ge(xt_ps.sem, xt_ps.due(dve))
                V.tensor_copy(two(xt, c), bank2(4 + c)).then_inc(xt_done.sem, xt_done.up())
                dve.wait_ge(xt_done.sem, xt_done.now())
            x_lo_dve(dve)

        def x_lo(dve, c, src=None):
            dve.wait_ge(xh_done.sem, xh_done.due(dve))
            V.tensor_tensor(two(xl, c), two(src if src is not None else xt, c), two(xh, c).bitcast(F32), ALU.subtract
            ).then_inc(x_ready.sem, x_ready.up())
            dve.wait_ge(x_ready.sem, x_ready.now())

        def x_lo_dve(dve):
            for c in range(4):
                x_lo(dve, c)

        def rope(dve, x, cs, heads, half):
            cos, sin = (cs[c].unsqueeze(1).to_broadcast([P, heads, half]) for c in range(2))
            lo_, up = x[:, :, 0:half], x[:, :, half:2 * half]
            m = [tmp[:, j, 0:heads * half].rearrange("p (h f) -> p h f", h=heads) for j in range(4)]
            V.tensor_tensor(m[0], lo_, cos, ALU.mult).then_inc(dve_step.sem, dve_step.up())
            dve.wait_ge(dve_step.sem, dve_step.now())
            V.tensor_tensor(m[1], up, sin, ALU.mult).then_inc(dve_step.sem, dve_step.up())
            dve.wait_ge(dve_step.sem, dve_step.now())
            V.tensor_tensor(m[2], up, cos, ALU.mult).then_inc(dve_step.sem, dve_step.up())
            dve.wait_ge(dve_step.sem, dve_step.now())
            V.tensor_tensor(m[3], lo_, sin, ALU.mult).then_inc(dve_step.sem, dve_step.up())
            dve.wait_ge(dve_step.sem, dve_step.now())
            V.tensor_tensor(lo_, m[0], m[1], ALU.subtract).then_inc(dve_step.sem, dve_step.up())
            dve.wait_ge(dve_step.sem, dve_step.now())
            V.tensor_tensor(up, m[2], m[3], ALU.add).then_inc(dve_step.sem, dve_step.up())
            dve.wait_ge(dve_step.sem, dve_step.now())

        def cs_q(t):
            return trig[:, 0, t, 0:ROT], trig[:, 1, t, 0:ROT]

        def cs_i(t):
            return trig[:, 0, t, ROT:24], trig[:, 1, t, ROT:24]

        def dsa_pe(pe):
            pe.wait_ge(x_ready.sem, x_ready.due(pe, 4))
            pe.wait_ge(gt_done.sem, gt_done.due(pe))
            for n in range(3):
                tile_b(pe, n, [(t, 0, ps[:, n, t * T:(t + 1) * T]) for t in range(2)])
            pe.wait_ge(cq_ready.sem, cq_ready.due(pe, 2))
            for k in range(2):
                for t in range(2):
                    last = nc.tensor.transpose(ps[:, 4, k * T + t * P:k * T + (t + 1) * P],
                                               cq[:, t, k * P:(k + 1) * P], ident[:])
            last.then_inc(cqt_ps.sem, cqt_ps.up())
            pe.wait_ge(kd_ready.sem, kd_ready.due(pe))
            for gr in range(KVH):
                for t in range(2):
                    nc.tensor.transpose(ps[:, 5, gr * T + t * P:gr * T + (t + 1) * P],
                                        kd[:, t, gr, :, :].rearrange("p a b -> p (a b)"), ident[:])
            for t in range(2):
                last = nc.tensor.transpose(ps[:, 6, t * P:(t + 1) * P], kis[:, t, :], ident[:])
            last.then_inc(kt_ps.sem, kt_ps.up())
            pe.wait_ge(x_ready.sem, x_ready.due(pe))
            for n, b in ((3, 0), (4, 4)):
                tile_b(pe, n, [(t, c * 512, ps[:, b + 2 * t + c, :]) for t in range(2) for c in range(2)],
                       kt=2, width=D, cols=512)
            pe.wait_ge(iq_rot.sem, iq_rot.due(pe))
            for h in range(IH):
                for t in range(2):
                    last = nc.tensor.transpose(ps[:, h // 2, h % 2 * T + t * P:h % 2 * T + (t + 1) * P],
                                               iq[:, t, h * P:(h + 1) * P], ident[:])
                if h % 2:
                    last.then_inc(iqt_ps.sem, iqt_ps.up())
            pe.wait_ge(iqt_done.sem, iqt_done.due(pe, 4))
            for h in range(IH):
                b = h % 4
                if h % 2 == 0 and h >= 4:
                    pe.wait_ge(relu_done.sem, relu_done.due(pe))
                mm(ps[:, b, 0:P], iqt[:, h, 0:P], kit[:, 0:P], start=True, stop=True)
                last = mm(ps[:, b, P:3 * P], iqt[:, h, P:T], kit, start=True, stop=True)
                if h % 2:
                    last.then_inc(ix_ps.sem, ix_ps.up())
            pe.wait_ge(q_rot.sem, q_rot.due(pe))
            for h in range(KD):
                for t in range(2):
                    last = nc.tensor.transpose(ps[:, 4 + h // 2, h % 2 * T + t * P:h % 2 * T + (t + 1) * P],
                                               q[:, t, h * P:(h + 1) * P], ident[:])
                if h % 2:
                    last.then_inc(qt_ps.sem, qt_ps.up())
            pe.wait_ge(relu_done.sem, relu_done.due(pe, 2))
            pe.wait_ge(qt_done.sem, qt_done.due(pe, 4))

            def logits(i):
                for e in range(2):
                    h = 2 * i + e
                    gr = h // (HEADS // KVH)
                    b = 2 * (i % 2) + e
                    mm(ps[:, b, 0:P], qt[:, i, 0:P], kpad[:, gr, e, 0:P], start=True, stop=True)
                    last = mm(ps[:, b, P:3 * P], qt[:, i, P:T], kpad[:, gr, e, :], start=True, stop=True)
                return last

            def weighted(i, e, pt, last_of_pair):
                gr = (2 * i + e) // (HEADS // KVH)
                o = ps[e * HD:(e + 1) * HD, 6 + i % 2, :]
                val = [kr[:, t, P + gr * HD:P + (gr + 1) * HD] for t in range(2)]
                mm(o[:, 0:P], val[0], pt[:, 0:P], start=True, stop=True)
                mm(o[:, P:T], val[0], pt[:, P:2 * P], start=True, stop=False)
                return mm(o[:, P:T], val[1], pt[:, 2 * P:3 * P], start=False, stop=True)

            attend_pe(pe, HEADS // 2, logits, weighted)
            out_pe(pe, t_wo)

        def out_pe(pe, base, moving=2):
            pe.wait_ge(x_ready.sem, x_ready.due(pe, moving))
            for j in range(4):
                tile_a(pe, base + j, 4 + j)

        def attend_pe(pe, pairs, logits, weighted):
            for i in range(2):
                logits(i).then_inc(lg_ps.sem, lg_ps.up())
            for i in range(pairs):
                pe.wait_ge(pn_ready.sem, pn_ready.due(pe))
                if i >= 1:
                    pe.wait_ge(pts_done.sem, pts_done.due(pe, 0))
                for e in range(2):
                    for c in range(3):
                        last = nc.tensor.transpose(ps[:, 4 + e, c * P:(c + 1) * P],
                                                   lg[:, i % 2, e, c * P:(c + 1) * P], ident[:])
                last.then_inc(pt_ps.sem, pt_ps.up())
                if i + 2 < pairs:
                    pe.wait_ge(lg_free.sem, lg_free.due(pe))
                    logits(i + 2).then_inc(lg_ps.sem, lg_ps.up())
                pe.wait_ge(pts_done.sem, pts_done.due(pe))
                if i >= 2:
                    pe.wait_ge(x_ready.sem, x_ready.due(pe))
                for e in range(2):
                    last = weighted(i, e, pts[:, i % 2, e, :], e)
                last.then_inc(ot_ps.sem, ot_ps.up())
            lg_free.skip(pe, 2)

        def attend_act(act, pairs, scale, outputs, before=None):
            def exps(i):
                act.wait_ge(nmx_ready.sem, nmx_ready.due(act))
                for e in range(2):
                    for t, (c0, c1) in enumerate(((0, P), (P, 3 * P))):
                        at = 8 + 8 * (i % 2) + 2 * e + t
                        x = lg[:, i % 2, e, c0:c1]
                        ins = nc.scalar.activation(x, x, ACT.Exp, bias=small[:, at + 4:at + 5], scale=scale,
                                                   accum_out=small[:, 16 + at:17 + at])
                ins.then_inc(p_ready.sem, p_ready.up())
                act.wait_ge(p_ready.sem, p_ready.now())

            exps(0)
            for i in range(pairs):
                if i + 1 < pairs:
                    exps(i + 1)
                act.wait_ge(pt_ps.sem, pt_ps.due(act))
                nc.scalar.activation(pts[:, i % 2, :, :], ps[:, 4:6, 0:3 * P], ACT.Copy
                ).then_inc(pts_done.sem, pts_done.up())
                act.wait_ge(pts_done.sem, pts_done.now())
                act.wait_ge(ot_ps.sem, ot_ps.due(act))
                outputs(i)

        def attend_dve(dve, pairs, scale, bias, outputs):
            def masked(i):
                dve.wait_ge(lg_ps.sem, lg_ps.due(dve))
                x = lg[:, i % 2, :, :]
                if i >= 2:
                    dve.wait_ge(pt_ps.sem, pt_ps.due(dve, 0))
                V.tensor_tensor(x, ps[:, 2 * (i % 2):2 * (i % 2) + 2, 0:3 * P],
                                bias.unsqueeze(1).to_broadcast([P, 2, 3 * P]), ALU.add
                ).then_inc(lg_free.sem, lg_free.up())
                dve.wait_ge(lg_free.sem, lg_free.now())
                at = 8 + 8 * (i % 2)
                mx = small[:, at:at + 4].rearrange("p (e t) -> p e t", e=2)
                V.tensor_reduce(mx[:, :, 0], x[:, :, 0:P], AX.X, ALU.max).then_inc(dve_step.sem, dve_step.up())
                dve.wait_ge(dve_step.sem, dve_step.now())
                V.tensor_reduce(mx[:, :, 1], x[:, :, P:3 * P], AX.X, ALU.max
                ).then_inc(dve_step.sem, dve_step.up())
                dve.wait_ge(dve_step.sem, dve_step.now())
                V.tensor_scalar(small[:, at + 4:at + 8], small[:, at:at + 4], -scale, None, ALU.mult
                ).then_inc(nmx_ready.sem, nmx_ready.up())
                dve.wait_ge(nmx_ready.sem, nmx_ready.now())

            masked(0)
            for i in range(pairs):
                if i + 1 < pairs:
                    masked(i + 1)
                dve.wait_ge(p_ready.sem, p_ready.due(dve))
                at = 24 + 8 * (i % 2)
                V.reciprocal(small[:, at + 4:at + 8], small[:, at:at + 4]).then_inc(dve_step.sem, dve_step.up())
                dve.wait_ge(dve_step.sem, dve_step.now())
                for e in range(2):
                    for t, (c0, c1) in enumerate(((0, P), (P, 3 * P))):
                        x = lg[:, i % 2, e, c0:c1]
                        w = at + 4 + 2 * e + t
                        ins = V.tensor_scalar(x, x, small[:, w:w + 1], None, ALU.mult)
                        if (e, t) != (1, 1):
                            ins.then_inc(dve_step.sem, dve_step.up())
                            dve.wait_ge(dve_step.sem, dve_step.now())
                ins.then_inc(pn_ready.sem, pn_ready.up())
                dve.wait_ge(pn_ready.sem, pn_ready.now())
                pt_ps.skip(dve, 1)
                dve.wait_ge(oh_done.sem, oh_done.due(dve))
                outputs(i)

        def dsa_act(act):
            act.wait_ge(used, 1)
            for t in range(2):
                nc.scalar.activation(iq[:, t, 0:T], ps[:, 0, t * T:(t + 1) * T], ACT.Square,
                                     accum_out=small[:, t:t + 1]).then_inc(act_step.sem, act_step.up())
                act.wait_ge(act_step.sem, act_step.now())
            nc.scalar.preload_act_table_set("natural_log_exp_and_others")
            nc.scalar.activation(small[:, 2:4], small[:, 0:2], ACT.Ln, scale=1.0 / 256, bias=eps[:, 1:2]
            ).then_inc(act_step.sem, act_step.up())
            act.wait_ge(act_step.sem, act_step.now())
            nc.scalar.activation(small[:, 4:6], small[:, 2:4], ACT.Exp, scale=-0.5
            ).then_inc(act_step.sem, act_step.up())
            act.wait_ge(act_step.sem, act_step.now())
            for t in range(2):
                nc.scalar.activation(cq[:, t, :], ps[:, 0, t * T:(t + 1) * T], ACT.Copy,
                                     scale=small[:, 4 + t:5 + t]).then_inc(cq_ready.sem, cq_ready.up())
                act.wait_ge(cq_ready.sem, cq_ready.now())
            hi_until(act, 4)
            act.wait_ge(ki_var.sem, ki_var.due(act))
            nc.scalar.activation(small[:, 66:70:2], small[:, 61:65:2], ACT.Ln, bias=eps[:, 0:1]
            ).then_inc(act_step.sem, act_step.up())
            act.wait_ge(act_step.sem, act_step.now())
            nc.scalar.activation(small[:, 70:74:2], small[:, 66:70:2], ACT.Exp, scale=-0.5
            ).then_inc(ki_rstd.sem, ki_rstd.up())
            act.wait_ge(ki_rstd.sem, ki_rstd.now())
            hi_until(act, 5)
            act.wait_ge(xt_done.sem, xt_done.due(act))
            nc.scalar.activation(xh[:, 0:2, :], cqt, ACT.Copy).then_inc(xh_done.sem, xh_done.up())
            act.wait_ge(xh_done.sem, xh_done.now())
            hi_until(act, 6)
            act.wait_ge(used, 4)
            for b in range(4):
                ins = nc.scalar.activation(iq[:, b // 2, b % 2 * 512:b % 2 * 512 + 512], ps[:, b, :], ACT.Copy)
                if b < 3:
                    ins.then_inc(act_step.sem, act_step.up())
                    act.wait_ge(act_step.sem, act_step.now())
            ins.then_inc(iq_copied.sem, iq_copied.up())
            act.wait_ge(iq_copied.sem, iq_copied.now())
            hi_until(act, 7)
            for c in range(4):
                act.wait_ge(iqt_ps.sem, iqt_ps.due(act))
                nc.scalar.activation(two(iqt, c), bank2(c), ACT.Copy).then_inc(iqt_done.sem, iqt_done.up())
                act.wait_ge(iqt_done.sem, iqt_done.now())
            hi_until(act, 8)
            for p in range(IH // 2):
                act.wait_ge(ix_ps.sem, ix_ps.due(act))
                if p >= 2:
                    act.wait_ge(relu_used.sem, relu_used.due(act))
                nc.scalar.activation(relu[:, p % 2, :, :], ps[:, 2 * (p % 2):2 * (p % 2) + 2, 0:3 * P], ACT.Relu
                ).then_inc(relu_done.sem, relu_done.up())
                act.wait_ge(relu_done.sem, relu_done.now())
            relu_used.skip(act, 2)
            for c in range(4):
                act.wait_ge(qt_ps.sem, qt_ps.due(act))
                nc.scalar.activation(two(qt, c), bank2(4 + c), ACT.Copy).then_inc(qt_done.sem, qt_done.up())
                act.wait_ge(qt_done.sem, qt_done.now())

            def outputs(i):
                nc.scalar.activation(xh[:, i, :], ps[:, 6 + i % 2, 0:T], ACT.Copy
                ).then_inc(oh_done.sem, oh_done.up())
                act.wait_ge(oh_done.sem, oh_done.now())

            attend_act(act, HEADS // 2, HD ** -0.5, outputs)


        def dsa_dve(dve):
            dve.wait_ge(used, 2)
            V.tensor_copy(kr, bank2(1)).then_inc(dve_step.sem, dve_step.up())
            dve.wait_ge(dve_step.sem, dve_step.now())
            dve.wait_ge(trig_done.sem, trig_done.due(dve))
            for t in range(2):
                rope(dve, kr[:, t, 0:P].rearrange("p (h f) -> p h f", h=KVH), cs_q(t), KVH, ROT)
                for gr in range(KVH):
                    V.tensor_copy(kd[:, t, gr, :, :],
                                  kr[:, t, gr * HD:(gr + 1) * HD].unsqueeze(1).to_broadcast([P, 2, HD])
                    ).then_inc(dve_step.sem, dve_step.up())
                    dve.wait_ge(dve_step.sem, dve_step.now())
            dve.wait_ge(used, 3)
            for t in range(2):
                key = ps[:, 2, t * T + 120:t * T + 248]
                V.bn_stats(small[:, 40 + 6 * t:46 + 6 * t], key).then_inc(dve_step.sem, dve_step.up())
                dve.wait_ge(dve_step.sem, dve_step.now())
                V.bn_aggr(small[:, 60 + 2 * t:62 + 2 * t], small[:, 40 + 6 * t:46 + 6 * t]
                ).then_inc(dve_step.sem, dve_step.up())
                dve.wait_ge(dve_step.sem, dve_step.now())
            V.tensor_copy(small[:, 74:78], small[:, 60:64]).then_inc(ki_var.sem, ki_var.up())
            dve.wait_ge(ki_var.sem, ki_var.now())
            V.tensor_scalar(wi, bank2(2)[:, :, 248:256], float(IH ** -0.5 * ID ** -0.5), None, ALU.mult
            ).then_inc(dve_step.sem, dve_step.up())
            dve.wait_ge(dve_step.sem, dve_step.now())
            dve.wait_ge(ki_rstd.sem, ki_rstd.due(dve))
            for t in range(2):
                key = ps[:, 2, t * T + 120:t * T + 248]
                V.tensor_scalar(kis[:, t, :], key, small[:, 60 + 2 * t:61 + 2 * t],
                                small[:, 70 + 2 * t:71 + 2 * t], ALU.subtract, ALU.mult
                ).then_inc(dve_step.sem, dve_step.up())
                dve.wait_ge(dve_step.sem, dve_step.now())
            V.tensor_tensor(kis, kis, kg[:, 0:1, :].to_broadcast([P, 2, P]), ALU.mult
            ).then_inc(dve_step.sem, dve_step.up())
            dve.wait_ge(dve_step.sem, dve_step.now())
            V.tensor_tensor(kis, kis, kg[:, 1:2, :].to_broadcast([P, 2, P]), ALU.add
            ).then_inc(dve_step.sem, dve_step.up())
            dve.wait_ge(dve_step.sem, dve_step.now())
            for t in range(2):
                rope(dve, kis[:, t, :].unsqueeze(1), cs_i(t), 1, IROT)
            V.tensor_copy(small[:, 78:80], small[:, 60:62]).then_inc(kd_ready.sem, kd_ready.up())
            dve.wait_ge(kd_ready.sem, kd_ready.now())
            dve.wait_ge(kt_ps.sem, kt_ps.due(dve))
            for e in range(2):
                V.tensor_copy(kpad[e * HD:(e + 1) * HD, :, e, :], bank2(5)[e * HD:(e + 1) * HD, :, :]
                ).then_inc(dve_step.sem, dve_step.up())
                dve.wait_ge(dve_step.sem, dve_step.now())
            V.tensor_copy(kit, ps[:, 6, 0:T]).then_inc(dve_step.sem, dve_step.up())
            dve.wait_ge(dve_step.sem, dve_step.now())
            dve.wait_ge(cqt_ps.sem, cqt_ps.due(dve))
            for k in range(2):
                ins = V.tensor_scalar(cqt[:, k, :], ps[:, 4, k * T:(k + 1) * T], gt[:, 140 + k:141 + k], None, ALU.mult)
                if k == 0:
                    ins.then_inc(dve_step.sem, dve_step.up())
                    dve.wait_ge(dve_step.sem, dve_step.now())
            ins.then_inc(xt_done.sem, xt_done.up())
            dve.wait_ge(xt_done.sem, xt_done.now())
            dve.wait_ge(xh_done.sem, xh_done.due(dve))
            V.tensor_tensor(xl[:, 0:2, :], cqt, xh[:, 0:2, :].bitcast(F32), ALU.subtract
            ).then_inc(x_ready.sem, x_ready.up())
            dve.wait_ge(x_ready.sem, x_ready.now())
            dve.wait_ge(iq_copied.sem, iq_copied.due(dve))
            for t in range(2):
                rope(dve, iq[:, t, :].rearrange("p (h f) -> p h f", h=IH), cs_i(t), IH, IROT)
            V.tensor_copy(small[:, 80:82], small[:, 60:62]).then_inc(iq_rot.sem, iq_rot.up())
            dve.wait_ge(iq_rot.sem, iq_rot.now())
            dve.wait_ge(used, 5)
            for b in range(4):
                V.tensor_copy(q[:, b // 2, b % 2 * 512:b % 2 * 512 + 512], ps[:, 4 + b, :]
                ).then_inc(dve_step.sem, dve_step.up())
                dve.wait_ge(dve_step.sem, dve_step.now())
            for t in range(2):
                rope(dve, q[:, t, :].rearrange("p (h f) -> p h f", h=HEADS), cs_q(t), HEADS, ROT)
            V.tensor_copy(small[:, 80:82], small[:, 60:62]).then_inc(q_rot.sem, q_rot.up())
            dve.wait_ge(q_rot.sem, q_rot.now())
            for p in range(IH // 2):
                dve.wait_ge(relu_done.sem, relu_done.due(dve))
                for e in range(2):
                    h = 2 * p + e
                    for t, (c0, c1) in enumerate(((0, P), (P, 3 * P))):
                        x, w = relu[:, p % 2, e, c0:c1], wi[:, t, h:h + 1]
                        if h == 0:
                            ins = V.tensor_scalar(score[:, c0:c1], x, w, None, ALU.mult)
                        else:
                            ins = V.scalar_tensor_tensor(out=score[:, c0:c1], in0=x, scalar=w, in1=score[:, c0:c1],
                                                         op0=ALU.mult, op1=ALU.add)
                        if (e, t) != (1, 1):
                            ins.then_inc(dve_step.sem, dve_step.up())
                            dve.wait_ge(dve_step.sem, dve_step.now())
                ins.then_inc(relu_used.sem, relu_used.up())
                dve.wait_ge(relu_used.sem, relu_used.now())
            V.tensor_copy(small[:, 80:82], small[:, 60:62]).then_inc(score_done.sem, score_done.up())
            dve.wait_ge(score_done.sem, score_done.now())
            dve.wait_ge(score_cut.sem, score_cut.due(dve))
            for _ in range(TOPK // 8):
                for t, (c0, c1) in enumerate(((0, P), (P, 3 * P))):
                    V.max(top8[:, t, :], score[:, c0:c1]).then_inc(dve_step.sem, dve_step.up())
                    dve.wait_ge(dve_step.sem, dve_step.now())
                    V.match_replace(score[:, c0:c1], top8[:, t, :], score[:, c0:c1], TAKEN
                    ).then_inc(dve_step.sem, dve_step.up())
                    dve.wait_ge(dve_step.sem, dve_step.now())
            V.tensor_scalar(sbias[:], score, TAKEN, -BIG, ALU.not_equal, ALU.mult
            ).then_inc(sel_done.sem, sel_done.up())
            dve.wait_ge(sel_done.sem, sel_done.now())
            dve.wait_ge(bias_ready.sem, bias_ready.due(dve))

            def outputs(i):
                V.tensor_tensor(xl[:, i, :], ps[:, 6 + i % 2, 0:T], xh[:, i, :].bitcast(F32), ALU.subtract
                ).then_inc(x_ready.sem, x_ready.up())
                dve.wait_ge(x_ready.sem, x_ready.now())

            attend_dve(dve, HEADS // 2, HD ** -0.5, sbias[:], outputs)

        def dsa_pool(pool):
            pool.wait_ge(score_done.sem, score_done.due(pool))
            for x, fill, done in ((score, NOT_CAUSAL, score_cut), (sbias[:], -BIG, bias_ready)):
                if done is bias_ready:
                    pool.wait_ge(sel_done.sem, sel_done.due(pool))
                nc.gpsimd.affine_select(out=x[:, 0:P], in_=x[:, 0:P], compare_op=ALU.is_ge, fill=fill, base=0,
                                        pattern=[[-1, P]], channel_multiplier=1
                ).then_inc(pool_step.sem, pool_step.up())
                pool.wait_ge(pool_step.sem, pool_step.now())
                nc.gpsimd.affine_select(out=x[:, 2 * P:3 * P], in_=x[:, 2 * P:3 * P], compare_op=ALU.is_ge,
                                        fill=fill, base=0, pattern=[[-1, P]], channel_multiplier=1
                ).then_inc(done.sem, done.up())
                pool.wait_ge(done.sem, done.now())

        def spread(x, k=2):
            return x.unsqueeze(1).to_broadcast([P, k, T])

        def ln_pe(pe):
            for c in range(4):
                pe.wait_ge(r_ready.sem, r_ready.due(pe))
                for k in range(2):
                    last = mm(ps[:, 0, 0:T], mean_d[:], r[:, 2 * c + k, :], start=c + k == 0, stop=c + k == 4)
            last.then_inc(mean_ps.sem, mean_ps.up())
            for c in range(4):
                pe.wait_ge(sq_ready.sem, sq_ready.due(pe))
                for k in range(2):
                    last = mm(ps[:, 1, 0:T], mean_d[:], sq[:, 2 * (c % 2) + k, :], start=c + k == 0, stop=c + k == 4)
                last.then_inc(sq_used.sem, sq_used.up())

        def ln_act(act, last, more=True):
            hi_until(act, last + 3)
            for c in range(4):
                act.wait_ge(d_ready.sem, d_ready.due(act))
                if c >= 2:
                    act.wait_ge(sq_used.sem, sq_used.due(act))
                nc.scalar.activation(two(sq, c % 2), two(r, c), ACT.Square
                ).then_inc(sq_ready.sem, sq_ready.up())
                act.wait_ge(sq_ready.sem, sq_ready.now())
            hi_until(act, last + 4)
            act.wait_ge(sq_used.sem, sq_used.due(act, 2))
            nc.scalar.preload_act_table_set("natural_log_exp_and_others")
            nc.scalar.activation(rs, ps[:, 1, 0:T], ACT.Ln, bias=eps[:, 0:1]
            ).then_inc(act_step.sem, act_step.up())
            act.wait_ge(act_step.sem, act_step.now())
            nc.scalar.activation(rs, rs, ACT.Exp, scale=-0.5).then_inc(rs_ready.sem, rs_ready.up())
            act.wait_ge(rs_ready.sem, rs_ready.now())
            if more:
                x_act(act)

        def ln_dve(dve, gain, bias, arrived, more=True):
            for c in range(4):
                arrived(dve, c)
                V.scalar_tensor_tensor(out=two(r, c), in0=two(xt, c), scalar=ALPHA, in1=bank2(4 + c),
                                       op0=ALU.mult, op1=ALU.add).then_inc(r_ready.sem, r_ready.up())
                dve.wait_ge(r_ready.sem, r_ready.now())
            dve.wait_ge(mean_ps.sem, mean_ps.due(dve))
            for c in range(4):
                V.tensor_tensor(two(r, c), two(r, c), spread(ps[:, 0, 0:T]), ALU.subtract
                ).then_inc(d_ready.sem, d_ready.up())
                dve.wait_ge(d_ready.sem, d_ready.now())
            dve.wait_ge(rs_ready.sem, rs_ready.due(dve))
            for c in range(4):
                V.tensor_tensor(two(r, c), two(r, c), spread(rs), ALU.mult
                ).then_inc(dve_step.sem, dve_step.up())
                dve.wait_ge(dve_step.sem, dve_step.now())
                for k in (2 * c, 2 * c + 1):
                    ins = V.tensor_scalar(xt[:, k, :], r[:, k, :], gt[:, gain + k:gain + k + 1],
                                          gt[:, bias + k:bias + k + 1], ALU.mult, ALU.add)
                    if k % 2 == 0:
                        ins.then_inc(dve_step.sem, dve_step.up())
                        dve.wait_ge(dve_step.sem, dve_step.now())
                if more:
                    ins.then_inc(xt_done.sem, xt_done.up())
                    dve.wait_ge(xt_done.sem, xt_done.now())
                else:
                    ins.then_inc(dve_step.sem, dve_step.up())
                    dve.wait_ge(dve_step.sem, dve_step.now())
                if c and more:
                    x_lo(dve, c - 1)
            if more:
                x_lo(dve, 3)
            else:
                V.tensor_copy(small[:, 80:82], small[:, 60:62]).then_inc(stream.sem, stream.up())
                dve.wait_ge(stream.sem, stream.now())

        def times(i, k):
            return 0 if i is None else i * k

        def ffn_pe(pe, base, xs=4):
            pe.wait_ge(x_ready.sem, x_ready.due(pe, xs))
            seen = h_ready.seen(pe)

            def pair(p, i=None):
                if p >= 2:
                    pe.wait_ge(h_ready.sem, times(i, 2) + (seen + p - 1))
                tile_a(pe, base + 2 * p, 2 * (p % 2), i=i)
                tile_a(pe, base + 2 * p + 1, 2 * (p % 2) + 1, i=i)

            PAIRS = NF // 2
            pair(0)
            pair(1)
            loops = (PAIRS - 2) // 2
            with pe.Fori(0, loops) as i:
                for j in range(2):
                    pair(2 + j, i)
            for p in range(2 + 2 * loops, PAIRS):
                pair(p)
            down = base + NF

            def products(n, j, i, ms, s=None):
                for m in ms:
                    for k in range(2):
                        o = k * D + m * P
                        f = times(i, 2 * RING) + (2 * j + k)
                        first = i is None and j + k == 0
                        x, y = ((hh[:, f, :], hl[:, f, :]) if i is None else
                                (hh[:, bass.ds(f, 1), :], hl[:, bass.ds(f, 1), :]))
                        last = mm3(ps[:, 4 + m // 2, m % 2 * T:(m % 2 + 1) * T],
                                   (wh[:, ring(n), o:o + P], wl[:, ring(n), o:o + P]), (x, y),
                                   first and m % 2 == 0, j == PAIRS - 1 and k == 1, skip=True)
                return last

            def tile(j, i=None):
                pe.wait_ge(h_ready.sem, times(i, RING) + (seen + j + 1))
                pe.wait_ge(lo_done, times(i, RING) + (down + j + 1))
                products(down + j, j, i, range(KD)).then_inc(used, 1)

            tile(0)
            with pe.Fori(0, (PAIRS - 3) // RING) as i:
                for j in range(1, 1 + RING):
                    tile(j, i)
            pe.wait_ge(h_ready.sem, seen + PAIRS)
            pe.wait_ge(lo_done, down + PAIRS)
            for m in range(KD):
                last = products(down + PAIRS - 2, PAIRS - 2, None, [m])
                if m == KD - 1:
                    last.then_inc(used, 1)
                last = products(down + PAIRS - 1, PAIRS - 1, None, [m])
                if m == KD - 1:
                    last.then_inc(used, 1)
                elif m % 2:
                    last.then_inc(y_done.sem, y_done.up())
            h_ready.skip(pe, PAIRS)

        def ffn_act(act, base):
            seen, mul = used, h_ready.seen(act)
            PAIRS = NF // 2

            def pair(p, i=None):
                n = base + 2 * p
                hi_at(act, n + 3, i)
                act.wait_ge(used, times(i, 4) + (n + 1))
                if p >= 2:
                    act.wait_ge(h_ready.sem, times(i, 2) + (mul + p - 1))
                nc.scalar.activation(silu_g[:, p % 2, :], ps[:, 2 * (p % 2), :], ACT.Silu).then_inc(s_done.sem, 1)
                hi_at(act, n + 4, i)

            def hi_at(act, n, i):
                if i is None:
                    hi_until(act, n)
                else:
                    hi(act, n, i)

            hi_until(act, base + 2)
            nc.scalar.preload_act_table(ACT.Silu)
            pair(0)
            pair(1)
            loops = (PAIRS - 2) // 2
            his_save = his[0]
            assert his_save == base + 7, his_save - base
            with act.Fori(0, loops) as i:
                for j in range(2):
                    pair(2 + j, i)
            his[0] = his_save + 4 * loops
            for p in range(2 + 2 * loops, PAIRS):
                pair(p)
            h_ready.skip(act, PAIRS)
            s_done.n += PAIRS
            down = base + NF
            n0 = his[0]
            loops = (PAIRS - 3) // RING
            with act.Fori(0, loops) as i:
                for j in range(RING):
                    hi(act, n0 + j, i)
            his[0] = n0 + RING * loops
            hi_until(act, down + PAIRS)

        def ffn_dve(dve, base):
            PAIRS = NF // 2
            s0, m0, u0 = s_done.seen(dve), h_mul.n, h_hi.n

            def pair(p, i=None):
                dve.wait_ge(s_done.sem, times(i, 2) + (s0 + p + 1))
                dve.wait_ge(used, times(i, 4) + (base + 2 * p + 2))
                nc.vector.tensor_tensor(hf[:, p % 2, :], silu_g[:, p % 2, :], ps[:, 2 * (p % 2) + 1, :],
                                        ALU.mult).then_inc(h_mul.sem, 1)
                dve.wait_ge(h_mul.sem, times(i, 2) + (m0 + p + 1))
                f = times(i, 4) + 2 * p
                x = (hh[:, f:f + 2, :], hl[:, f:f + 2, :]) if i is None else (
                    hh[:, bass.ds(f, 2), :], hl[:, bass.ds(f, 2), :])
                y = hf[:, p % 2, :].rearrange("p (k t) -> p k t", k=2)
                nc.vector.tensor_copy(x[0], y).then_inc(h_hi.sem, 1)
                dve.wait_ge(h_hi.sem, times(i, 2) + (u0 + p + 1))
                nc.vector.tensor_tensor(x[1], y, x[0].bitcast(F32), ALU.subtract).then_inc(h_ready.sem, 1)
                dve.wait_ge(h_ready.sem, times(i, 2) + (r0 + p + 1))

            r0 = h_ready.n
            pair(0)
            pair(1)
            loops = (PAIRS - 2) // 2
            with dve.Fori(0, loops) as i:
                for j in range(2):
                    pair(2 + j, i)
            for p in range(2 + 2 * loops, PAIRS):
                pair(p)
            for x in (h_mul, h_hi, h_ready):
                x.n += PAIRS
            s_done.skip(dve, PAIRS)

        def ffn_arrived(base):
            def arrived(dve, c):
                if c < 3:
                    dve.wait_ge(y_done.sem, y_done.due(dve))
                else:
                    dve.wait_ge(used, base + NF + NF // 2)
            return arrived

        def out_arrived(base):
            def arrived(dve, c):
                dve.wait_ge(used, base + c + 1)
            return arrived

        def flat(x):
            return x.rearrange("p a b -> p (a b)")

        def hgrn_pe(pe):
            pe.wait_ge(x_ready.sem, x_ready.due(pe, 4))
            for j in range(4):
                tile_b(pe, t_hi + j, [(t, 0, ps[:, j, t * T:(t + 1) * T]) for t in range(2)])
            for o, n in enumerate((*range(t_hq, t_hq + 4), *range(t_hf, t_hf + 4), *range(t_hg, t_hg + 4))):
                evacuated = hg_v if o < 4 else hg_a
                pe.wait_ge(evacuated.sem, evacuated.due(pe))
                tile_a(pe, n, o % 4)
            pe.wait_ge(hg_a.sem, hg_a.due(pe, 4))
            for p in range(KD // 2):
                pe.wait_ge(hg_p.sem, hg_p.due(pe, 8))
                for e in range(2):
                    h = 2 * p + e
                    for i in range(2):
                        b = 2 * i
                        if h >= 1:
                            pe.wait_ge(hg_free.sem, hg_free.due(pe))
                        x = slice(i * P, (i + 1) * P)
                        for l in range(8):
                            k_, q_ = (hk[:, h, x], hq[:, h, x]) if l == 0 else (lev[:, l, e, x], lev[:, l, e, x])
                            last = mm(ps[:, b + l // 4, l % 4 * P:(l % 4 + 1) * P], k_, q_, start=True, stop=True)
                        if i == 0:
                            last = mm(ps[:, 4, e * P:(e + 1) * P], lev[:, 0, e, 0:P], lev[:, 0, e, P:T],
                                      start=True, stop=True)
                        last.then_inc(hg_ps.sem, hg_ps.up())
                    pe.wait_ge(hg_at.sem, hg_at.due(pe))
                    o_ = ps[:, 6 + p % 2, e * T:(e + 1) * T]
                    val = [hv[:, t, h * P:(h + 1) * P] for t in range(2)]
                    mm(o_[:, 0:P], val[0], at_h[:, e, 0, :], start=True, stop=True)
                    mm(o_[:, P:T], val[0], at_h[:, e, 2, :], start=True, stop=False)
                    last = mm(o_[:, P:T], val[1], at_h[:, e, 1, :], start=False, stop=True)
                last.then_inc(hg_o.sem, hg_o.up())
                pe.wait_ge(hg_sq.sem, hg_sq.due(pe))
                mm(ps[:, 5, :], mean_hd[:], o_tmp, start=True, stop=True).then_inc(hg_mean.sem, hg_mean.up())
            pe.wait_ge(hg_free.sem, hg_free.due(pe, 2))
            out_pe(pe, t_hwo, moving=4)

        def hgrn_act(act):
            nc.scalar.preload_act_table(ACT.Silu)
            for func, to, t0 in ((ACT.Silu, hq, t_hq), (ACT.Sigmoid, hk, t_hf), (ACT.Silu, hgate, t_hg)):
                for j in range(4):
                    hi_until(act, t0 + j + 3)
                    act.wait_ge(used, t0 + j + 1)
                    nc.scalar.activation(two(to, j), bank2(j), func).then_inc(hg_a.sem, hg_a.up())
                    act.wait_ge(hg_a.sem, hg_a.now())
            hi_until(act, t_hg + 7)
            nc.scalar.preload_act_table_set("natural_log_exp_and_others")
            act.wait_ge(hg_g.sem, hg_g.due(act))
            for j in range(4):
                nc.scalar.activation(two(hb, j), two(hb, j), ACT.Ln).then_inc(hg_ln.sem, hg_ln.up())
                act.wait_ge(hg_ln.sem, hg_ln.now())
            for p in range(KD // 2):
                for l in range(8):
                    act.wait_ge(hg_d.sem, hg_d.due(act))
                    nc.scalar.activation(dec[:, l % 2, :], dec[:, l % 2, :], ACT.Exp
                    ).then_inc(hg_e.sem, hg_e.up())
                    act.wait_ge(hg_e.sem, hg_e.now())
                act.wait_ge(hg_o.sem, hg_o.due(act))
                nc.scalar.activation(o_tmp, ps[:, 6 + p % 2, :], ACT.Square).then_inc(hg_sq.sem, hg_sq.up())
                act.wait_ge(hg_sq.sem, hg_sq.now())
                act.wait_ge(hg_mean.sem, hg_mean.due(act))
                nc.scalar.activation(o_tmp, ps[:, 5, :], ACT.Ln, bias=eps[:, 1:2]
                ).then_inc(act_step.sem, act_step.up())
                act.wait_ge(act_step.sem, act_step.now())
                nc.scalar.activation(o_tmp, o_tmp, ACT.Exp, scale=-0.5).then_inc(hg_rs.sem, hg_rs.up())
                act.wait_ge(hg_rs.sem, hg_rs.now())
                act.wait_ge(xt_done.sem, xt_done.due(act))
                nc.scalar.activation(two(xh, p), two(hgate, p), ACT.Copy).then_inc(xh_done.sem, xh_done.up())
                act.wait_ge(xh_done.sem, xh_done.now())

        def hgrn_pool(pool):
            gp = nc.gpsimd
            for p in range(KD // 2):
                pool.wait_ge(hg_b.sem, hg_b.due(pool))
                x = flat(hb[:, 2 * p:2 * p + 2, :])
                for l, d in enumerate(LEVELS):
                    y = dec[:, l % 2, :]
                    if p or l >= 2:
                        pool.wait_ge(hg_p.sem, hg_p.due(pool))
                    if d == 2 * CH:
                        xc = x.rearrange("p (h c t) -> p h c t", h=2, c=NCH)
                        yc = y.rearrange("p (h c t) -> p h c t", h=2, c=NCH)

                        def end(c):
                            return xc[:, :, c, CH - 1:CH].to_broadcast([P, 2, CH])

                        gp.tensor_tensor(yc[:, :, 0, :], end(0), xc[:, :, 0, :], ALU.subtract
                        ).then_inc(pool_step.sem, pool_step.up())
                        pool.wait_ge(pool_step.sem, pool_step.now())
                        gp.tensor_tensor(yc[:, :, 0, :], yc[:, :, 0, :], end(1), ALU.add
                        ).then_inc(pool_step.sem, pool_step.up())
                        pool.wait_ge(pool_step.sem, pool_step.now())
                        gp.tensor_tensor(yc[:, :, 1, :], end(1), xc[:, :, 1, :], ALU.subtract
                        ).then_inc(pool_step.sem, pool_step.up())
                        pool.wait_ge(pool_step.sem, pool_step.now())
                        gp.tensor_scalar(yc[:, :, 2, :], xc[:, :, 2, :], 1.0, 0.0, ALU.mult, ALU.add
                        ).then_inc(pool_step.sem, pool_step.up())
                        pool.wait_ge(pool_step.sem, pool_step.now())
                        gp.tensor_tensor(yc[:, :, 3, :], xc[:, :, 3, :], end(2), ALU.add
                        ).then_inc(hg_d.sem, hg_d.up())
                        pool.wait_ge(hg_d.sem, hg_d.now())
                        continue
                    xb, yb = (w.rearrange("p (n w) -> p n w", w=2 * d) for w in (x, y))
                    mid = xb[:, :, d - 1:d].to_broadcast([P, 256 // d, d])
                    gp.tensor_tensor(yb[:, :, 0:d], mid, xb[:, :, 0:d], ALU.subtract
                    ).then_inc(pool_step.sem, pool_step.up())
                    pool.wait_ge(pool_step.sem, pool_step.now())
                    if d == CH:
                        gp.tensor_scalar(yb[:, :, d:2 * d], xb[:, :, d:2 * d], 1.0, 0.0, ALU.mult, ALU.add
                        ).then_inc(hg_d.sem, hg_d.up())
                        pool.wait_ge(hg_d.sem, hg_d.now())
                    else:
                        gp.tensor_tensor(yb[:, :, d:2 * d], xb[:, :, d:2 * d], mid, ALU.subtract
                        ).then_inc(hg_d.sem, hg_d.up())
                        pool.wait_ge(hg_d.sem, hg_d.now())
            pool.wait_ge(hg_p.sem, hg_p.due(pool, 2))

        def hgrn_dve(dve):
            for j in range(4):
                dve.wait_ge(used, t_hi + j + 1)
                V.tensor_copy(hv[:, :, j * T:(j + 1) * T], bank2(j)).then_inc(hg_v.sem, hg_v.up())
                dve.wait_ge(hg_v.sem, hg_v.now())
            dve.wait_ge(hg_a.sem, hg_a.due(dve, 8))
            for h in range(KD):
                V.tensor_scalar(hb[:, h, :], hk[:, h, :], one_lb[:, h:h + 1], lb[:, h:h + 1], ALU.mult, ALU.add
                ).then_inc(dve_step.sem, dve_step.up())
                dve.wait_ge(dve_step.sem, dve_step.now())
            V.tensor_scalar(flat(hk), flat(hb), -1.0, 1.0, ALU.mult, ALU.add).then_inc(hg_g.sem, hg_g.up())
            dve.wait_ge(hg_g.sem, hg_g.now())
            dve.wait_ge(hg_a.sem, hg_a.due(dve, 4))
            for p in range(KD // 2):
                dve.wait_ge(hg_ln.sem, hg_ln.due(dve))
                for h in (2 * p, 2 * p + 1):
                    ins = V.tensor_tensor_scan(hb[:, h, :], restart[:], hb[:, h, :], 0.0, ALU.mult, ALU.add)
                    if h % 2 == 0:
                        ins.then_inc(dve_step.sem, dve_step.up())
                        dve.wait_ge(dve_step.sem, dve_step.now())
                ins.then_inc(hg_b.sem, hg_b.up())
                dve.wait_ge(hg_b.sem, hg_b.now())
            for p in range(KD // 2):
                for l, d in enumerate(LEVELS):
                    dve.wait_ge(hg_e.sem, hg_e.due(dve))
                    y, e = (w.rearrange("p (n w) -> p n w", w=2 * d) for w in (flat(lev[:, l, :, :]), dec[:, l % 2, :]))
                    k_, q_ = (flat(w[:, 2 * p:2 * p + 2, :]).rearrange("p (n w) -> p n w", w=2 * d) for w in (hk, hq))
                    V.tensor_tensor(y[:, :, 0:d], k_[:, :, 0:d], e[:, :, 0:d], ALU.mult
                    ).then_inc(dve_step.sem, dve_step.up())
                    dve.wait_ge(dve_step.sem, dve_step.now())
                    V.tensor_tensor(y[:, :, d:2 * d], q_[:, :, d:2 * d], e[:, :, d:2 * d], ALU.mult
                    ).then_inc(hg_p.sem, hg_p.up())
                    dve.wait_ge(hg_p.sem, hg_p.now())
                for e in range(2):
                    for i in range(2):
                        dve.wait_ge(hg_ps.sem, hg_ps.due(dve))
                        V.tensor_tensor(masked_a, ps[:, 2 * i:2 * i + 2, :].rearrange("p b (l t) -> p (b l) t", t=P),
                                        lmask[:], ALU.mult).then_inc(hg_free.sem, hg_free.up())
                        dve.wait_ge(hg_free.sem, hg_free.now())
                        V.tensor_reduce(at_h[:, e, i, :], masked_a.rearrange("p l t -> p t l"), AX.X, ALU.add
                        ).then_inc(dve_step.sem, dve_step.up())
                        dve.wait_ge(dve_step.sem, dve_step.now())
                    V.tensor_copy(at_h[:, e, 2, :], ps[:, 4, e * P:(e + 1) * P]).then_inc(hg_at.sem, hg_at.up())
                    dve.wait_ge(hg_at.sem, hg_at.now())
                dve.wait_ge(hg_rs.sem, hg_rs.due(dve))
                V.scalar_tensor_tensor(out=o_tmp, in0=ps[:, 6 + p % 2, :], scalar=gt[:, 139:140], in1=o_tmp,
                                       op0=ALU.mult, op1=ALU.mult).then_inc(dve_step.sem, dve_step.up())
                dve.wait_ge(dve_step.sem, dve_step.now())
                V.tensor_tensor(flat(two(hgate, p)), o_tmp, flat(two(hgate, p)), ALU.mult
                ).then_inc(xt_done.sem, xt_done.up())
                dve.wait_ge(xt_done.sem, xt_done.now())
                x_lo(dve, p, hgate)

        def rms_pe(pe):
            for c in range(4):
                pe.wait_ge(sq_ready.sem, sq_ready.due(pe))
                for k in range(2):
                    last = mm(ps[:, 1, 0:T], mean_d[:], sq[:, 2 * (c % 2) + k, :], start=c + k == 0, stop=c + k == 4)
                last.then_inc(sq_used.sem, sq_used.up())

        def rms_act(act, source, last):
            hi_until(act, last + 3)
            for c in range(4):
                x = source(act, c)
                if c >= 2:
                    act.wait_ge(sq_used.sem, sq_used.due(act))
                nc.scalar.activation(two(sq, c % 2), x, ACT.Square).then_inc(sq_ready.sem, sq_ready.up())
                act.wait_ge(sq_ready.sem, sq_ready.now())
            hi_until(act, last + 4)
            act.wait_ge(sq_used.sem, sq_used.due(act, 2))
            nc.scalar.preload_act_table_set("natural_log_exp_and_others")
            nc.scalar.activation(rs, ps[:, 1, 0:T], ACT.Ln, bias=eps[:, 1:2]
            ).then_inc(act_step.sem, act_step.up())
            act.wait_ge(act_step.sem, act_step.now())
            nc.scalar.activation(rs, rs, ACT.Exp, scale=-0.5).then_inc(rs_ready.sem, rs_ready.up())
            act.wait_ge(rs_ready.sem, rs_ready.now())

        def pre_dve(dve, gain):
            dve.wait_ge(rs_ready.sem, rs_ready.due(dve))
            for c in range(4):
                V.tensor_tensor(two(r, c), two(xt, c), spread(rs), ALU.mult
                ).then_inc(dve_step.sem, dve_step.up())
                dve.wait_ge(dve_step.sem, dve_step.now())
                for k in (2 * c, 2 * c + 1):
                    ins = V.tensor_scalar(r[:, k, :], r[:, k, :], gt[:, gain + k:gain + k + 1], None, ALU.mult)
                    if k % 2 == 0:
                        ins.then_inc(dve_step.sem, dve_step.up())
                        dve.wait_ge(dve_step.sem, dve_step.now())
                ins.then_inc(xt_done.sem, xt_done.up())
                dve.wait_ge(xt_done.sem, xt_done.now())
                if c:
                    x_lo(dve, c - 1, r)
            x_lo(dve, 3, r)

        def from_x(act, c):
            if c == 0:
                act.wait_ge(stream.sem, stream.due(act))
            return two(xt, c)

        def post_dve(dve, gain):
            dve.wait_ge(rs_ready.sem, rs_ready.due(dve))
            for c in range(4):
                V.tensor_tensor(two(r, c), bank2(4 + c), spread(rs), ALU.mult
                ).then_inc(dve_step.sem, dve_step.up())
                dve.wait_ge(dve_step.sem, dve_step.now())
                for k in (2 * c, 2 * c + 1):
                    V.scalar_tensor_tensor(out=xt[:, k, :], in0=r[:, k, :], scalar=gt[:, gain + k:gain + k + 1],
                                           in1=xt[:, k, :], op0=ALU.mult, op1=ALU.add
                    ).then_inc(dve_step.sem, dve_step.up())
                    dve.wait_ge(dve_step.sem, dve_step.now())
            V.tensor_copy(small[:, 80:82], small[:, 60:62]).then_inc(stream.sem, stream.up())
            dve.wait_ge(stream.sem, stream.now())

        B2_EVAC = "ddd" + "dddd" + "aaaa" + "aaaa" + "aaaaaaaa"

        def gla_pe(pe):
            pe.wait_ge(x_ready.sem, x_ready.due(pe, 4))
            for o, who in enumerate(B2_EVAC):
                n = t_rest + o
                if o >= 4:
                    evacuated = b2_d if B2_EVAC[o - 4] == "d" else b2_a
                    pe.wait_ge(evacuated.sem, evacuated.due(pe))
                if o < 7:
                    tile_b(pe, n, [(t, 0, ps[:, o % 4, t * T:(t + 1) * T]) for t in range(2)])
                else:
                    tile_a(pe, n, o % 4)
            for t in range(2):
                last = nc.tensor.transpose(ps[0:GLR, 4, t * P:(t + 1) * P], tk[:, t, 0:GLR], ident[:])
            last.then_inc(ha_ps.sem, ha_ps.up())
            pe.wait_ge(ha_done.sem, ha_done.due(pe))
            for h in range(GH):
                last = mm(ps[:, 5 + h // 2, h % 2 * T:(h % 2 + 1) * T], wa[:, h * GK:(h + 1) * GK], ha,
                          start=True, stop=True)
            last.then_inc(z_ps.sem, z_ps.up())
            pe.wait_ge(gqh_done.sem, gqh_done.due(pe))
            pe.wait_ge(b2_a.sem, b2_a.due(pe, 4))

            def scores(h):
                b = ps[:, 4 + h % 2, :]
                k_ = kdec[:, h, :]
                mm(b[0:CH, 0:T], k_[:, 0:CH], gqh[:, 0, h, :], start=True, stop=True)
                mm(b[CH:P, CH:T], k_[:, CH:P], gqh[:, 1, h, CH:T], start=True, stop=True)
                mm(b[0:CH, T:T + P], k_[:, P:P + CH], gqh[:, 2, h, P:T], start=True, stop=True)
                mm(b[CH:P, T + CH:T + P], k_[:, P + CH:T], gq[:, h, P + CH:T], start=True, stop=True).then_inc(ga_ps.sem, ga_ps.up())

            scores(0)
            for h in range(GH):
                if h + 1 < GH:
                    scores(h + 1)
                pe.wait_ge(ga_at.sem, ga_at.due(pe))
                for j in range(2):
                    o_ = ps[:, 6 + h % 2, j * T:(j + 1) * T]
                    c = h * GV + j * P
                    mm(o_[:, 0:P], gv[:, 0, c:c + P], at_g[:, h % 2, 0:P], start=True, stop=True)
                    mm(o_[:, P:T], gv[:, 0, c:c + P], at_g[:, h % 2, P:T], start=True, stop=False)
                    last = mm(o_[:, P:T], gv[:, 1, c:c + P], at_g[:, h % 2, T:T + P], start=False, stop=True)
                last.then_inc(go_ps.sem, go_ps.up())
                pe.wait_ge(go_sq.sem, go_sq.due(pe))
                for j in range(2):
                    last = mm(ps[:, h % 2, 0:T], mean_hd[:], g_sq[:, h % 2, j * T:(j + 1) * T],
                              start=j == 0, stop=j == 1)
                last.then_inc(go_mean.sem, go_mean.up())
            out_pe(pe, t_gwo, moving=4)

        def gla_act(act):
            nc.scalar.preload_act_table(ACT.Silu)
            for o, who in enumerate(B2_EVAC):
                n = t_rest + o
                hi_until(act, n + 3)
                if who == "d":
                    continue
                act.wait_ge(used, n + 1)
                b = bank2(o % 4)
                j = n - t_gq
                if j < 2:
                    nc.scalar.activation(gq[:, 2 * j:2 * j + 2, :], b, ACT.Copy, scale=GK ** -0.5
                    ).then_inc(b2_a.sem, b2_a.up())
                    act.wait_ge(b2_a.sem, b2_a.now())
                elif j < 4:
                    nc.scalar.activation(gk[:, 2 * j - 4:2 * j - 2, :], b, ACT.Copy
                    ).then_inc(b2_a.sem, b2_a.up())
                    act.wait_ge(b2_a.sem, b2_a.now())
                elif j < 8:
                    nc.scalar.activation(two(sg, j - 4), b, ACT.Silu).then_inc(b2_a.sem, b2_a.up())
                    act.wait_ge(b2_a.sem, b2_a.now())
                else:
                    for k in range(2):
                        m = 2 * (j - 8) + k
                        ins = nc.scalar.activation(gates[:, m, :], b[:, k, :], ACT.Sigmoid, bias=gt[:, 96 + m:97 + m])
                        if k == 0:
                            ins.then_inc(act_step.sem, act_step.up())
                            act.wait_ge(act_step.sem, act_step.now())
                    ins.then_inc(b2_a.sem, b2_a.up())
                    act.wait_ge(b2_a.sem, b2_a.now())
            hi_until(act, t_gwo + 3)
            nc.scalar.preload_act_table_set("natural_log_exp_and_others")
            act.wait_ge(z_ps.sem, z_ps.due(act))
            for h in range(GH):
                ins = nc.scalar.activation(z[:, h * T:(h + 1) * T], ps[:, 5 + h // 2, h % 2 * T:(h % 2 + 1) * T],
                                           ACT.Identity, bias=gt[:, 128 + h:129 + h])
                if h + 1 < GH:
                    ins.then_inc(act_step.sem, act_step.up())
                    act.wait_ge(act_step.sem, act_step.now())
            ins.then_inc(z_done.sem, z_done.up())
            act.wait_ge(z_done.sem, z_done.now())
            act.wait_ge(nz_done.sem, nz_done.due(act))
            nc.scalar.activation(nz, nz, ACT.Exp).then_inc(act_step.sem, act_step.up())
            act.wait_ge(act_step.sem, act_step.now())
            nc.scalar.activation(nz, nz, ACT.Ln, bias=1.0).then_inc(sp_done.sem, sp_done.up())
            act.wait_ge(sp_done.sem, sp_done.now())
            act.wait_ge(gb_done.sem, gb_done.due(act))
            nc.scalar.activation(flat(fl), flat(fl), ACT.Exp).then_inc(act_step.sem, act_step.up())
            act.wait_ge(act_step.sem, act_step.now())
            nc.scalar.activation(flat(kdec), flat(kdec), ACT.Exp).then_inc(kdec_e.sem, kdec_e.up())
            act.wait_ge(kdec_e.sem, kdec_e.now())
            for h in range(GH):
                act.wait_ge(go_ps.sem, go_ps.due(act))
                nc.scalar.activation(g_sq[:, h % 2, :], ps[:, 6 + h % 2, :], ACT.Square
                ).then_inc(go_sq.sem, go_sq.up())
                act.wait_ge(go_sq.sem, go_sq.now())
                act.wait_ge(go_mean.sem, go_mean.due(act))
                nc.scalar.activation(g_rs[:, h % 2, :], ps[:, h % 2, 0:T], ACT.Ln, scale=0.5, bias=eps[:, 1:2]
                ).then_inc(act_step.sem, act_step.up())
                act.wait_ge(act_step.sem, act_step.now())
                nc.scalar.activation(g_rs[:, h % 2, :], g_rs[:, h % 2, :], ACT.Exp, scale=-0.5
                ).then_inc(go_rs.sem, go_rs.up())
                act.wait_ge(go_rs.sem, go_rs.now())
                act.wait_ge(xt_done.sem, xt_done.due(act))
                nc.scalar.activation(two(xh, h), two(sg, h), ACT.Copy).then_inc(xh_done.sem, xh_done.up())
                act.wait_ge(xh_done.sem, xh_done.now())

        def gla_dve(dve):
            for o, who in enumerate(B2_EVAC):
                if who != "d":
                    continue
                dve.wait_ge(used, t_rest + o + 1)
                b = bank2(o % 4)
                if o < 2:
                    V.tensor_copy(tk[:, :, o * 256:(o + 1) * 256], b).then_inc(b2_d.sem, b2_d.up())
                    dve.wait_ge(b2_d.sem, b2_d.now())
                elif o == 2:
                    V.tensor_copy(tk[:, :, 512:NREST], b[:, :, 768 - NREST:256]).then_inc(b2_d.sem, b2_d.up())
                    dve.wait_ge(b2_d.sem, b2_d.now())
                else:
                    V.tensor_copy(gv[:, :, (o - 3) * T:(o - 2) * T], b).then_inc(b2_d.sem, b2_d.up())
                    dve.wait_ge(b2_d.sem, b2_d.now())
            dve.wait_ge(ha_ps.sem, ha_ps.due(dve))
            V.tensor_copy(ha, ps[0:GLR, 4, 0:T]).then_inc(ha_done.sem, ha_done.up())
            dve.wait_ge(ha_done.sem, ha_done.now())
            dve.wait_ge(z_done.sem, z_done.due(dve))
            V.scalar_tensor_tensor(out=nz, in0=z, scalar=-1.0, in1=z, op0=ALU.mult, op1=ALU.min
            ).then_inc(nz_done.sem, nz_done.up())
            dve.wait_ge(nz_done.sem, nz_done.now())
            dve.wait_ge(sp_done.sem, sp_done.due(dve))
            V.scalar_tensor_tensor(out=z, in0=z, scalar=0.0, in1=nz, op0=ALU.min, op1=ALU.subtract
            ).then_inc(dve_step.sem, dve_step.up())
            dve.wait_ge(dve_step.sem, dve_step.now())
            V.tensor_scalar(z, z, 1.0 / 16, None, ALU.mult).then_inc(dve_step.sem, dve_step.up())
            dve.wait_ge(dve_step.sem, dve_step.now())
            for h in range(GH):
                V.tensor_tensor_scan(gb[:, h, :], restart[:], z[:, h * T:(h + 1) * T], 0.0, ALU.mult, ALU.add
                ).then_inc(dve_step.sem, dve_step.up())
                dve.wait_ge(dve_step.sem, dve_step.now())
            ends = gb[:, :, CH - 1:T:CH]
            V.tensor_copy(fl[:, :, 0:3], ends[:, :, 1:4]).then_inc(dve_step.sem, dve_step.up())
            dve.wait_ge(dve_step.sem, dve_step.now())
            V.tensor_tensor(fl[:, :, 3:5], ends[:, :, 1:3], ends[:, :, 2:4], ALU.add
            ).then_inc(dve_step.sem, dve_step.up())
            dve.wait_ge(dve_step.sem, dve_step.now())
            V.tensor_tensor(fl[:, :, 5:6], fl[:, :, 3:4], ends[:, :, 3:4], ALU.add
            ).then_inc(dve_step.sem, dve_step.up())
            dve.wait_ge(dve_step.sem, dve_step.now())
            by_chunk = flat(gb).rearrange("p (c t) -> p c t", t=CH)
            V.tensor_tensor(flat(kdec).rearrange("p (c t) -> p c t", t=CH),
                            by_chunk[:, :, CH - 1:CH].to_broadcast([P, GH * NCH, CH]), by_chunk, ALU.subtract
            ).then_inc(gb_done.sem, gb_done.up())
            dve.wait_ge(gb_done.sem, gb_done.now())
            dve.wait_ge(kdec_e.sem, kdec_e.due(dve))
            V.tensor_tensor(flat(kdec), flat(kdec), flat(gk), ALU.mult).then_inc(dve_step.sem, dve_step.up())
            dve.wait_ge(dve_step.sem, dve_step.now())
            for c0 in range(3):
                V.tensor_copy(gqh[:, c0, :, c0 * CH:(c0 + 1) * CH], gq[:, :, c0 * CH:(c0 + 1) * CH]
                ).then_inc(dve_step.sem, dve_step.up())
                dve.wait_ge(dve_step.sem, dve_step.now())
                for c in range(c0 + 1, NCH):
                    f = {(0, 1): 0, (1, 2): 1, (2, 3): 2, (0, 2): 3, (1, 3): 4, (0, 3): 5}[c0, c]
                    V.tensor_tensor(gqh[:, c0, :, c * CH:(c + 1) * CH], gq[:, :, c * CH:(c + 1) * CH],
                                    fl[:, :, f:f + 1].to_broadcast([P, GH, CH]), ALU.mult
                    ).then_inc(dve_step.sem, dve_step.up())
                    dve.wait_ge(dve_step.sem, dve_step.now())
            V.memset(at_g, 0.0).then_inc(gqh_done.sem, gqh_done.up())
            dve.wait_ge(gqh_done.sem, gqh_done.now())

            def weights(h):
                dve.wait_ge(ga_ps.sem, ga_ps.due(dve))
                b, x = ps[:, 4 + h % 2, :], at_g[:, h % 2, :]
                V.tensor_copy(x[0:CH, :], b[0:CH, 0:3 * P]).then_inc(dve_step.sem, dve_step.up())
                dve.wait_ge(dve_step.sem, dve_step.now())
                V.tensor_copy(x[CH:P, CH:T], b[CH:P, CH:T]).then_inc(dve_step.sem, dve_step.up())
                dve.wait_ge(dve_step.sem, dve_step.now())
                V.tensor_copy(x[CH:P, T + CH:T + P], b[CH:P, T + CH:T + P]).then_inc(ga_at.sem, ga_at.up())
                dve.wait_ge(ga_at.sem, ga_at.now())

            weights(0)
            for h in range(GH):
                dve.wait_ge(go_rs.sem, go_rs.due(dve))
                if h + 1 < GH:
                    weights(h + 1)
                y = g_tmp.rearrange("p (j t) -> p j t", j=2)
                V.tensor_tensor(y, bank2(6 + h % 2), spread(g_rs[:, h % 2, :]), ALU.mult
                ).then_inc(dve_step.sem, dve_step.up())
                dve.wait_ge(dve_step.sem, dve_step.now())
                for j in range(2):
                    ins = V.scalar_tensor_tensor(out=sg[:, 2 * h + j, :], in0=y[:, j, :], scalar=gt[:, 132 + j:133 + j],
                                                 in1=sg[:, 2 * h + j, :], op0=ALU.mult, op1=ALU.mult)
                    if j == 0:
                        ins.then_inc(dve_step.sem, dve_step.up())
                        dve.wait_ge(dve_step.sem, dve_step.now())
                ins.then_inc(xt_done.sem, xt_done.up())
                dve.wait_ge(xt_done.sem, xt_done.now())
                x_lo(dve, h, sg)
            for c in range(4):
                dve.wait_ge(used, t_gwo + c + 1)
                V.tensor_tensor(two(ya, c), bank2(4 + c), two(gates, c), ALU.mult
                ).then_inc(dve_step.sem, dve_step.up())
                dve.wait_ge(dve_step.sem, dve_step.now())
            V.tensor_copy(small[:, 80:82], small[:, 60:62]).then_inc(ya_done.sem, ya_done.up())
            dve.wait_ge(ya_done.sem, ya_done.now())

        def mla_pe(pe):
            pe.wait_ge(lat_scaled.sem, lat_scaled.due(pe))
            pe.wait_ge(kx_done.sem, kx_done.due(pe))
            for m in range(5):
                for t in range(2):
                    c = GLR + m * P
                    nc.tensor.transpose(ps[:, m // 2, m % 2 * T + t * P:m % 2 * T + (t + 1) * P], tk[:, t, c:c + P], ident[:])
            for x in range(2):
                for t in range(2):
                    last = nc.tensor.transpose(ps[:, 3, x * T + t * P:x * T + (t + 1) * P], kx[:, t, x, :], ident[:])
            last.then_inc(lat_ps.sem, lat_ps.up())
            pe.wait_ge(x_ready.sem, x_ready.due(pe))
            pe.wait_ge(ya_done.sem, ya_done.due(pe))
            four = (0, P, 2 * P, 3 * P)
            tile_a(pe, t_uq, 4, kt=KQ, width=512, m_cols=four)
            tile_a(pe, t_uq + 1, 6, kt=KQ, width=512, m_cols=four)
            tile_a(pe, t_uq + 2, 0, kt=KQ, width=512, m_cols=four)
            for j, (kb, vb) in enumerate(((2, 4), (6, 0))):
                n = t_ukv + j
                evacuated = m_d if j == 0 else m_a
                pe.wait_ge(evacuated.sem, evacuated.due(pe))
                tile_a(pe, n, kb, kt=2, width=1024, m_cols=tuple(h * 256 for h in range(4)), x0=3, done=False)
 
                pe.wait_ge(evacuated.sem, evacuated.due(pe))
                s = ring(n)
                for t in range(2):
                    for k in range(2):
                        x = slice(t * P, (t + 1) * P)
                        w = [y[:, s, k * 1024:(k + 1) * 1024].rearrange("p (h c) -> p h c", h=4)[:, :, MN:MN + MV]
                             for y in (wh, wl)]
                        last = mm3(ps[:, vb + t, :].rearrange("p (h c) -> p h c", h=4),
                                   (xh[:, 3 + k, x], xl[:, 3 + k, x]), w, k == 0, k == 1)
                last.then_inc(used, 1)
            pe.wait_ge(m_a.sem, m_a.due(pe, 2))
            pe.wait_ge(m_d.sem, m_d.due(pe, 3))

            def logits(i):
                for e in range(2):
                    h = 2 * i + e
                    b = 2 * (i % 2) + e
                    for t, (c0, c1) in enumerate(((0, P), (P, 3 * P))):
                        y = slice(t * P, (t + 1) * P)
                        mm(ps[:, b, c0:c1], qn[:, h, y], kn[:, h, 0:c1 - c0], start=True, stop=False)
                        for x in range(2):
                            last = mm(ps[:, b, c0:c1], rr[:, x, h // 4, y], kp[x][:, h % 4, 0:c1 - c0],
                                      start=False, stop=x == 1)
                return last

            def weighted(i, e, pt, _):
                h = 2 * i + e
                o_ = ps[:, 6 + i % 2, e * T:(e + 1) * T]
                val = [vm[:, t, h * MV:(h + 1) * MV] for t in range(2)]
                mm(o_[:, 0:P], val[0], pt[:, 0:P], start=True, stop=True)
                mm(o_[:, P:T], val[0], pt[:, P:2 * P], start=True, stop=False)
                return mm(o_[:, P:T], val[1], pt[:, 2 * P:3 * P], start=False, stop=True)

            attend_pe(pe, MH // 2, logits, weighted)
            out_pe(pe, t_mwo)
            out_pe(pe, t_out, moving=4)

        def mla_act(act):
            for i, (c0, c1) in enumerate(((GLR, GLR + QL2), (GLR + QL2, GLR + QL2 + KVL2))):
                for t in range(2):
                    nc.scalar.activation(flat(lat)[:, 0:c1 - c0], tk[:, t, c0:c1], ACT.Square,
                                         accum_out=small[:, 2 * i + t:2 * i + t + 1]
                    ).then_inc(act_step.sem, act_step.up())
                    act.wait_ge(act_step.sem, act_step.now())
                nc.scalar.activation(small[:, 4 + 2 * i:6 + 2 * i], small[:, 2 * i:2 * i + 2], ACT.Ln,
                                     scale=1.0 / (c1 - c0), bias=eps[:, 1:2]).then_inc(act_step.sem, act_step.up())
                act.wait_ge(act_step.sem, act_step.now())
                nc.scalar.activation(small[:, 4 + 2 * i:6 + 2 * i], small[:, 4 + 2 * i:6 + 2 * i], ACT.Exp, scale=-0.5
                ).then_inc(act_step.sem, act_step.up())
                act.wait_ge(act_step.sem, act_step.now())
                for t in range(2):
                    ins = nc.scalar.activation(tk[:, t, c0:c1], tk[:, t, c0:c1], ACT.Copy,
                                               scale=small[:, 4 + 2 * i + t:5 + 2 * i + t])
                    if (i, t) != (1, 1):
                        ins.then_inc(act_step.sem, act_step.up())
                        act.wait_ge(act_step.sem, act_step.now())
            ins.then_inc(lat_scaled.sem, lat_scaled.up())
            act.wait_ge(lat_scaled.sem, lat_scaled.now())
            hi_until(act, t_gwo + 7)
            act.wait_ge(xt_done.sem, xt_done.due(act))
            nc.scalar.activation(xh[:, 0:5, :], lat, ACT.Copy).then_inc(xh_done.sem, xh_done.up())
            act.wait_ge(xh_done.sem, xh_done.now())

            for j, (to, n, b) in enumerate(((qn[:, 0:4, :], t_uq + 1, 6), (qn[:, 4:8, :], t_uq + 2, 0),
                                            (kn[:, 0:4, :], t_ukv, 2), (kn[:, 4:8, :], t_ukv + 1, 6))):
                hi_until(act, n + 3)
                act.wait_ge(used, n + 1)
                nc.scalar.activation(to, ps[:, b:b + 2, :].rearrange("p b (k t) -> p (b k) t", t=T), ACT.Copy
                ).then_inc(m_a.sem, m_a.up())
                act.wait_ge(m_a.sem, m_a.now())
            hi_until(act, t_mwo + 3)

            def outputs(i):
                nc.scalar.activation(two(xh, i), bank2(6 + i % 2), ACT.Copy).then_inc(oh_done.sem, oh_done.up())
                act.wait_ge(oh_done.sem, oh_done.now())

            attend_act(act, MH // 2, (MN + MR) ** -0.5, outputs)
            hi_until(act, t_mwo + 6)
            for c in range(4):
                act.wait_ge(xt_done.sem, xt_done.due(act))
                if c == 3:
                    hi_until(act, t_mwo + 7)
                nc.scalar.activation(two(xh, c), two(r, c), ACT.Copy).then_inc(xh_done.sem, xh_done.up())
                act.wait_ge(xh_done.sem, xh_done.now())
            def mixed(act, c):
                act.wait_ge(used, t_out + c + 1)
                return bank2(4 + c)
            rms_act(act, mixed, t_out + 3)

        def mla_dve(dve):
            for t in range(2):
                for x in range(2):
                    c = GLR + QL2 + KVL2 + x * HR
                    ins = V.tensor_copy(kx[:, t, x, :].rearrange("p (a b) -> p a b", a=4),
                                        tk[:, t, c:c + HR].unsqueeze(1).to_broadcast([P, 4, HR]))
                    if (t, x) != (1, 1):
                        ins.then_inc(dve_step.sem, dve_step.up())
                        dve.wait_ge(dve_step.sem, dve_step.now())
            ins.then_inc(kx_done.sem, kx_done.up())
            dve.wait_ge(kx_done.sem, kx_done.now())
            dve.wait_ge(lat_ps.sem, lat_ps.due(dve))
            for m in range(5):
                ins = V.tensor_scalar(lat[:, m, :], ps[:, m // 2, m % 2 * T:(m % 2 + 1) * T], gt[:, 134 + m:135 + m],
                                      None, ALU.mult)
                if m < 4:
                    ins.then_inc(dve_step.sem, dve_step.up())
                    dve.wait_ge(dve_step.sem, dve_step.now())
            ins.then_inc(xt_done.sem, xt_done.up())
            dve.wait_ge(xt_done.sem, xt_done.now())
            dve.wait_ge(xh_done.sem, xh_done.due(dve))
            V.tensor_tensor(xl[:, 0:5, :], lat, xh[:, 0:5, :].bitcast(F32), ALU.subtract
            ).then_inc(x_ready.sem, x_ready.up())
            dve.wait_ge(x_ready.sem, x_ready.now())
            cos, sin = trig_t[:, 0, :], trig_t[:, 1, :]
            k1, k2 = ps[:, 3, 0:T], ps[:, 3, T:2 * T]
            for j, (x, y) in enumerate(((k1, cos), (k2, sin), (k2, cos), (k1, sin))):
                V.tensor_tensor(tmp2[:, j, :], x, y, ALU.mult).then_inc(dve_step.sem, dve_step.up())
                dve.wait_ge(dve_step.sem, dve_step.now())
            V.tensor_tensor(tmp2[:, 0, :], tmp2[:, 0, :], tmp2[:, 1, :], ALU.subtract
            ).then_inc(dve_step.sem, dve_step.up())
            dve.wait_ge(dve_step.sem, dve_step.now())
            V.tensor_tensor(tmp2[:, 2, :], tmp2[:, 2, :], tmp2[:, 3, :], ALU.add
            ).then_inc(dve_step.sem, dve_step.up())
            dve.wait_ge(dve_step.sem, dve_step.now())
            for x in range(2):
                V.memset(kp[x], 0.0).then_inc(dve_step.sem, dve_step.up())
                dve.wait_ge(dve_step.sem, dve_step.now())
                for h in range(4):
                    V.tensor_copy(kp[x][HR * h:HR * (h + 1), h, :], tmp2[HR * h:HR * (h + 1), 2 * x, :]
                    ).then_inc(dve_step.sem, dve_step.up())
                    dve.wait_ge(dve_step.sem, dve_step.now())
            V.tensor_copy(small[:, 80:82], small[:, 60:62]).then_inc(m_d.sem, m_d.up())
            dve.wait_ge(m_d.sem, m_d.now())
            dve.wait_ge(used, t_uq + 1)
            q1, q2 = bank2(4), bank2(5)
            rv = [rp[:, j, :].rearrange("p (k t) -> p k t", k=2) for j in range(2)]
            for x, (y, w, op) in enumerate(((q1, q2, ALU.subtract), (q2, q1, ALU.add))):
                V.tensor_tensor(rv[0], y, spread(cos), ALU.mult).then_inc(dve_step.sem, dve_step.up())
                dve.wait_ge(dve_step.sem, dve_step.now())
                V.tensor_tensor(rv[1], w, spread(sin), ALU.mult).then_inc(dve_step.sem, dve_step.up())
                dve.wait_ge(dve_step.sem, dve_step.now())
                V.tensor_tensor(rr[:, x, :, :], rv[0], rv[1], op).then_inc(dve_step.sem, dve_step.up())
                dve.wait_ge(dve_step.sem, dve_step.now())
            V.tensor_copy(small[:, 80:82], small[:, 60:62]).then_inc(m_d.sem, m_d.up())
            dve.wait_ge(m_d.sem, m_d.now())
            for j, vb in enumerate((4, 0)):
                dve.wait_ge(used, t_ukv + j + 1)
                for t in range(2):
                    ins = V.tensor_copy(vm[:, t, j * 512:(j + 1) * 512], ps[:, vb + t, :])
                    if t == 0:
                        ins.then_inc(dve_step.sem, dve_step.up())
                        dve.wait_ge(dve_step.sem, dve_step.now())
                ins.then_inc(m_d.sem, m_d.up())
                dve.wait_ge(m_d.sem, m_d.now())
            V.tensor_copy(small[:, 80:82], small[:, 60:62]).then_inc(m_d.sem, m_d.up())
            dve.wait_ge(m_d.sem, m_d.now())

            def outputs(i):
                V.tensor_tensor(two(xl, i), bank2(6 + i % 2), two(xh, i).bitcast(F32), ALU.subtract
                ).then_inc(x_ready.sem, x_ready.up())
                dve.wait_ge(x_ready.sem, x_ready.now())

            attend_dve(dve, MH // 2, (MN + MR) ** -0.5, mbias[:], outputs)
            for c in range(4):
                dve.wait_ge(used, t_mwo + c + 1)
                V.tensor_tensor(two(r, c), bank2(4 + c), two(gates, 4 + c), ALU.mult
                ).then_inc(dve_step.sem, dve_step.up())
                dve.wait_ge(dve_step.sem, dve_step.now())
                if c == 3:
                    for k in range(4):
                        V.tensor_tensor(two(r, k), two(r, k), two(ya, k), ALU.add
                        ).then_inc(xt_done.sem, xt_done.up())
                        dve.wait_ge(xt_done.sem, xt_done.now())
            for c in range(4):
                x_lo(dve, c, r)

        def finish_pe(pe):
            pe.wait_ge(stream.sem, stream.due(pe, 3))
            for t in range(2):
                for k in range(KD):
                    last = nc.tensor.transpose(ps[:, 2 * t + k // 4, k % 4 * P:(k % 4 + 1) * P],
                                               xt[:, k, t * P:(t + 1) * P], ident[:])
                last.then_inc(out_ps.sem, out_ps.up())

        def finish_act(act):
            for t in range(2):
                act.wait_ge(out_ps.sem, out_ps.due(act))
                for c in range(2):
                    ins = nc.scalar.activation(out_sb[:, t, c * 512:(c + 1) * 512], ps[:, 2 * t + c, :], ACT.Copy)
                    if c == 0:
                        ins.then_inc(act_step.sem, act_step.up())
                        act.wait_ge(act_step.sem, act_step.now())
                ins.then_inc(out_done.sem, out_done.up())
                act.wait_ge(out_done.sem, out_done.now())

        def finish_sp(sp):
            for t in range(2):
                sp.wait_ge(out_done.sem, out_done.due(sp))
                sp.dma_start(out[0, t * P:(t + 1) * P, :], out_sb[:, t, :]).then_inc(stored, 16)
            sp.wait_ge(stored, 32)

        block = ctx.enter_context(nc.Block())

        @block.sync
        def _(sp):
            sp.dma_start(x_tok, A["x"][0].rearrange("(t p) d -> p t d", p=P)).then_inc(x_in, 16)
            n = 0
            while n < len(tiles):
                run = runs.get(n)
                if run is None:
                    load(sp, n)
                    n += 1
                    continue
                count, stride, sources = run
                with sp.Fori(0, count) as i:
                    for j, source in enumerate(sources):
                        load(sp, n + j, i, source)
                n += count * len(sources)
            finish_sp(sp)

        def ffn_y(base):
            def source(act, c):
                if c < 3:
                    act.wait_ge(y_done.sem, y_done.due(act))
                else:
                    act.wait_ge(used, base + NF + NF // 2)
                return bank2(4 + c)
            return source

        @block.scalar
        def _(act):
            setup_act(act)
            setup_act2(act)
            x_act(act)
            hi_until(act, 3)
            dsa_act(act)
            ln_act(act, t_wo + 3)
            ffn_act(act, t_ffn0)
            ln_act(act, t_ffn0 + 32)
            hgrn_act(act)
            ln_act(act, t_hwo + 3)
            ffn_act(act, t_ffn1)
            ln_act(act, t_ffn1 + 32, more=False)
            rms_act(act, from_x, t_ffn1 + 32)
            x_act(act, r)
            gla_act(act)
            mla_act(act)
            rms_act(act, from_x, t_out + 3)
            x_act(act, r)
            ffn_act(act, t_ffn2)
            y_done.skip(act, 6)
            rms_act(act, ffn_y(t_ffn2), t_ffn2 + 32)
            finish_act(act)

        @block.gpsimd
        def _(pool):
            setup_pool(pool)
            for n in range(4):
                lo(pool, n)
            setup_pool2(pool)
            for n in range(4, 9):
                lo(pool, n)
            dsa_pool(pool)
            n = 9

            def until(n, m):
                passes = (m - n) // RING
                with pool.Fori(0, passes) as i:
                    for j in range(RING):
                        lo(pool, n + j, i)
                for n in range(n + passes * RING, m):
                    lo(pool, n)

            until(n, t_hwo + 4)
            hgrn_pool(pool)
            until(t_hwo + 4, len(tiles))

        @block.vector
        def _(dve):
            setup_dve(dve)
            setup_dve2(dve)
            setup_x_dve(dve)
            dsa_dve(dve)
            ln_dve(dve, 0, 32, out_arrived(t_wo))
            ffn_dve(dve, t_ffn0)
            ln_dve(dve, 8, 40, ffn_arrived(t_ffn0))
            hgrn_dve(dve)
            ln_dve(dve, 16, 48, out_arrived(t_hwo))
            ffn_dve(dve, t_ffn1)
            ln_dve(dve, 24, 56, ffn_arrived(t_ffn1), more=False)
            pre_dve(dve, 64)
            gla_dve(dve)
            mla_dve(dve)
            post_dve(dve, 72)
            pre_dve(dve, 80)
            ffn_dve(dve, t_ffn2)
            post_dve(dve, 88)

        @block.tensor
        def _(pe):
            setup_pe(pe)
            dsa_pe(pe)
            ln_pe(pe)
            ffn_pe(pe, t_ffn0)
            ln_pe(pe)
            hgrn_pe(pe)
            ln_pe(pe)
            ffn_pe(pe, t_ffn1)
            ln_pe(pe)
            rms_pe(pe)
            gla_pe(pe)
            mla_pe(pe)
            rms_pe(pe)
            rms_pe(pe)
            ffn_pe(pe, t_ffn2)
            rms_pe(pe)
            finish_pe(pe)


def kernel(**inputs):
    import concourse.bacc as bacc
    from concourse.bass_utils import run_bass_kernel_spmd

    def frequencies(theta, pairs):
        return np.float32(theta) ** (-np.arange(pairs, dtype=np.float32) / np.float32(pairs))

    arrays = dict(inputs)
    arrays["inv24"] = np.concatenate([frequencies(500000.0, ROT), frequencies(500000.0, IROT)])[None, :]
    arrays["inv_t"] = np.tile(np.float32(1) / np.float32(10000.0) ** (
        np.arange(MR // 2, dtype=np.float32) / np.float32(MR // 2)), 4)[:, None]
    nc = bacc.Bacc("TRN2", target_bir_lowering=False, num_devices=1)
    given, aps = {}, {}
    for name, x in arrays.items():
        x = np.ascontiguousarray(x)
        given[f"in_{name}"] = x
        aps[name] = nc.dram_tensor(f"in_{name}", x.shape, mybir.dt.from_np(x.dtype), kind="ExternalInput").ap()
    out = nc.dram_tensor("out", (1, T, D), F32, kind="ExternalOutput").ap()
    build(nc, aps, out)
    return run_bass_kernel_spmd(nc, [given], core_ids=[0]).results[0]["out"]
```

```python
import math

import numpy as np
import concourse.bass as bass
from concourse import mybir
from contextlib import ExitStack

F32 = mybir.dt.float32
F32R = mybir.dt.float32r
BF16 = mybir.dt.bfloat16
I32 = mybir.dt.int32
ALU = mybir.AluOpType
ACT = mybir.ActivationFunctionType
AX = mybir.AxisListType

T = 256
D = 1024
P = 128
KD = D // P
DFF = -(-8 * D // (3 * 256)) * 256
NF = DFF // P
ALPHA = float((2 * 2) ** 0.25)
LN_EPS, RMS_EPS = 1e-5, 1e-6
HEADS, HD, KVH = 16, 64, 2
IH, ID = 8, 128
TOPK = min(256, T // 4)
ROT, IROT = HD // 4 // 2, ID // 4 // 2
GH, GK, GV, GLR = 4, 128, 256, 16
MH, MN, MR, MV = 8, 128, 64, 128
QL2, KVL2 = 384, 256
CH = 64
NCH = T // CH
LEVELS = [128, 64, 32, 16, 8, 4, 2, 1]
MASKED = [0] + LEVELS[2:]
BIG = 1e30
NOT_CAUSAL, TAKEN = -3.0e38, -3.3e38
MAGIC = 1.5 * 2.0 ** 23

RING = 4
TW = 2048


class Signal:

    def __init__(self, sem):
        self.sem, self.n, self.read = sem, 0, {}

    def up(self, k=1):
        self.n += k
        return k

    def now(self):
        return self.n

    def due(self, engine, k=1):
        self.read[id(engine)] = self.read.get(id(engine), 0) + k
        return self.read[id(engine)]

    def seen(self, engine):
        return self.read.get(id(engine), 0)

    def skip(self, engine, k):
        self.read[id(engine)] = self.read.get(id(engine), 0) + k


def build(nc, A, out):
    ctx = ExitStack()
    with ctx:
        def sb(name, shape, dt=F32):
            return ctx.enter_context(nc.sbuf_tensor(name, shape, dt))

        def sem(name):
            return ctx.enter_context(nc.semaphore(name))

        stage = sb("stage", [P, RING, TW])
        wh = sb("wh", [P, RING, TW], F32R)
        wl = sb("wl", [P, RING, TW], F32R)
        xt = sb("xt", [P, KD, T])
        xh = sb("xh", [P, KD, T], F32R)
        xl = sb("xl", [P, KD, T], F32R)
        ident = sb("ident", [P, P])
        mean_d = sb("mean_d", [P, P])
        mean_hd = sb("mean_hd", [P, P])
        vec = sb("vec", [P, P])
        vec2 = sb("vec2", [14, P])
        gt = sb("gt", [P, 142])
        restart = sb("restart", [P, T])
        lmask = sb("lmask", [P, len(MASKED), CH], BF16)
        mbias = sb("mbias", [P, 3 * P])
        sbias = sb("sbias", [P, 3 * P])
        trig = sb("trig", [P, 2, 2, 24])
        trig_t = sb("trig_t", [P, 2, T])
        inv24 = sb("inv24", [P, 24])
        inv_t = sb("inv_t", [P, 1])
        kg = sb("kg", [P, 2, P])
        wa = sb("wa", [GLR, GH * GK])
        small = sb("small", [P, 128])
        eps = sb("eps", [P, 2])

        ARENA = 18000
        with nc.sbuf_tensor("arena", [P, ARENA], F32) as arena:
            pass
        hh = sb("hh", [P, NF, T], F32R)
        hl = sb("hl", [P, NF, T], F32R)

        def cut(at, *shape):
            n = math.prod(shape)
            assert at + n <= ARENA
            ap = arena[:, at:at + n]
            if len(shape) == 2:
                ap = ap.rearrange("p (a b) -> p a b", a=shape[0])
            if len(shape) == 3:
                ap = ap.rearrange("p (a b c) -> p a b c", a=shape[0], b=shape[1])
            if len(shape) == 4:
                ap = ap.rearrange("p (a b c d) -> p a b c d", a=shape[0], b=shape[1], c=shape[2])
            return ap

        NREST = GLR + QL2 + KVL2 + MR
        above = 2 * NF * T
        r = cut(above, KD, T)
        sq = cut(above + 2048, 4, T)
        rs = cut(above + 3072, T)
        silu_g = cut(above + 3328, 2, 512)
        hf = cut(above, 2, 512)
        q, iq = cut(0, 2, D), cut(2048, 2, D)
        qt, iqt = cut(4096, KD, T), cut(6144, KD, T)
        x_tok = cut(4096, 2, D)
        kr = cut(8192, 2, 256)
        kd = cut(8704, 2, KVH, 2, HD)
        kpad = cut(9216, KVH, 2, T)
        cq, cqt = cut(10240, 2, 256), cut(10752, 2, T)
        relu = cut(11264, 2, 2, 3 * P)
        score = cut(12800, 3 * P)
        top8 = cut(13184, 2, 8)
        wi = cut(13200, 2, IH)
        lg = [cut(at, 2, 3 * P) for at in (13216, 13984, 12288)]
        pts = cut(14752, 2, 2, 3 * P)
        kit, kis = cut(16288, T), cut(16544, 2, P)
        tmp = cut(16800, 4, 256)
        causal = cut(17824, P)
        pos_i, pos_t = small[:, 126:128].bitcast(I32), cut(11264, T).bitcast(I32)
        ang, turn = cut(11520, 2, T), cut(12032, 2, T)
        ang24, turn24 = cut(12544, 2, 48), cut(12640, 2, 48)
        row_i, col_i, xor_i = (cut(15616 + j * CH, CH).bitcast(I32) for j in range(3))
        row_f, col_f, apart, far, ge = (*(cut(15808 + j * CH, CH) for j in range(4)), cut(16064, 6, CH))

        hv, hq, hgate = cut(0, 2, D), cut(2048, KD, T), cut(4096, KD, T)
        hk, hb = cut(6144, KD, T), cut(8192, KD, T)
        lev = cut(10240, 2, 8, T)
        dec = cut(14336, 4, T)
        masked_a = cut(15360, 2, len(MASKED) * CH)
        at_h = cut(16256, 2, 3, P)
        o_tmp = cut(17024, 512)
        at_c = cut(17536, 2, CH)
        ends01 = small[:, 100:108]
        lb, one_lb, lb_x = small[:, 84:92], small[:, 92:100], small[:, 100:124]
        gates, sg, gv = cut(0, 16, T), cut(4096, KD, T), cut(6144, 2, D)
        gq, gk, gb = cut(8192, GH, T), cut(9216, GH, T), cut(10240, GH, T)
        kdec, tk = cut(11264, GH, T), cut(12288, 2, NREST)
        gqh = cut(13728, 3, GH, T)
        z, nz = cut(11264, GH * T), cut(13728, GH * T)
        at_g = cut(16800, 2, 3 * P)
        ha = cut(17568, T)[0:GLR, :]
        fl = cut(17824, GH, 6)
        g_sq, g_rs, g_tmp = cut(9216, 2, 512), cut(10240, 2, T), cut(10752, 512)
        qn, rr, ya = cut(0, KD, T), cut(4096, 2, 2, T), cut(6144, KD, T)
        kn, vm = cut(8192, KD, T), cut(10240, 2, D)
        kp = [cut(5120, 4, T), cut(16288, 4, T)]
        lat, kx = cut(14752, 5, T), cut(17312, 2, 2, P)
        tmp2 = cut(13728, 4, T)
        rp = cut(14752, 4, 2 * T)
        out_sb = cut(0, 2, D)

        ps = ctx.enter_context(nc.psum_tensor("ps", [P, 8, 512], F32))

        x_in, pos_in, c_in, stored = sem("x_in"), sem("pos_in"), sem("c_in"), sem("stored")
        stage_in = [sem(f"stage_in{s}") for s in range(RING)]
        hi_done, lo_done, used = sem("hi_done"), sem("lo_done"), sem("used")
        act_step, dve_step, pool_step = Signal(sem("act_step")), Signal(sem("dve_step")), Signal(sem("pool_step"))

        def signals(names):
            return [Signal(sem(n)) for n in names.split()]

        consts, vt_ps, gt_done, reduced, xt_ps, xt_done, xh_done, x_ready, nh_done, nx_ready = signals(
            "consts vt_ps gt_done reduced xt_ps xt_done xh_done x_ready nh_done nx_ready")
        numbers, trig_done = signals("numbers trig_done")
        ki_var, ki_rstd, cq_ready, cqt_ps, kd_ready, kt_ps, kt_ready = signals(
            "ki_var ki_rstd cq_ready cqt_ps kd_ready kt_ps kt_ready")
        iq_copied, iq_rot, iqt_ps, iqt_done, ix_ps, relu_done, q_copied, scored, taken, best = signals(
            "iq_copied iq_rot iqt_ps iqt_done ix_ps relu_done q_copied scored taken best")
        q_rot, qt_ps, qt_done, sel_done = signals("q_rot qt_ps qt_done sel_done")
        lg_ps, lg_free, nmx_ready, p_ready, pn_ready, pt_ps, pts_done, ot_ps, oh_done = signals(
            "lg_ps lg_free nmx_ready p_ready pn_ready pt_ps pts_done ot_ps oh_done")
        r_ready, mean_ps, d_ready, sq_ready, sq_used, rs_ready = signals(
            "r_ready mean_ps d_ready sq_ready sq_used rs_ready")
        s_done, h_mul, h_hi, h_ready, y_done = signals("s_done h_mul h_hi h_ready y_done")

        lb_in, lb_exp, hg_v, hg_a, hg_raw, hg_g, hg_ln, hg_b = signals("lb_in lb_exp hg_v hg_a hg_raw hg_g hg_ln hg_b")
        log_ready, decay_ready, level_ready, levels_ps, at_ready, cross_ready = signals(
            "log_ready decay_ready level_ready levels_ps at_ready cross_ready")
        av_ps, hg_sq, hg_mean, hg_rs, normed, silu_done, masked_ready, added = signals(
            "av_ps hg_sq hg_mean hg_rs normed silu_done masked_ready added")
        b2_d, b2_a, ha_ps, ha_done, z_ps, z_done, nz_done, sp_done, gb_done, kdec_e, gqh_done, gates_done = signals(
            "b2_d b2_a ha_ps ha_done z_ps z_done nz_done sp_done gb_done kdec_e gqh_done gates_done")
        ga_ps, ga_at, go_ps, go_sq, go_mean, go_rs, ya_done = signals("ga_ps ga_at go_ps go_sq go_mean go_rs ya_done")
        lat_scaled, kx_done, lat_ps, m_a, m_d = signals("lat_scaled kx_done lat_ps m_a m_d")
        out_ps, out_done, out_done2, stream, scaled = signals("out_ps out_done out_done2 stream scaled")

        tiles = []
        runs = {}

        def rows(w, a, b):
            return w[a * P:b * P, :].rearrange("(k p) n -> p k n", p=P)

        def columns(w, a, n):
            tiles.append([(None, w.rearrange("(k p) n -> p k n", p=P)[:, :, a:a + n])])

        def tile_range(count):
            return range(len(tiles), len(tiles) + count)

        FFNS = [(A["ffn_w_gate"][0], A["ffn_w_up"][0], A["ffn_w_down"][0]),
                (A["ffn_w_gate"][1], A["ffn_w_up"][1], A["ffn_w_down"][1]),
                (A["w_ffn_gate_2"][0], A["w_ffn_up_2"][0], A["w_ffn_down_2"][0])]

        def plan_ffn(f):
            gate, up, down = FFNS[f]
            base = len(tiles)
            gates, ups = (w.rearrange("(k p) n -> p k n", p=P) for w in (gate, up))
            pair = [lambda i, w=w, p=p: w[:, :, bass.ds(i * 512 + 256 * p, 256)] for p in range(2) for w in (gates, ups)]
            downs = down.rearrange("(j k p) n -> p j k n", p=P, k=2)
            runs[base] = (NF // 4, pair)
            runs[base + NF] = (2, [lambda i, j=j: downs[:, bass.ds(i * 4 + j, 1), :, :].rearrange(
                "p a k n -> p (a k) n") for j in range(4)])
            for p in range(NF // 2):
                columns(gate, 256 * p, 256)
                columns(up, 256 * p, 256)
            for j in range(NF // 2):
                tiles.append([(None, rows(down, 2 * j, 2 * j + 2))])
            return base

        w_att = A["att_w_in"][0]
        for a in (0, 256, 648 - 256):
            columns(w_att, a, 256)
        tiles.append([(None, rows(A["att_w_iq"][0], 0, 2))])
        tiles.append([(None, rows(A["att_w_uq"][0], 0, 2))])
        t_wo = len(tiles)
        for m in range(4):
            columns(A["att_w_o"][0], 256 * m, 256)
        t_ffn0 = plan_ffn(0)
        def column_blocks(w, a, count):
            at = len(tiles)
            for j in range(count):
                columns(w, a + 256 * j, 256)
            return at

        w_h = A["hgrn_w_in"][0]
        t_hi, t_hq, t_hf, t_hg = (column_blocks(w_h, a, 4) for a in (2 * D, 0, D, 3 * D))
        t_hwo = column_blocks(A["hgrn_w_o"][0], 0, 4)
        t_ffn1 = plan_ffn(1)
        w_2 = A["w_in_2"][0]
        GQ = GH * GK
        REST = 2 * GQ + 2 * GH * GV
        t_rest = len(tiles)
        for a in (REST, REST + 256, REST + NREST - 256):
            columns(w_2, a, 256)
        t_gv = column_blocks(w_2, 2 * GQ, 4)
        t_gq = column_blocks(w_2, 0, 2)
        t_gk = column_blocks(w_2, GQ, 2)
        t_gg = column_blocks(w_2, 2 * GQ + GH * GV, 4)
        t_gate = column_blocks(A["w_gate_2"][0], 0, 8)
        t_gwo = column_blocks(A["w_o_gla_2"][0], 0, 4)
        t_uq = len(tiles)
        uq = A["w_uq_2"][0].rearrange("(k p) (h c) -> p k h c", p=P, c=MN + MR)
        KQ = QL2 // P
        HR = MR // 2
        tiles.append([((k * 512 + x * 256, 8 * HR, 8), uq[:, k, :, MN + x * HR:MN + (x + 1) * HR])
                      for k in range(KQ) for x in range(2)])
        for j in range(2):
            tiles.append([((k * 512, 512, 4), uq[:, k, 4 * j:4 * j + 4, 0:MN]) for k in range(KQ)])
        t_ukv = len(tiles)
        for j in range(2):
            tiles.append([(None, rows(A["w_ukv_2"][0], 0, 2)[:, :, j * 1024:(j + 1) * 1024])])
        t_mwo = column_blocks(A["w_o_mla_2"][0], 0, 4)
        t_out = column_blocks(A["w_out_2"][0], 0, 4)
        t_ffn2 = plan_ffn(2)

        come, total = [], [0] * RING
        for n, parts in enumerate(tiles):
            total[n % RING] += 16 * len(parts)
            come.append(total[n % RING])

        def load(sp, n, i=None, source=None):
            if n >= RING:
                sp.wait_ge(lo_done, (n - RING + 1) if i is None else i * RING + (n - RING + 1))
            for place, src in ([(None, source(i))] if source else tiles[n]):
                if place is None:
                    to = stage[:, ring(n), :].rearrange("p (k n) -> p k n", k=src.shape[1])
                else:
                    at, words, k = place
                    to = stage[:, ring(n), at:at + words].rearrange("p (k n) -> p k n", k=k)
                sp.dma_start(to, src).then_inc(stage_in[ring(n)], 16)

        def ring(n):
            return n % RING

        def hi(act, n, i=None, base=None):
            off = 0 if i is None else i
            act.wait_ge(stage_in[ring(n)], off * 16 + come[n])
            if n >= RING:
                act.wait_ge(used, off * RING + (n - RING + 1))
            nc.scalar.activation(wh[:, ring(n), :], stage[:, ring(n), :], ACT.Copy).then_inc(hi_done, 1)

        def lo(pool, n, i=None):
            off = 0 if i is None else i
            pool.wait_ge(hi_done, off * RING + (n + 1))
            nc.gpsimd.tensor_tensor(wl[:, ring(n), :], stage[:, ring(n), :], wh[:, ring(n), :].bitcast(F32),
                                    ALU.subtract).then_inc(lo_done, 1)

        his = [0]

        def hi_until(act, n):
            while his[0] <= min(n, len(tiles) - 1):
                hi(act, his[0])
                his[0] += 1

        V = nc.vector
        mm = nc.tensor.matmul

        def mm3(out_, lhs, rhs, start, stop, skip=False):
            (lh, ll), (rh, rl) = lhs, rhs
            mm(out_, lh, rh, start=start, stop=False, skip_group_check=skip)
            mm(out_, lh, rl, start=False, stop=False, skip_group_check=skip)
            return mm(out_, ll, rh, start=False, stop=stop, skip_group_check=skip)

        def tile_a(pe, n, b, kt=KD, width=256, i=None, m_cols=(0, 128), x0=0, done=True, fresh=None):
            pe.wait_ge(lo_done, (n + 1) if i is None else i * RING + (n + 1))
            s = ring(n)
            for m, c in enumerate(m_cols):
                for k in range(kt):
                    o = k * width + c
                    if fresh and m == 0 and k % 2 == 0:
                        pe.wait_ge(fresh.sem, fresh.due(pe))
                    last = mm3(ps[:, b + m // 2, m % 2 * T:(m % 2 + 1) * T],
                               (wh[:, s, o:o + P], wl[:, s, o:o + P]), (xh[:, x0 + k, :], xl[:, x0 + k, :]),
                               k == 0, k == kt - 1)
            if done:
                last.then_inc(used, 1)
            return last

        def tile_b(pe, n, outs, kt=KD, width=256, cols=256, fresh=None):
            pe.wait_ge(lo_done, n + 1)
            s = ring(n)
            for t, c, out_ in outs:
                for k in range(kt):
                    o = k * width + c
                    if fresh and (t, c) == outs[0][0:2] and k % 2 == 0:
                        pe.wait_ge(fresh.sem, fresh.due(pe))
                    x = slice(t * P, (t + 1) * P)
                    last = mm3(out_, (xh[:, k, x], xl[:, k, x]),
                               (wh[:, s, o:o + cols], wl[:, s, o:o + cols]), k == 0, k == kt - 1)
            last.then_inc(used, 1)

        def setup_pool(pool):
            nc.gpsimd.memset(ident[:], 0.0).then_inc(pool_step.sem, pool_step.up())
            pool.wait_ge(pool_step.sem, pool_step.now())
            nc.gpsimd.affine_select(out=ident[:], in_=ident[:], compare_op=ALU.not_equal, fill=1.0, base=0,
                                    pattern=[[-1, P]], channel_multiplier=1).then_inc(consts.sem, consts.up())
            nc.gpsimd.memset(mean_d[:], 1.0 / D)
            nc.gpsimd.memset(mean_hd[:], 1.0 / P)
            nc.gpsimd.memset(restart[:], 1.0).then_inc(pool_step.sem, pool_step.up())
            pool.wait_ge(pool_step.sem, pool_step.now())
            nc.gpsimd.memset(restart[:, 0:T:CH], 0.0)
            nc.gpsimd.memset(mbias[:], 0.0).then_inc(pool_step.sem, pool_step.up())
            pool.wait_ge(pool_step.sem, pool_step.now())
            nc.gpsimd.memset(mbias[0:CH, CH:P], -BIG)
            nc.gpsimd.memset(mbias[0:CH, 2 * P + CH:3 * P], -BIG)
            nc.gpsimd.memset(eps[:, 0:1], LN_EPS)
            nc.gpsimd.memset(kpad, 0.0)
            nc.gpsimd.memset(causal, 3.4e38).then_inc(pool_step.sem, pool_step.up())
            pool.wait_ge(pool_step.sem, pool_step.now())
            nc.gpsimd.affine_select(out=causal, in_=causal, compare_op=ALU.is_ge, fill=NOT_CAUSAL, base=0,
                                    pattern=[[-1, P]], channel_multiplier=1)
            nc.gpsimd.memset(eps[:, 1:2], RMS_EPS).then_inc(consts.sem, consts.up())

        def setup_pool2(pool):
            nc.gpsimd.iota(row_i, [[0, CH]], base=0, channel_multiplier=1)
            nc.gpsimd.iota(col_i, [[1, CH]], base=0, channel_multiplier=0).then_inc(numbers.sem, numbers.up())

        def setup_sp(sp):
            def load(to, src):
                sp.dma_start(to, src, allow_slow_non_contiguous=True).then_inc(c_in, 16)

            def blocks(x):
                return x.rearrange("a (k p) -> (a k) p", p=P)

            load(vec[0:32, :], A["ln_g"].rearrange("l j (k p) -> (l j k) p", p=P))
            load(vec[32:64, :], A["ln_b"].rearrange("l j (k p) -> (l j k) p", p=P))
            for at, name in ((64, "pre_mix_norm_2"), (72, "post_mix_norm_2"), (80, "pre_ffn_norm_2"),
                             (88, "post_ffn_norm_2"), (96, "b_gate_2"), (112, "hgrn_lb_logits")):
                n = math.prod(A[name].shape) // P
                load(vec[at:at + n, :], blocks(A[name]))
            for at, name in ((0, "b_a2_2"), (4, "gla_norm_2"), (6, "q_norm_2"), (9, "kv_norm_2"),
                             (11, "hgrn_g_norm"), (12, "att_g_cq")):
                n = math.prod(A[name].shape) // P
                load(vec2[at:at + n, :], blocks(A[name]))
            load(kg[:, 0, :], A["att_g_ik"][0, :].partition_broadcast(P))
            load(kg[:, 1, :], A["att_b_ik"][0, :].partition_broadcast(P))
            load(wa[:], A["w_a2_2"][0])
        N_CONST = 17

        def setup_act2(act):
            act.wait_ge(reduced.sem, reduced.due(act))
            nc.scalar.activation(trig[:, :, :, :].rearrange("p c t f -> p (c t f)"),
                                 ang24.rearrange("p c f -> p (c f)"), ACT.Sin).then_inc(act_step.sem, act_step.up())
            nc.scalar.activation(trig_t[:, :, :].rearrange("p c t -> p (c t)"),
                                 ang.rearrange("p c t -> p (c t)"), ACT.Sin).then_inc(trig_done.sem, trig_done.up())

        def reduce_angle(dve, x, n, quarter):
            parts, left = [], 2 * math.pi
            for bits in (8, 8, 8):
                unit = 2.0 ** (math.floor(math.log2(left)) - bits + 1)
                parts.append(math.floor(left / unit) * unit)
                left -= parts[-1]
            parts.append(left)
            V.tensor_scalar(n, x, 1 / (2 * math.pi), 0.25 if quarter else 0.0, ALU.mult, ALU.add
            ).then_inc(dve_step.sem, dve_step.up())
            dve.wait_ge(dve_step.sem, dve_step.now())
            V.tensor_scalar(n, n, MAGIC, MAGIC, ALU.add, ALU.subtract).then_inc(dve_step.sem, dve_step.up())
            dve.wait_ge(dve_step.sem, dve_step.now())
            for part in parts:
                V.scalar_tensor_tensor(out=x, in0=n, scalar=-part, in1=x, op0=ALU.mult, op1=ALU.add
                ).then_inc(dve_step.sem, dve_step.up())
                dve.wait_ge(dve_step.sem, dve_step.now())
            if quarter:
                V.tensor_scalar(x, x, math.pi / 2, None, ALU.add).then_inc(dve_step.sem, dve_step.up())
                dve.wait_ge(dve_step.sem, dve_step.now())
            V.tensor_scalar(x, x, 3.1415925, -3.1415925, ALU.min, ALU.max).then_inc(dve_step.sem, dve_step.up())

        def setup_dve(dve):
            dve.wait_ge(pos_in, 16 * 4)
            f24 = tmp[:, 0, 0:2]
            V.tensor_copy(f24, pos_i).then_inc(dve_step.sem, dve_step.up())
            dve.wait_ge(dve_step.sem, dve_step.now())
            for t in range(2):
                V.tensor_scalar(ang24[:, 0, t * 24:(t + 1) * 24], inv24[:], f24[:, t:t + 1], None, ALU.mult
                ).then_inc(dve_step.sem, dve_step.up())
                dve.wait_ge(dve_step.sem, dve_step.now())
            V.tensor_copy(ang24[:, 1, :], ang24[:, 0, :]).then_inc(dve_step.sem, dve_step.up())
            V.tensor_copy(ang[:, 1, :], pos_t).then_inc(dve_step.sem, dve_step.up())
            dve.wait_ge(dve_step.sem, dve_step.now())
            V.tensor_scalar(ang[:, 0, :], ang[:, 1, :], inv_t[:, 0:1], None, ALU.mult
            ).then_inc(dve_step.sem, dve_step.up())
            dve.wait_ge(dve_step.sem, dve_step.now())
            V.tensor_copy(ang[:, 1, :], ang[:, 0, :]).then_inc(dve_step.sem, dve_step.up())
            for c in range(2):
                reduce_angle(dve, ang24[:, c, :], turn24[:, c, :], c == 0)
                reduce_angle(dve, ang[:, c, :], turn[:, c, :], c == 0)
            V.tensor_copy(f24, f24).then_inc(reduced.sem, reduced.up())

        def gains_dve(dve):
            dve.wait_ge(consts.sem, consts.due(dve, 2))
            dve.wait_ge(vt_ps.sem, vt_ps.due(dve))
            V.tensor_copy(gt[:, 0:142], ps[:, 3, 0:142]).then_inc(gt_done.sem, gt_done.up())
            dve.wait_ge(gt_done.sem, gt_done.now())
            l0, l1, top = gt[:, 112:120], gt[:, 120:128], lb_x[:, 16:24]
            V.tensor_tensor(top, l0, l1, ALU.max).then_inc(dve_step.sem, dve_step.up())
            dve.wait_ge(dve_step.sem, dve_step.now())
            V.tensor_tensor(lb_x[:, 0:8], l0, top, ALU.subtract).then_inc(dve_step.sem, dve_step.up())
            V.tensor_tensor(lb_x[:, 8:16], l1, top, ALU.subtract).then_inc(lb_in.sem, lb_in.up())

        def setup_dve2(dve):
            dve.wait_ge(numbers.sem, numbers.due(dve))
            V.tensor_tensor(xor_i, row_i, col_i, ALU.bitwise_xor).then_inc(dve_step.sem, dve_step.up())
            V.tensor_copy(row_f, row_i)
            V.tensor_copy(col_f, col_i).then_inc(dve_step.sem, dve_step.up())
            dve.wait_ge(dve_step.sem, dve_step.now())
            V.tensor_copy(apart, xor_i).then_inc(dve_step.sem, dve_step.up())
            dve.wait_ge(dve_step.sem, dve_step.now())
            for x in (apart, row_f):
                V.tensor_scalar(far, x, float(CH), float(-CH), ALU.is_ge, ALU.mult).then_inc(dve_step.sem, dve_step.up())
                dve.wait_ge(dve_step.sem, dve_step.now())
                V.tensor_tensor(x, x, far, ALU.add).then_inc(dve_step.sem, dve_step.up())
                dve.wait_ge(dve_step.sem, dve_step.now())
            V.tensor_scalar(lmask[:, 0, :], apart, 0.0, None, ALU.is_equal)
            V.tensor_tensor(far, col_f, row_f, ALU.is_gt).then_inc(dve_step.sem, dve_step.up())
            dve.wait_ge(dve_step.sem, dve_step.now())
            V.tensor_tensor(apart, apart, far, ALU.mult).then_inc(dve_step.sem, dve_step.up())
            dve.wait_ge(dve_step.sem, dve_step.now())
            for l, d in enumerate(MASKED[1:]):
                V.tensor_scalar(ge[:, l, :], apart, float(d), None, ALU.is_ge).then_inc(dve_step.sem, dve_step.up())
            dve.wait_ge(dve_step.sem, dve_step.now())
            V.tensor_copy(lmask[:, 1, :], ge[:, 0, :])
            V.tensor_tensor(lmask[:, 2:, :], ge[:, 1:, :], ge[:, :5, :], ALU.subtract
            ).then_inc(dve_step.sem, dve_step.up())
            dve.wait_ge(lb_exp.sem, lb_exp.due(dve))
            top = lb_x[:, 16:24]
            V.tensor_scalar(gt[:, 96:112], gt[:, 96:112], -1.0, None, ALU.mult)
            V.tensor_tensor(top, lb_x[:, 0:8], lb_x[:, 8:16], ALU.add).then_inc(dve_step.sem, dve_step.up())
            dve.wait_ge(dve_step.sem, dve_step.now())
            V.reciprocal(top, top).then_inc(dve_step.sem, dve_step.up())
            dve.wait_ge(dve_step.sem, dve_step.now())
            V.tensor_tensor(lb_x[:, 0:8], lb_x[:, 0:8], top, ALU.mult).then_inc(dve_step.sem, dve_step.up())
            dve.wait_ge(dve_step.sem, dve_step.now())
            V.tensor_tensor(lb_x[:, 8:16], lb_x[:, 8:16], top, ALU.mult).then_inc(dve_step.sem, dve_step.up())
            dve.wait_ge(dve_step.sem, dve_step.now())
            V.tensor_tensor(lb, lb_x[:, 0:8], lb_x[:, 8:16], ALU.add).then_inc(dve_step.sem, dve_step.up())
            dve.wait_ge(dve_step.sem, dve_step.now())
            V.tensor_tensor(lb, lb, lb_x[:, 0:8], ALU.subtract).then_inc(dve_step.sem, dve_step.up())
            dve.wait_ge(dve_step.sem, dve_step.now())
            V.tensor_scalar(one_lb, lb, -1.0, 1.0, ALU.mult, ALU.add).then_inc(dve_step.sem, dve_step.up())

        def setup_pe(pe):
            pe.wait_ge(consts.sem, consts.due(pe))
            pe.wait_ge(x_in, 16)
            for c in range(4):
                for k in range(2):
                    for t in range(2):
                        last = nc.tensor.transpose(ps[:, 4 + c, k * T + t * P:k * T + (t + 1) * P],
                                                   x_tok[:, t, (2 * c + k) * P:(2 * c + k + 1) * P], ident[:])
                last.then_inc(xt_ps.sem, xt_ps.up())
            pe.wait_ge(c_in, 16 * N_CONST)
            nc.tensor.transpose(ps[:, 3, 0:P], vec[:], ident[:])
            nc.tensor.transpose(ps[:, 3, P:P + 14], vec2[:], ident[0:14, 0:14]).then_inc(vt_ps.sem, vt_ps.up())

        def two(x, c):
            return x[:, 2 * c:2 * c + 2, :]

        def x_act(act, src=xt, done=xh_done):
            for c in range(4):
                act.wait_ge(xt_done.sem, xt_done.due(act))
                nc.scalar.activation(two(xh, c), two(src, c), ACT.Copy).then_inc(done.sem, done.up())

        def norm_pool(pool, src=xt):
            for c in range(4):
                pool.wait_ge(nh_done.sem, nh_done.due(pool))
                nc.gpsimd.tensor_tensor(two(xl, c), two(src, c), two(xh, c).bitcast(F32), ALU.subtract
                ).then_inc(nx_ready.sem, nx_ready.up())

        def bank2(b):
            return ps[:, b, :].rearrange("p (k t) -> p k t", k=2)

        def setup_x_dve(dve):
            for c in range(4):
                dve.wait_ge(xt_ps.sem, xt_ps.due(dve))
                V.tensor_copy(two(xt, c), bank2(4 + c)).then_inc(xt_done.sem, xt_done.up())
            x_lo_dve(dve)

        def x_lo(dve, c, src=None):
            dve.wait_ge(xh_done.sem, xh_done.due(dve))
            V.tensor_tensor(two(xl, c), two(src if src is not None else xt, c), two(xh, c).bitcast(F32), ALU.subtract
            ).then_inc(x_ready.sem, x_ready.up())

        def x_lo_dve(dve):
            for c in range(4):
                x_lo(dve, c)

        def rope(engine, step, done, scratch, x, cs, heads, half):
            cos, sin = (cs[c].unsqueeze(1).to_broadcast([P, heads, half]) for c in range(2))
            lo_, up = x[:, :, 0:half], x[:, :, half:2 * half]
            m = [scratch[:, j, 0:heads * half].rearrange("p (h f) -> p h f", h=heads) for j in range(4)]
            engine.tensor_tensor(m[0], lo_, cos, ALU.mult)
            engine.tensor_tensor(m[1], up, sin, ALU.mult)
            engine.tensor_tensor(m[2], up, cos, ALU.mult)
            engine.tensor_tensor(m[3], lo_, sin, ALU.mult).then_inc(step.sem, step.up())
            engine.wait_ge(step.sem, step.now())
            engine.tensor_tensor(lo_, m[0], m[1], ALU.subtract)
            engine.tensor_tensor(up, m[2], m[3], ALU.add).then_inc(done.sem, done.up())
            engine.wait_ge(done.sem, done.now())

        def cs_q(t):
            return trig[:, 0, t, 0:ROT], trig[:, 1, t, 0:ROT]

        def cs_i(t):
            return trig[:, 0, t, ROT:24], trig[:, 1, t, ROT:24]

        def dsa_pe(pe):
            for n in range(3):
                if n == 2:
                    pe.wait_ge(cq_ready.sem, cq_ready.due(pe, 2))
                    for k in range(2):
                        for t in range(2):
                            last = nc.tensor.transpose(ps[:, 4, k * T + t * P:k * T + (t + 1) * P],
                                                       cq[:, t, k * P:(k + 1) * P], ident[:])
                    last.then_inc(cqt_ps.sem, cqt_ps.up())
                tile_b(pe, n, [(t, 0, ps[:, n, t * T:(t + 1) * T]) for t in range(2)], fresh=None if n else x_ready)
            pe.wait_ge(gt_done.sem, gt_done.due(pe))
            pe.wait_ge(consts.sem, consts.due(pe))

            def queries(n, b):
                tile_b(pe, n, [(t, c * 512, ps[:, b + 2 * t + c, :]) for t in range(2) for c in range(2)],
                       kt=2, width=D, cols=512)

            pe.wait_ge(x_ready.sem, x_ready.due(pe))
            queries(3, 0)
            pe.wait_ge(kd_ready.sem, kd_ready.due(pe, 6))
            for gr in range(KVH):
                for t in range(2):
                    nc.tensor.transpose(ps[:, 5, gr * T + t * P:gr * T + (t + 1) * P],
                                        kd[:, t, gr, :, :].rearrange("p a b -> p (a b)"), ident[:])
            for t in range(2):
                last = nc.tensor.transpose(ps[:, 6, t * P:(t + 1) * P], kis[:, t, :], ident[:])
            last.then_inc(kt_ps.sem, kt_ps.up())
            pe.wait_ge(kt_ready.sem, kt_ready.due(pe))
            queries(4, 4)
            pe.wait_ge(iq_rot.sem, iq_rot.due(pe, 2))
            for h in range(IH):
                for t in range(2):
                    last = nc.tensor.transpose(ps[:, h // 2, h % 2 * T + t * P:h % 2 * T + (t + 1) * P],
                                               iq[:, t, h * P:(h + 1) * P], ident[:])
                if h % 2:
                    last.then_inc(iqt_ps.sem, iqt_ps.up())
            pe.wait_ge(iqt_done.sem, iqt_done.due(pe, 4))
            for h in range(IH):
                b = h % 4
                if h % 2 == 0 and h >= 4:
                    pe.wait_ge(relu_done.sem, relu_done.due(pe))
                mm(ps[:, b, 0:P], iqt[:, h, 0:P], kit[:, 0:P], start=True, stop=True)
                last = mm(ps[:, b, P:3 * P], iqt[:, h, P:T], kit, start=True, stop=True)
                if h % 2:
                    last.then_inc(ix_ps.sem, ix_ps.up())
            pe.wait_ge(q_rot.sem, q_rot.due(pe, 2))
            for h in range(KD):
                for t in range(2):
                    last = nc.tensor.transpose(ps[:, 4 + h // 2, h % 2 * T + t * P:h % 2 * T + (t + 1) * P],
                                               q[:, t, h * P:(h + 1) * P], ident[:])
                if h % 2:
                    last.then_inc(qt_ps.sem, qt_ps.up())
            pe.wait_ge(relu_done.sem, relu_done.due(pe, 2))
            pe.wait_ge(qt_done.sem, qt_done.due(pe, 4))

            def logits(i):
                for e in range(2):
                    h = 2 * i + e
                    gr = h // (HEADS // KVH)
                    b = 2 * (i % 2) + e
                    mm(ps[:, b, 0:P], qt[:, i, 0:P], kpad[:, gr, e, 0:P], start=True, stop=True)
                    last = mm(ps[:, b, P:3 * P], qt[:, i, P:T], kpad[:, gr, e, :], start=True, stop=True)
                return last

            def weighted(i, e, pt, last_of_pair):
                gr = (2 * i + e) // (HEADS // KVH)
                o = ps[e * HD:(e + 1) * HD, 6 + i % 2, :]
                val = [kr[:, t, P + gr * HD:P + (gr + 1) * HD] for t in range(2)]
                mm(o[:, 0:P], val[0], pt[:, 0:P], start=True, stop=True)
                mm(o[:, P:T], val[0], pt[:, P:2 * P], start=True, stop=False)
                return mm(o[:, P:T], val[1], pt[:, 2 * P:3 * P], start=False, stop=True)

            attend_pe(pe, HEADS // 2, logits, weighted)
            out_pe(pe, t_wo)

        def out_pe(pe, base, moving=2):
            if moving < 4:
                pe.wait_ge(x_ready.sem, x_ready.due(pe, moving))
            for j in range(4):
                tile_a(pe, base + j, 4 + j, fresh=x_ready if moving == 4 and j == 0 else None)

        def attend_pe(pe, pairs, logits, weighted):
            def value(i):
                pe.wait_ge(pts_done.sem, pts_done.due(pe))
                if i >= 2:
                    pe.wait_ge(x_ready.sem, x_ready.due(pe))
                for e in range(2):
                    last = weighted(i, e, pts[:, i % 2, e, :], e)
                last.then_inc(ot_ps.sem, ot_ps.up())

            for i in range(2):
                logits(i).then_inc(lg_ps.sem, lg_ps.up())
            for i in range(pairs):
                if i + 2 < pairs:
                    pe.wait_ge(lg_free.sem, lg_free.due(pe))
                    logits(i + 2).then_inc(lg_ps.sem, lg_ps.up())
                pe.wait_ge(pn_ready.sem, pn_ready.due(pe))
                if i >= 1:
                    pe.wait_ge(pts_done.sem, pts_done.seen(pe) + 1)
                for e in range(2):
                    for c in range(3):
                        last = nc.tensor.transpose(ps[:, 4 + e, c * P:(c + 1) * P],
                                                   lg[i % 3][:, e, c * P:(c + 1) * P], ident[:])
                last.then_inc(pt_ps.sem, pt_ps.up())
                if i >= 1:
                    value(i - 1)
            value(pairs - 1)
            lg_free.skip(pe, 2)

        def attend_act(act, pairs, scale, outputs):
            def exps(i):
                act.wait_ge(nmx_ready.sem, nmx_ready.due(act))
                for e in range(2):
                    for t, (c0, c1) in enumerate(((0, P), (P, 3 * P))):
                        at = 8 + 8 * (i % 2) + 2 * e + t
                        x = lg[i % 3][:, e, c0:c1]
                        ins = nc.scalar.activation(x, x, ACT.Exp, bias=small[:, at + 4:at + 5], scale=scale,
                                                   accum_out=small[:, 16 + at:17 + at])
                ins.then_inc(p_ready.sem, p_ready.up())

            exps(0)
            exps(1)
            for i in range(pairs):
                act.wait_ge(pt_ps.sem, pt_ps.due(act))
                nc.scalar.activation(pts[:, i % 2, :, :], ps[:, 4:6, 0:3 * P], ACT.Copy
                ).then_inc(pts_done.sem, pts_done.up())
                if i >= 1:
                    act.wait_ge(ot_ps.sem, ot_ps.due(act))
                    outputs(i - 1)
                if i + 2 < pairs:
                    exps(i + 2)
            act.wait_ge(ot_ps.sem, ot_ps.due(act))
            outputs(pairs - 1)

        def attend_dve(dve, pairs, scale, bias, outputs):
            def masked(i):
                dve.wait_ge(lg_ps.sem, lg_ps.due(dve))
                x = lg[i % 3]
                if i >= 3:
                    dve.wait_ge(pt_ps.sem, pt_ps.seen(dve) + i - 2)
                V.tensor_tensor(x, ps[:, 2 * (i % 2):2 * (i % 2) + 2, 0:3 * P],
                                bias.unsqueeze(1).to_broadcast([P, 2, 3 * P]), ALU.add
                ).then_inc(lg_free.sem, lg_free.up())
                dve.wait_ge(lg_free.sem, lg_free.now())
                at = 8 + 8 * (i % 2)
                mx = small[:, at:at + 4].rearrange("p (e t) -> p e t", e=2)
                V.tensor_reduce(mx[:, :, 0], x[:, :, 0:P], AX.X, ALU.max)
                V.tensor_reduce(mx[:, :, 1], x[:, :, P:3 * P], AX.X, ALU.max
                ).then_inc(dve_step.sem, dve_step.up())
                dve.wait_ge(dve_step.sem, dve_step.now())
                V.tensor_scalar(small[:, at + 4:at + 8], small[:, at:at + 4], -scale, None, ALU.mult
                ).then_inc(nmx_ready.sem, nmx_ready.up())

            def normalised(i):
                dve.wait_ge(p_ready.sem, p_ready.due(dve))
                at = 24 + 8 * (i % 2)
                V.reciprocal(small[:, at + 4:at + 8], small[:, at:at + 4]).then_inc(dve_step.sem, dve_step.up())
                dve.wait_ge(dve_step.sem, dve_step.now())
                for e in range(2):
                    for t, (c0, c1) in enumerate(((0, P), (P, 3 * P))):
                        x = lg[i % 3][:, e, c0:c1]
                        w = at + 4 + 2 * e + t
                        ins = V.tensor_scalar(x, x, small[:, w:w + 1], None, ALU.mult)
                ins.then_inc(pn_ready.sem, pn_ready.up())

            masked(0)
            masked(1)
            normalised(0)
            for i in range(pairs):
                if i + 2 < pairs:
                    masked(i + 2)
                if i + 1 < pairs:
                    normalised(i + 1)
                if i >= 1:
                    dve.wait_ge(oh_done.sem, oh_done.due(dve))
                    outputs(i - 1)
            pt_ps.skip(dve, pairs)
            dve.wait_ge(oh_done.sem, oh_done.due(dve))
            outputs(pairs - 1)

        def dsa_act(act):
            act.wait_ge(consts.sem, consts.due(act, 2))
            act.wait_ge(used, 1)
            for t in range(2):
                nc.scalar.activation(iq[:, t, 0:T], ps[:, 0, t * T:(t + 1) * T], ACT.Square,
                                     accum_out=small[:, t:t + 1]).then_inc(act_step.sem, act_step.up())
                act.wait_ge(act_step.sem, act_step.now())
            nc.scalar.preload_act_table_set("natural_log_exp_and_others")
            nc.scalar.activation(small[:, 2:4], small[:, 0:2], ACT.Ln, scale=1.0 / 256, bias=eps[:, 1:2]
            ).then_inc(act_step.sem, act_step.up())
            act.wait_ge(act_step.sem, act_step.now())
            nc.scalar.activation(small[:, 4:6], small[:, 2:4], ACT.Exp, scale=-0.5
            ).then_inc(act_step.sem, act_step.up())
            act.wait_ge(act_step.sem, act_step.now())
            for t in range(2):
                nc.scalar.activation(cq[:, t, :], ps[:, 0, t * T:(t + 1) * T], ACT.Copy,
                                     scale=small[:, 4 + t:5 + t]).then_inc(cq_ready.sem, cq_ready.up())
            act.wait_ge(used, 3)
            act.wait_ge(xt_done.sem, xt_done.due(act))
            nc.scalar.activation(xh[:, 0:2, :], cqt, ACT.Copy).then_inc(xh_done.sem, xh_done.up())
            act.wait_ge(ki_var.sem, ki_var.due(act))
            nc.scalar.activation(small[:, 66:70:2], small[:, 61:65:2], ACT.Ln, bias=eps[:, 0:1]
            ).then_inc(act_step.sem, act_step.up())
            act.wait_ge(act_step.sem, act_step.now())
            nc.scalar.activation(small[:, 70:74:2], small[:, 66:70:2], ACT.Exp, scale=-0.5
            ).then_inc(ki_rstd.sem, ki_rstd.up())
            hi_until(act, 4)
            act.wait_ge(used, 4)
            for b in range(4):
                ins = nc.scalar.activation(iq[:, b // 2, b % 2 * 512:b % 2 * 512 + 512], ps[:, b, :], ACT.Copy)
                if b % 2:
                    ins.then_inc(iq_copied.sem, iq_copied.up())
            hi_until(act, 5)
            act.wait_ge(lb_in.sem, lb_in.due(act))
            nc.scalar.activation(lb_x[:, 0:16], lb_x[:, 0:16], ACT.Exp).then_inc(lb_exp.sem, lb_exp.up())
            for c in range(4):
                act.wait_ge(iqt_ps.sem, iqt_ps.due(act))
                nc.scalar.activation(two(iqt, c), bank2(c), ACT.Copy).then_inc(iqt_done.sem, iqt_done.up())
            hi_until(act, 8)
            for p in range(IH // 2):
                act.wait_ge(ix_ps.sem, ix_ps.due(act))
                if p >= 2:
                    act.wait_ge(scored.sem, 4 * (p - 1))
                nc.scalar.activation(relu[:, p % 2, :, :], ps[:, 2 * (p % 2):2 * (p % 2) + 2, 0:3 * P], ACT.Relu
                ).then_inc(relu_done.sem, relu_done.up())
                if p == 1:
                    act.wait_ge(used, 5)
                    for b in range(4):
                        ins = nc.scalar.activation(q[:, b // 2, b % 2 * 512:b % 2 * 512 + 512], ps[:, 4 + b, :], ACT.Copy)
                        if b % 2:
                            ins.then_inc(q_copied.sem, q_copied.up())
            for c in range(4):
                act.wait_ge(qt_ps.sem, qt_ps.due(act))
                nc.scalar.activation(two(qt, c), bank2(4 + c), ACT.Copy).then_inc(qt_done.sem, qt_done.up())

            def outputs(i):
                nc.scalar.activation(xh[:, i, :], ps[:, 6 + i % 2, 0:T], ACT.Copy
                ).then_inc(oh_done.sem, oh_done.up())

            attend_act(act, HEADS // 2, HD ** -0.5, outputs)

        def dsa_dve(dve):
            dve.wait_ge(used, 2)
            V.tensor_copy(kr, bank2(1)).then_inc(dve_step.sem, dve_step.up())
            dve.wait_ge(cqt_ps.sem, cqt_ps.due(dve))
            for k in range(2):
                ins = V.tensor_scalar(cqt[:, k, :], ps[:, 4, k * T:(k + 1) * T], gt[:, 140 + k:141 + k], None, ALU.mult)
            ins.then_inc(xt_done.sem, xt_done.up())
            dve.wait_ge(dve_step.sem, dve_step.now())
            dve.wait_ge(trig_done.sem, trig_done.due(dve))
            for t in range(2):
                rope(V, dve_step, dve_step, tmp, kr[:, t, 0:P].rearrange("p (h f) -> p h f", h=KVH), cs_q(t), KVH, ROT)
                for gr in range(KVH):
                    V.tensor_copy(kd[:, t, gr, :, :],
                                  kr[:, t, gr * HD:(gr + 1) * HD].unsqueeze(1).to_broadcast([P, 2, HD])
                    ).then_inc(kd_ready.sem, kd_ready.up())
            dve.wait_ge(used, 3)
            V.tensor_copy(kis, bank2(2)[:, :, 120:248]).then_inc(dve_step.sem, dve_step.up())
            V.tensor_scalar(wi, bank2(2)[:, :, 248:256], float(IH ** -0.5 * ID ** -0.5), None, ALU.mult
            ).then_inc(dve_step.sem, dve_step.up())
            dve.wait_ge(dve_step.sem, dve_step.now())
            for t in range(2):
                V.bn_stats(small[:, 40 + 6 * t:46 + 6 * t], kis[:, t, :]).then_inc(dve_step.sem, dve_step.up())
            dve.wait_ge(dve_step.sem, dve_step.now())
            for t in range(2):
                ins = V.bn_aggr(small[:, 60 + 2 * t:62 + 2 * t], small[:, 40 + 6 * t:46 + 6 * t])
            ins.then_inc(ki_var.sem, ki_var.up())
            dve.wait_ge(xh_done.sem, xh_done.due(dve))
            V.tensor_tensor(xl[:, 0:2, :], cqt, xh[:, 0:2, :].bitcast(F32), ALU.subtract
            ).then_inc(x_ready.sem, x_ready.up())
            dve.wait_ge(ki_rstd.sem, ki_rstd.due(dve))
            for t in range(2):
                V.tensor_scalar(kis[:, t, :], kis[:, t, :], small[:, 60 + 2 * t:61 + 2 * t],
                                small[:, 70 + 2 * t:71 + 2 * t], ALU.subtract, ALU.mult
                ).then_inc(dve_step.sem, dve_step.up())
            dve.wait_ge(dve_step.sem, dve_step.now())
            V.tensor_tensor(kis, kis, kg[:, 0:1, :].to_broadcast([P, 2, P]), ALU.mult
            ).then_inc(dve_step.sem, dve_step.up())
            dve.wait_ge(dve_step.sem, dve_step.now())
            V.tensor_tensor(kis, kis, kg[:, 1:2, :].to_broadcast([P, 2, P]), ALU.add
            ).then_inc(dve_step.sem, dve_step.up())
            dve.wait_ge(dve_step.sem, dve_step.now())
            for t in range(2):
                rope(V, dve_step, kd_ready, tmp, kis[:, t, :].unsqueeze(1), cs_i(t), 1, IROT)
            dve.wait_ge(kt_ps.sem, kt_ps.due(dve))
            V.tensor_copy(kit, ps[:, 6, 0:T]).then_inc(dve_step.sem, dve_step.up())
            for e in range(2):
                ins = V.tensor_copy(kpad[e * HD:(e + 1) * HD, :, e, :], bank2(5)[e * HD:(e + 1) * HD, :, :])
            ins.then_inc(kt_ready.sem, kt_ready.up())
            for t in range(2):
                dve.wait_ge(iq_copied.sem, iq_copied.due(dve))
                rope(V, dve_step, iq_rot, tmp, iq[:, t, :].rearrange("p (h f) -> p h f", h=IH), cs_i(t), IH, IROT)
            for p in range(IH // 2):
                dve.wait_ge(relu_done.sem, relu_done.due(dve))
                for e in range(2):
                    h = 2 * p + e
                    for t, (c0, c1) in enumerate(((0, P), (P, 3 * P))):
                        x, w = relu[:, p % 2, e, c0:c1], wi[:, t, h:h + 1]
                        if h == 0:
                            V.tensor_scalar(score[:, c0:c1], x, w, None, ALU.mult).then_inc(scored.sem, scored.up())
                        else:
                            dve.wait_ge(scored.sem, scored.now() - 1)
                            V.scalar_tensor_tensor(out=score[:, c0:c1], in0=x, scalar=w, in1=score[:, c0:c1],
                                                   op0=ALU.mult, op1=ALU.add).then_inc(scored.sem, scored.up())
            dve.wait_ge(scored.sem, scored.now())
            diagonal = score.rearrange("p (c t) -> p c t", c=3)[:, 0:3:2, :]
            V.tensor_tensor(diagonal, diagonal, causal.unsqueeze(1).to_broadcast([P, 2, P]), ALU.min
            ).then_inc(taken.sem, taken.up(2))
            for _ in range(TOPK // 8):
                for t, (c0, c1) in enumerate(((0, P), (P, 3 * P))):
                    dve.wait_ge(taken.sem, taken.now() - 1 + t)
                    V.max(top8[:, t, :], score[:, c0:c1]).then_inc(best.sem, best.up())
                for t, (c0, c1) in enumerate(((0, P), (P, 3 * P))):
                    dve.wait_ge(best.sem, best.now() - 1 + t)
                    V.match_replace(score[:, c0:c1], top8[:, t, :], score[:, c0:c1], TAKEN
                    ).then_inc(taken.sem, taken.up())
            dve.wait_ge(taken.sem, taken.now())
            V.tensor_scalar(sbias[:], score, TAKEN, -BIG, ALU.not_equal, ALU.mult
            ).then_inc(sel_done.sem, sel_done.up())
            dve.wait_ge(sel_done.sem, sel_done.now())
            diagonal = sbias[:].rearrange("p (c t) -> p c t", c=3)[:, 0:3:2, :]
            V.tensor_tensor(diagonal, diagonal, causal.unsqueeze(1).to_broadcast([P, 2, P]), ALU.min
            ).then_inc(sel_done.sem, sel_done.up())
            dve.wait_ge(sel_done.sem, sel_done.now())

            def outputs(i):
                V.tensor_tensor(xl[:, i, :], ps[:, 6 + i % 2, 0:T], xh[:, i, :].bitcast(F32), ALU.subtract
                ).then_inc(x_ready.sem, x_ready.up())

            attend_dve(dve, HEADS // 2, HD ** -0.5, sbias[:], outputs)

        def dsa_pool(pool):
            for t in range(2):
                pool.wait_ge(q_copied.sem, q_copied.due(pool))
                pool.wait_ge(trig_done.sem, 1)
                rope(nc.gpsimd, pool_step, q_rot, tmp[:, :, P:], q[:, t, :].rearrange("p (h f) -> p h f", h=HEADS),
                     cs_q(t), HEADS, ROT)

        def spread(x, k=2):
            return x.unsqueeze(1).to_broadcast([P, k, T])

        def mean_pe(pe, c, b=0):
            pe.wait_ge(r_ready.sem, r_ready.due(pe))
            for k in range(2):
                last = mm(ps[:, b, 0:T], mean_d[:], r[:, 2 * c + k, :], start=c + k == 0, stop=c + k == 4)
            if c == 3:
                last.then_inc(mean_ps.sem, mean_ps.up())

        def square_pe(pe, c, b=1):
            pe.wait_ge(sq_ready.sem, sq_ready.due(pe))
            for k in range(2):
                last = mm(ps[:, b, 0:T], mean_d[:], sq[:, 2 * (c % 2) + k, :], start=c + k == 0, stop=c + k == 4)
            last.then_inc(sq_used.sem, sq_used.up())

        def ln_pe(pe, b=0):
            for c in range(4):
                mean_pe(pe, c, b)
            for c in range(4):
                square_pe(pe, c, b + 1)

        def ln_act(act, last, more=True, b=0):
            hi_until(act, last + 4)
            nc.scalar.preload_act_table_set("natural_log_exp_and_others")
            for c in range(4):
                act.wait_ge(d_ready.sem, d_ready.due(act))
                if c >= 2:
                    act.wait_ge(sq_used.sem, sq_used.due(act))
                nc.scalar.activation(two(sq, c % 2), two(r, c), ACT.Square
                ).then_inc(sq_ready.sem, sq_ready.up())
            act.wait_ge(sq_used.sem, sq_used.due(act, 2))
            nc.scalar.activation(rs, ps[:, b + 1, 0:T], ACT.Ln, bias=eps[:, 0:1]
            ).then_inc(act_step.sem, act_step.up())
            act.wait_ge(act_step.sem, act_step.now())
            nc.scalar.activation(rs, rs, ACT.Exp, scale=-0.5).then_inc(rs_ready.sem, rs_ready.up())
            if more:
                x_act(act, done=nh_done)

        def ln_dve(dve, gain, bias, arrived, more=True, b=0):
            for c in range(4):
                arrived(dve, c)
                V.scalar_tensor_tensor(out=two(r, c), in0=two(xt, c), scalar=ALPHA, in1=bank2((b + 4) % 8 + c),
                                       op0=ALU.mult, op1=ALU.add).then_inc(r_ready.sem, r_ready.up())
            dve.wait_ge(mean_ps.sem, mean_ps.due(dve))
            for c in range(4):
                V.tensor_tensor(two(r, c), two(r, c), spread(ps[:, b, 0:T]), ALU.subtract
                ).then_inc(d_ready.sem, d_ready.up())
            dve.wait_ge(rs_ready.sem, rs_ready.due(dve))
            done = xt_done if more else stream
            for c in range(5):
                if c < 4:
                    V.tensor_tensor(two(r, c), two(r, c), spread(rs), ALU.mult).then_inc(scaled.sem, scaled.up())
                if c >= 1:
                    dve.wait_ge(scaled.sem, scaled.now() - (1 if c < 4 else 0))
                    for k in (2 * c - 2, 2 * c - 1):
                        ins = V.tensor_scalar(xt[:, k, :], r[:, k, :], gt[:, gain + k:gain + k + 1],
                                              gt[:, bias + k:bias + k + 1], ALU.mult, ALU.add)
                    ins.then_inc(done.sem, done.up())

        def times(i, k):
            return 0 if i is None else i * k

        def ffn_pe(pe, base):
            seen = h_ready.seen(pe)

            def pair(p, i=None):
                if p >= 2:
                    pe.wait_ge(h_ready.sem, times(i, 2) + (seen + p - 1))
                tile_a(pe, base + 2 * p, 2 * (p % 2), i=i, fresh=None if p else nx_ready)
                tile_a(pe, base + 2 * p + 1, 2 * (p % 2) + 1, i=i)

            PAIRS = NF // 2
            pair(0)
            pair(1)
            loops = (PAIRS - 2) // 2
            with pe.Fori(0, loops) as i:
                for j in range(2):
                    pair(2 + j, i)
            for p in range(2 + 2 * loops, PAIRS):
                pair(p)
            down = base + NF

            def products(n, j, i, ms, s=None):
                for m in ms:
                    for k in range(2):
                        o = k * D + m * P
                        f = times(i, 2 * RING) + (2 * j + k)
                        first = i is None and j + k == 0
                        x, y = ((hh[:, f, :], hl[:, f, :]) if i is None else
                                (hh[:, bass.ds(f, 1), :], hl[:, bass.ds(f, 1), :]))
                        last = mm3(ps[:, 4 + m // 2, m % 2 * T:(m % 2 + 1) * T],
                                   (wh[:, ring(n), o:o + P], wl[:, ring(n), o:o + P]), (x, y),
                                   first and m % 2 == 0, j == PAIRS - 1 and k == 1, skip=True)
                return last

            def tile(j, i=None):
                pe.wait_ge(h_ready.sem, times(i, RING) + (seen + j + 1))
                pe.wait_ge(lo_done, times(i, RING) + (down + j + 1))
                products(down + j, j, i, range(KD)).then_inc(used, 1)

            tile(0)
            with pe.Fori(0, (PAIRS - 3) // RING) as i:
                for j in range(1, 1 + RING):
                    tile(j, i)
            pe.wait_ge(h_ready.sem, seen + PAIRS)
            pe.wait_ge(lo_done, down + PAIRS)
            for m in range(KD):
                last = products(down + PAIRS - 2, PAIRS - 2, None, [m])
                if m == KD - 1:
                    last.then_inc(used, 1)
                last = products(down + PAIRS - 1, PAIRS - 1, None, [m])
                if m == KD - 1:
                    last.then_inc(used, 1)
                elif m % 2:
                    last.then_inc(y_done.sem, y_done.up())
            h_ready.skip(pe, PAIRS)

        def ffn_act(act, base):
            seen, mul = used, h_ready.seen(act)
            PAIRS = NF // 2

            def pair(p, i=None):
                n = base + 2 * p
                hi_at(act, n + 3, i)
                act.wait_ge(used, times(i, 4) + (n + 1))
                if p >= 2:
                    act.wait_ge(h_ready.sem, times(i, 2) + (mul + p - 1))
                nc.scalar.activation(silu_g[:, p % 2, :], ps[:, 2 * (p % 2), :], ACT.Silu).then_inc(s_done.sem, 1)
                hi_at(act, n + 4, i)

            def hi_at(act, n, i):
                if i is None:
                    hi_until(act, n)
                else:
                    hi(act, n, i)

            hi_until(act, base + 2)
            nc.scalar.preload_act_table(ACT.Silu)
            pair(0)
            pair(1)
            loops = (PAIRS - 2) // 2
            his_save = his[0]
            assert his_save == base + 7, his_save - base
            with act.Fori(0, loops) as i:
                for j in range(2):
                    pair(2 + j, i)
            his[0] = his_save + 4 * loops
            for p in range(2 + 2 * loops, PAIRS):
                pair(p)
            h_ready.skip(act, PAIRS)
            s_done.n += PAIRS
            down = base + NF
            n0 = his[0]
            loops = (PAIRS - 3) // RING
            with act.Fori(0, loops) as i:
                for j in range(RING):
                    hi(act, n0 + j, i)
            his[0] = n0 + RING * loops
            hi_until(act, down + PAIRS)

        def ffn_dve(dve, base):
            PAIRS = NF // 2
            s0, m0, u0 = s_done.seen(dve), h_mul.n, h_hi.n

            def pair(p, i=None):
                dve.wait_ge(s_done.sem, times(i, 2) + (s0 + p + 1))
                dve.wait_ge(used, times(i, 4) + (base + 2 * p + 2))
                nc.vector.tensor_tensor(hf[:, p % 2, :], silu_g[:, p % 2, :], ps[:, 2 * (p % 2) + 1, :],
                                        ALU.mult).then_inc(h_mul.sem, 1)
                dve.wait_ge(h_mul.sem, times(i, 2) + (m0 + p + 1))
                f = times(i, 4) + 2 * p
                x = (hh[:, f:f + 2, :], hl[:, f:f + 2, :]) if i is None else (
                    hh[:, bass.ds(f, 2), :], hl[:, bass.ds(f, 2), :])
                y = hf[:, p % 2, :].rearrange("p (k t) -> p k t", k=2)
                nc.vector.tensor_copy(x[0], y).then_inc(h_hi.sem, 1)
                dve.wait_ge(h_hi.sem, times(i, 2) + (u0 + p + 1))
                nc.vector.tensor_tensor(x[1], y, x[0].bitcast(F32), ALU.subtract).then_inc(h_ready.sem, 1)
                dve.wait_ge(h_ready.sem, times(i, 2) + (r0 + p + 1))

            r0 = h_ready.n
            pair(0)
            pair(1)
            loops = (PAIRS - 2) // 2
            with dve.Fori(0, loops) as i:
                for j in range(2):
                    pair(2 + j, i)
            for p in range(2 + 2 * loops, PAIRS):
                pair(p)
            for x in (h_mul, h_hi, h_ready):
                x.n += PAIRS
            s_done.skip(dve, PAIRS)

        def ffn_arrived(base):
            def arrived(dve, c):
                if c < 3:
                    dve.wait_ge(y_done.sem, y_done.due(dve))
                else:
                    dve.wait_ge(used, base + NF + NF // 2)
            return arrived

        def out_arrived(base):
            def arrived(dve, c):
                dve.wait_ge(used, base + c + 1)
            return arrived

        def flat(x):
            return x.rearrange("p a b -> p (a b)")

        def hgrn_pe(pe):
            for j in range(4):
                tile_b(pe, t_hi + j, [(t, 0, ps[:, j, t * T:(t + 1) * T]) for t in range(2)],
                       fresh=None if j else nx_ready)
            for o, n in enumerate((*range(t_hq, t_hq + 4), *range(t_hf, t_hf + 4), *range(t_hg, t_hg + 4))):
                evacuated = hg_v if o < 4 else hg_a
                pe.wait_ge(evacuated.sem, evacuated.due(pe))
                tile_a(pe, n, o % 4)
            pe.wait_ge(hg_raw.sem, 4)

            def levels(h):
                b, x = 2 * (h % 2), lev[:, h % 2, :, :]

                def chunks(l, k_, q_):
                    for c in range(NCH):
                        t = slice(c * CH, (c + 1) * CH)
                        last = mm(ps[c % 2 * CH:(c % 2 + 1) * CH, b + c // 2, l * CH:(l + 1) * CH], k_[:, t], q_[:, t],
                                  start=True, stop=True)
                    return last

                if h >= 2:
                    pe.wait_ge(at_ready.sem, h - 1)
                chunks(0, hk[:, h, :], hq[:, h, :])
                pe.wait_ge(level_ready.sem, 8 * h + 1)
                if h:
                    pe.wait_ge(cross_ready.sem, h)
                mm(ps[:, 4, 0:P], x[:, 0, 0:P], x[:, 0, P:T], start=True, stop=True)
                pe.wait_ge(level_ready.sem, 8 * h + 2)
                for i in range(2):
                    c = 2 * i * CH
                    mm(ps[0:CH, b + i, 7 * CH:8 * CH], x[:, 1, c:c + CH], x[:, 1, c + CH:c + 2 * CH], start=True, stop=True)
                for l in range(2, 8):
                    pe.wait_ge(level_ready.sem, 8 * h + l + 1)
                    last = chunks(l - 1, x[:, l, :], x[:, l, :])
                last.then_inc(levels_ps.sem, levels_ps.up())

            def values(h):
                pe.wait_ge(at_ready.sem, h + 1)
                pe.wait_ge(cross_ready.sem, h + 1)
                if h >= 4:
                    pe.wait_ge(normed.sem, h // 2 - 1)
                e = h % 2
                o_ = ps[:, 6 + h // 2 % 2, e * T:(e + 1) * T]
                val = [hv[:, t, h * P:(h + 1) * P] for t in range(2)]
                mm(o_[:, 0:P], val[0], at_h[:, e, 0, :], start=True, stop=True)
                mm(o_[:, P:T], val[0], at_h[:, e, 2, :], start=True, stop=False)
                mm(o_[:, P:T], val[1], at_h[:, e, 1, :], start=False, stop=True).then_inc(av_ps.sem, av_ps.up())

            def mean(p):
                pe.wait_ge(hg_sq.sem, p + 1)
                mm(ps[:, 5, :], mean_hd[:], o_tmp, start=True, stop=True).then_inc(hg_mean.sem, hg_mean.up())

            for h in range(IH):
                if h >= 4 and h % 2 == 0:
                    mean(h // 2 - 2)
                levels(h)
                if h >= 1:
                    values(h - 1)
            def part(j, ks, wait):
                pe.wait_ge(lo_done, t_hwo + j + 1)
                s = ring(t_hwo + j)
                for m in range(2):
                    for k in ks:
                        if wait and m == 0 and k % 2 == 0:
                            pe.wait_ge(x_ready.sem, x_ready.due(pe))
                        o = k * 256 + m * P
                        last = mm3(ps[:, j, m * T:(m + 1) * T], (wh[:, s, o:o + P], wl[:, s, o:o + P]),
                                   (xh[:, k, :], xl[:, k, :]), k + m == 0, k == KD - 1, skip=True)
                return last

            mean(2)
            part(0, range(4), True)
            values(IH - 1)
            part(1, range(4), False)
            part(2, range(4), False)
            mean(3)
            part(3, range(4), False)
            for j in range(4):
                part(j, range(4, KD), j == 0).then_inc(used, 1)

        def hgrn_act(act):
            nc.scalar.preload_act_table(ACT.Silu)
            for func, to, t0 in ((ACT.Silu, hq, t_hq), (ACT.Sigmoid, hk, t_hf)):
                for j in range(4):
                    hi_until(act, t0 + j + 3)
                    act.wait_ge(used, t0 + j + 1)
                    nc.scalar.activation(two(to, j), bank2(j), func).then_inc(hg_a.sem, hg_a.up())
            nc.scalar.preload_act_table_set("natural_log_exp_and_others")
            for j in range(4):
                act.wait_ge(hg_g.sem, hg_g.due(act))
                nc.scalar.activation(two(hb, j), two(hb, j), ACT.Ln).then_inc(hg_ln.sem, hg_ln.up())

            def decays(h):
                x = hb[:, h, :]
                for l in range(8):
                    y = dec[:, l % 4, :]
                    if l < 2:
                        if h:
                            act.wait_ge(level_ready.sem, 8 * h + l - 3)
                    else:
                        act.wait_ge(log_ready.sem, 6 * h + l - 1)
                    if l == 0:
                        nc.scalar.activation(y[:, 0:CH], x[:, 0:CH], ACT.Exp, scale=-1.0, bias=ends01[:, h:h + 1])
                        nc.scalar.activation(y[:, CH:P], x[:, CH:P], ACT.Exp, scale=-1.0, bias=x[:, P - 1:P])
                        nc.scalar.activation(y[:, P:P + CH], x[:, P:P + CH], ACT.Exp)
                        ins = nc.scalar.activation(y[:, P + CH:T], x[:, P + CH:T], ACT.Exp, bias=x[:, P + CH - 1:P + CH])
                    elif l == 1:
                        for c in (0, P):
                            nc.scalar.activation(y[:, c:c + CH], x[:, c:c + CH], ACT.Exp, scale=-1.0,
                                                 bias=x[:, c + CH - 1:c + CH])
                            ins = nc.scalar.activation(y[:, c + CH:c + P], x[:, c + CH:c + P], ACT.Exp)
                    else:
                        ins = nc.scalar.activation(y, y, ACT.Exp)
                    ins.then_inc(decay_ready.sem, decay_ready.up())

            def crossings(h):
                act.wait_ge(levels_ps.sem, h + 1)
                nc.scalar.activation(at_h[:, h % 2, 2, :], ps[:, 4, 0:P], ACT.Copy
                ).then_inc(cross_ready.sem, cross_ready.up())

            def squares(p):
                act.wait_ge(av_ps.sem, 2 * p + 2)
                if p:
                    act.wait_ge(normed.sem, p)
                nc.scalar.activation(o_tmp, ps[:, 6 + p % 2, :], ACT.Square).then_inc(hg_sq.sem, hg_sq.up())

            def roots(p):
                act.wait_ge(hg_mean.sem, p + 1)
                nc.scalar.activation(o_tmp, ps[:, 5, :], ACT.Ln, bias=eps[:, 1:2]).then_inc(act_step.sem, act_step.up())
                act.wait_ge(act_step.sem, act_step.now())
                nc.scalar.activation(o_tmp, o_tmp, ACT.Exp, scale=-0.5).then_inc(hg_rs.sem, hg_rs.up())

            def uppers(p):
                act.wait_ge(xt_done.sem, xt_done.due(act))
                nc.scalar.activation(two(xh, p), two(hgate, p), ACT.Copy).then_inc(xh_done.sem, xh_done.up())

            hi_until(act, t_hg + 3)
            for h in range(IH):
                if h % 2 == 0:
                    act.wait_ge(hg_b.sem, h // 2 + 1)
                decays(h)
                if h >= 1:
                    hi_until(act, min(t_hwo + h - 1, t_hwo + 3))
                if h == 1:
                    act.wait_ge(hg_raw.sem, 4)
                    nc.scalar.preload_act_table(ACT.Silu)
                    for j in range(4):
                        nc.scalar.activation(two(hgate, j), two(hgate, j), ACT.Silu
                        ).then_inc(silu_done.sem, silu_done.up())
                    nc.scalar.preload_act_table_set("natural_log_exp_and_others")
                if h >= 1:
                    crossings(h - 1)
                if h >= 3 and h % 2 == 1:
                    squares((h - 3) // 2)
                if h >= 4 and h % 2 == 0:
                    roots(h // 2 - 2)
                if h >= 5 and h % 2 == 1:
                    uppers((h - 5) // 2)
            crossings(IH - 1)
            roots(2)
            squares(3)
            uppers(2)
            roots(3)
            uppers(3)

        def hgrn_pool(pool):
            gp = nc.gpsimd
            for h in range(IH):
                if h % 2 == 0:
                    pool.wait_ge(hg_b.sem, h // 2 + 1)
                for l in range(2, 8):
                    d = LEVELS[l]
                    if h or l >= 4:
                        pool.wait_ge(level_ready.sem, 8 * h + l - 3)
                    xb, yb = (w.rearrange("p (n w) -> p n w", w=2 * d) for w in (hb[:, h, :], dec[:, l % 4, :]))
                    mid = xb[:, :, d - 1:d].to_broadcast([P, T // 2 // d, d])
                    gp.tensor_tensor(yb[:, :, 0:d], mid, xb[:, :, 0:d], ALU.subtract)
                    gp.tensor_tensor(yb[:, :, d:2 * d], xb[:, :, d:2 * d], mid, ALU.subtract
                    ).then_inc(log_ready.sem, log_ready.up())
                if h in (1, 3, 4, 6):
                    lo(pool, t_hwo + (1, 3, 4, 6).index(h))

        def hgrn_dve(dve):
            V.memset(at_h, 0.0).then_inc(dve_step.sem, dve_step.up())
            for j in range(4):
                dve.wait_ge(used, t_hi + j + 1)
                V.tensor_copy(hv[:, :, j * T:(j + 1) * T], bank2(j)).then_inc(hg_v.sem, hg_v.up())
            dve.wait_ge(hg_a.sem, hg_a.due(dve, 4))
            for j in range(4):
                dve.wait_ge(hg_a.sem, hg_a.due(dve))
                for h in (2 * j, 2 * j + 1):
                    V.tensor_scalar(hb[:, h, :], hk[:, h, :], one_lb[:, h:h + 1], lb[:, h:h + 1], ALU.mult, ALU.add
                    ).then_inc(dve_step.sem, dve_step.up())
                dve.wait_ge(dve_step.sem, dve_step.now())
                V.tensor_scalar(flat(two(hk, j)), flat(two(hb, j)), -1.0, 1.0, ALU.mult, ALU.add
                ).then_inc(hg_g.sem, hg_g.up())
            for j in range(4):
                dve.wait_ge(hg_ln.sem, hg_ln.due(dve))
                for h in (2 * j, 2 * j + 1):
                    V.tensor_tensor_scan(hb[:, h, :], restart[:], hb[:, h, :], 0.0, ALU.mult, ALU.add
                    ).then_inc(dve_step.sem, dve_step.up())
                dve.wait_ge(dve_step.sem, dve_step.now())
                V.tensor_tensor(ends01[:, 2 * j:2 * j + 2], two(hb, j)[:, :, CH - 1], two(hb, j)[:, :, P - 1], ALU.add
                ).then_inc(hg_b.sem, hg_b.up())

            def products(h, between):
                for l, d in enumerate(LEVELS):
                    dve.wait_ge(decay_ready.sem, 8 * h + l + 1)
                    if h >= 2 and l == 0:
                        dve.wait_ge(levels_ps.sem, h - 1)
                    y, e, k_, q_ = (w.rearrange("p (n w) -> p n w", w=2 * d) for w in (
                        lev[:, h % 2, l, :], dec[:, l % 4, :], hk[:, h, :], hq[:, h, :]))
                    V.tensor_tensor(y[:, :, 0:d], k_[:, :, 0:d], e[:, :, 0:d], ALU.mult)
                    V.tensor_tensor(y[:, :, d:2 * d], q_[:, :, d:2 * d], e[:, :, d:2 * d], ALU.mult
                    ).then_inc(level_ready.sem, level_ready.up())
                    if l in between:
                        between[l]()

            def mask(h):
                dve.wait_ge(levels_ps.sem, h + 1)
                V.tensor_tensor(masked_a, ps[:, 2 * (h % 2):2 * (h % 2) + 2, 0:len(MASKED) * CH],
                                lmask[:, :, :].rearrange("p l t -> p (l t)").unsqueeze(1).to_broadcast(
                                    [P, 2, len(MASKED) * CH]), ALU.mult).then_inc(masked_ready.sem, masked_ready.up())

            def add_levels(h):
                dve.wait_ge(masked_ready.sem, h + 1)
                V.tensor_reduce(at_c, masked_a.rearrange("p i (l t) -> p i t l", t=CH), AX.X, ALU.add)
                V.tensor_copy(at_h[0:CH, h % 2, 0:2, CH:P], ps[0:CH, 2 * (h % 2):2 * (h % 2) + 2, 7 * CH:8 * CH]
                ).then_inc(added.sem, added.up())

            def place(h):
                dve.wait_ge(added.sem, h + 1)
                V.tensor_copy(at_h[0:CH, h % 2, 0:2, 0:CH], at_c[0:CH, :, :])
                V.tensor_copy(at_h[CH:P, h % 2, 0:2, CH:P], at_c[CH:P, :, :]).then_inc(at_ready.sem, at_ready.up())

            def norm(p):
                if p == 0:
                    dve.wait_ge(silu_done.sem, 4)
                dve.wait_ge(hg_rs.sem, p + 1)
                V.scalar_tensor_tensor(out=o_tmp, in0=ps[:, 6 + p % 2, :], scalar=gt[:, 139:140], in1=o_tmp,
                                       op0=ALU.mult, op1=ALU.mult).then_inc(dve_step.sem, dve_step.up())
                dve.wait_ge(dve_step.sem, dve_step.now())
                V.tensor_tensor(flat(two(hgate, p)), o_tmp, flat(two(hgate, p)), ALU.mult
                ).then_inc(xt_done.sem, xt_done.up())
                V.tensor_copy(small[:, 80:82], small[:, 60:62]).then_inc(normed.sem, normed.up())

            for h in range(IH):
                between = {}
                if h >= 1:
                    between[4] = lambda: mask(h - 1)
                    between[5] = lambda: add_levels(h - 1)
                    between[6] = lambda: place(h - 1)
                if h >= 5 and h % 2 == 1:
                    between[1] = lambda: norm((h - 5) // 2)
                if h >= 6 and h % 2 == 0:
                    between[1] = lambda: x_lo(dve, h // 2 - 3, hgate)
                products(h, between)
                if h == 0:
                    for j in range(4):
                        dve.wait_ge(used, t_hg + j + 1)
                        V.tensor_copy(two(hgate, j), bank2(j)).then_inc(hg_raw.sem, hg_raw.up())
            x_lo(dve, 1, hgate)
            mask(IH - 1)
            add_levels(IH - 1)
            place(IH - 1)
            norm(2)
            x_lo(dve, 2, hgate)
            norm(3)
            x_lo(dve, 3, hgate)

        def rms_act(act, source, last):
            for c in range(4):
                hi_until(act, last + c)
                x = source(act, c)
                if c >= 2:
                    act.wait_ge(sq_used.sem, sq_used.due(act))
                nc.scalar.activation(two(sq, c % 2), x, ACT.Square).then_inc(sq_ready.sem, sq_ready.up())
            act.wait_ge(sq_used.sem, sq_used.due(act, 2))
            nc.scalar.activation(rs, ps[:, 1, 0:T], ACT.Ln, bias=eps[:, 1:2]
            ).then_inc(act_step.sem, act_step.up())
            act.wait_ge(act_step.sem, act_step.now())
            nc.scalar.activation(rs, rs, ACT.Exp, scale=-0.5).then_inc(rs_ready.sem, rs_ready.up())
            hi_until(act, last + 4)

        def pre_dve(dve, gain):
            dve.wait_ge(rs_ready.sem, rs_ready.due(dve))
            for c in range(4):
                for k in (2 * c, 2 * c + 1):
                    ins = V.scalar_tensor_tensor(out=r[:, k, :], in0=xt[:, k, :], scalar=gt[:, gain + k:gain + k + 1],
                                                 in1=rs, op0=ALU.mult, op1=ALU.mult)
                ins.then_inc(xt_done.sem, xt_done.up())

        def from_x(act, c):
            act.wait_ge(stream.sem, stream.due(act))
            return two(xt, c)

        def post_dve(dve, gain):
            dve.wait_ge(rs_ready.sem, rs_ready.due(dve))
            for c in range(5):
                if c < 4:
                    V.tensor_tensor(two(r, c), bank2(4 + c), spread(rs), ALU.mult).then_inc(scaled.sem, scaled.up())
                if c >= 1:
                    dve.wait_ge(scaled.sem, scaled.now() - (1 if c < 4 else 0))
                    for k in (2 * c - 2, 2 * c - 1):
                        ins = V.scalar_tensor_tensor(out=xt[:, k, :], in0=r[:, k, :], scalar=gt[:, gain + k:gain + k + 1],
                                                     in1=xt[:, k, :], op0=ALU.mult, op1=ALU.add)
                    ins.then_inc(stream.sem, stream.up())

        B2_D = 7
        GATES_AT = 15

        def gla_pe(pe):
            for o in range(GATES_AT):
                n = t_rest + o
                if 4 <= o < 4 + B2_D:
                    pe.wait_ge(b2_d.sem, o - 3)
                elif o >= 4:
                    pe.wait_ge(b2_a.sem, o - 3 - B2_D)
                if o < B2_D:
                    tile_b(pe, n, [(t, 0, ps[:, o % 4, t * T:(t + 1) * T]) for t in range(2)],
                           fresh=None if o else nx_ready)
                else:
                    tile_a(pe, n, o % 4)
                if o == 3:
                    pe.wait_ge(b2_d.sem, 3)
                    for t in range(2):
                        last = nc.tensor.transpose(ps[0:GLR, 4, t * P:(t + 1) * P], tk[:, t, 0:GLR], ident[:])
                    last.then_inc(ha_ps.sem, ha_ps.up())
                if o == 4:
                    pe.wait_ge(ha_done.sem, ha_done.due(pe))
                    for h in range(GH):
                        last = mm(ps[:, 5 + h // 2, h % 2 * T:(h % 2 + 1) * T], wa[:, h * GK:(h + 1) * GK], ha,
                                  start=True, stop=True)
                    last.then_inc(z_ps.sem, z_ps.up())

            def gate(j):
                pe.wait_ge(b2_a.sem, GATES_AT - 2 - B2_D + j)
                tile_a(pe, t_gate + j, j % 3)

            def scores(h):
                b = ps[:, 4 + h % 2, :]
                k_ = kdec[:, h, :]
                mm(b[0:CH, 0:T], k_[:, 0:CH], gqh[:, 0, h, :], start=True, stop=True)
                mm(b[CH:P, CH:T], k_[:, CH:P], gqh[:, 1, h, CH:T], start=True, stop=True)
                mm(b[0:CH, T:T + P], k_[:, P:P + CH], gqh[:, 2, h, P:T], start=True, stop=True)
                mm(b[CH:P, T + CH:T + P], k_[:, P + CH:T], gq[:, h, P + CH:T], start=True, stop=True).then_inc(ga_ps.sem, ga_ps.up())

            def values(h):
                pe.wait_ge(ga_at.sem, ga_at.due(pe))
                for j in range(2):
                    o_ = ps[:, 6 + h % 2, j * T:(j + 1) * T]
                    c = h * GV + j * P
                    mm(o_[:, 0:P], gv[:, 0, c:c + P], at_g[:, h % 2, 0:P], start=True, stop=True)
                    mm(o_[:, P:T], gv[:, 0, c:c + P], at_g[:, h % 2, P:T], start=True, stop=False)
                    last = mm(o_[:, P:T], gv[:, 1, c:c + P], at_g[:, h % 2, T:T + P], start=False, stop=True)
                last.then_inc(go_ps.sem, go_ps.up())

            def mean(h):
                pe.wait_ge(go_sq.sem, go_sq.due(pe))
                if h:
                    pe.wait_ge(go_rs.sem, h)
                for j in range(2):
                    last = mm(ps[:, 3, 0:T], mean_hd[:], g_sq[:, h % 2, j * T:(j + 1) * T], start=j == 0, stop=j == 1)
                last.then_inc(go_mean.sem, go_mean.up())

            pe.wait_ge(gqh_done.sem, gqh_done.due(pe))
            for h in range(GH):
                scores(h)
                gate(2 * h)
                gate(2 * h + 1)
                if h:
                    mean(h - 1)
                values(h)
            mean(GH - 1)
            for j in range(4):
                tile_a(pe, t_gwo + j, 4 + j, fresh=None if j else nx_ready)
                if j == 2:
                    pe.wait_ge(b2_a.sem, GATES_AT + 8 - B2_D)
                    pe.wait_ge(go_rs.sem, GH)
                    pe.wait_ge(lat_scaled.sem, lat_scaled.due(pe))
                    pe.wait_ge(kx_done.sem, kx_done.due(pe))
                    for m in range(5):
                        for t in range(2):
                            c = GLR + m * P
                            nc.tensor.transpose(ps[:, m // 2, m % 2 * T + t * P:m % 2 * T + (t + 1) * P],
                                                tk[:, t, c:c + P], ident[:])
                    for x in range(2):
                        for t in range(2):
                            last = nc.tensor.transpose(ps[:, 3, x * T + t * P:x * T + (t + 1) * P], kx[:, t, x, :],
                                                       ident[:])
                    last.then_inc(lat_ps.sem, lat_ps.up())

        def gla_act(act):
            for o in range(GATES_AT):
                n = t_rest + o
                hi_until(act, n + 3)
                if o == 5:
                    act.wait_ge(z_ps.sem, z_ps.due(act))
                    for h in range(GH):
                        ins = nc.scalar.activation(z[:, h * T:(h + 1) * T],
                                                   ps[:, 5 + h // 2, h % 2 * T:(h % 2 + 1) * T],
                                                   ACT.Identity, bias=gt[:, 128 + h:129 + h])
                    ins.then_inc(z_done.sem, z_done.up())
                if o < B2_D:
                    continue
                act.wait_ge(used, n + 1)
                b = bank2(o % 4)
                j = n - t_gq
                if j < 2:
                    nc.scalar.activation(gq[:, 2 * j:2 * j + 2, :], b, ACT.Copy, scale=GK ** -0.5
                    ).then_inc(b2_a.sem, b2_a.up())
                elif j < 4:
                    nc.scalar.activation(gk[:, 2 * j - 4:2 * j - 2, :], b, ACT.Copy).then_inc(b2_a.sem, b2_a.up())
                else:
                    nc.scalar.activation(two(sg, j - 4), b, ACT.Silu).then_inc(b2_a.sem, b2_a.up())
                if o == 7:
                    act.wait_ge(nz_done.sem, nz_done.due(act))
                    nc.scalar.activation(nz, nz, ACT.Exp).then_inc(act_step.sem, act_step.up())
                    act.wait_ge(act_step.sem, act_step.now())
                    nc.scalar.activation(nz, nz, ACT.Ln, bias=1.0).then_inc(sp_done.sem, sp_done.up())
                if o == 10:
                    act.wait_ge(gb_done.sem, gb_done.due(act))
                    nc.scalar.activation(flat(fl), flat(fl), ACT.Exp)
                    nc.scalar.activation(flat(kdec), flat(kdec), ACT.Exp).then_inc(kdec_e.sem, kdec_e.up())
                    nc.scalar.preload_act_table(ACT.Silu)
            nc.scalar.preload_act_table_set("natural_log_exp_and_others")

            def gate(j):
                hi_until(act, t_gate + j + 3)
                act.wait_ge(used, t_gate + j + 1)
                for k in range(2):
                    m = 2 * j + k
                    ins = nc.scalar.activation(gates[:, m, :], bank2(j % 3)[:, k, :], ACT.Exp, scale=-1.0,
                                               bias=gt[:, 96 + m:97 + m])
                ins.then_inc(b2_a.sem, b2_a.up())

            def sigmoid(c):
                act.wait_ge(b2_a.sem, GATES_AT + 2 * c + 2 - B2_D)
                x = flat(gates[:, 4 * c:4 * c + 4, :])
                nc.scalar.activation(x, x, ACT.Ln, bias=1.0).then_inc(act_step.sem, act_step.up())
                act.wait_ge(act_step.sem, act_step.now())
                nc.scalar.activation(x, x, ACT.Exp, scale=-1.0).then_inc(gates_done.sem, gates_done.up())

            def squares(h):
                act.wait_ge(go_ps.sem, go_ps.due(act))
                nc.scalar.activation(g_sq[:, h % 2, :], ps[:, 6 + h % 2, :], ACT.Square
                ).then_inc(go_sq.sem, go_sq.up())

            def roots(h):
                act.wait_ge(go_mean.sem, go_mean.due(act))
                nc.scalar.activation(g_rs[:, h % 2, :], ps[:, 3, 0:T], ACT.Ln, scale=0.5, bias=eps[:, 1:2]
                ).then_inc(act_step.sem, act_step.up())
                act.wait_ge(act_step.sem, act_step.now())
                nc.scalar.activation(g_rs[:, h % 2, :], g_rs[:, h % 2, :], ACT.Exp, scale=-0.5
                ).then_inc(go_rs.sem, go_rs.up())

            def uppers(h):
                act.wait_ge(xt_done.sem, xt_done.due(act))
                nc.scalar.activation(two(xh, h), two(sg, h), ACT.Copy).then_inc(nh_done.sem, nh_done.up())

            for h in range(GH):
                gate(2 * h)
                gate(2 * h + 1)
                if h:
                    roots(h - 1)
                squares(h)
                if h < 2:
                    sigmoid(h)
            for h in range(GH - 1):
                uppers(h)
            roots(GH - 1)
            uppers(GH - 1)
            hi_until(act, t_gwo + 4)
            sigmoid(2)
            sigmoid(3)

        def gla_dve(dve):
            for o in range(B2_D):
                dve.wait_ge(used, t_rest + o + 1)
                b = bank2(o % 4)
                if o < 2:
                    V.tensor_copy(tk[:, :, o * 256:(o + 1) * 256], b).then_inc(b2_d.sem, b2_d.up())
                elif o == 2:
                    V.tensor_copy(tk[:, :, 512:NREST], b[:, :, 768 - NREST:256]).then_inc(b2_d.sem, b2_d.up())
                else:
                    V.tensor_copy(gv[:, :, (o - 3) * T:(o - 2) * T], b).then_inc(b2_d.sem, b2_d.up())
                if o == 3:
                    dve.wait_ge(ha_ps.sem, ha_ps.due(dve))
                    V.tensor_copy(ha, ps[0:GLR, 4, 0:T]).then_inc(ha_done.sem, ha_done.up())
            dve.wait_ge(z_done.sem, z_done.due(dve))
            V.scalar_tensor_tensor(out=nz, in0=z, scalar=-1.0, in1=z, op0=ALU.mult, op1=ALU.min
            ).then_inc(nz_done.sem, nz_done.up())
            dve.wait_ge(sp_done.sem, sp_done.due(dve))
            V.scalar_tensor_tensor(out=z, in0=z, scalar=0.0, in1=nz, op0=ALU.min, op1=ALU.subtract
            ).then_inc(dve_step.sem, dve_step.up())
            dve.wait_ge(dve_step.sem, dve_step.now())
            V.tensor_scalar(z, z, 1.0 / 16, None, ALU.mult).then_inc(dve_step.sem, dve_step.up())
            dve.wait_ge(dve_step.sem, dve_step.now())
            for h in range(GH):
                V.tensor_tensor_scan(gb[:, h, :], restart[:], z[:, h * T:(h + 1) * T], 0.0, ALU.mult, ALU.add
                ).then_inc(dve_step.sem, dve_step.up())
                dve.wait_ge(dve_step.sem, dve_step.now())
            ends = gb[:, :, CH - 1:T:CH]
            V.tensor_copy(fl[:, :, 0:3], ends[:, :, 1:4]).then_inc(dve_step.sem, dve_step.up())
            V.tensor_tensor(fl[:, :, 3:5], ends[:, :, 1:3], ends[:, :, 2:4], ALU.add
            ).then_inc(dve_step.sem, dve_step.up())
            dve.wait_ge(dve_step.sem, dve_step.now())
            V.tensor_tensor(fl[:, :, 5:6], fl[:, :, 3:4], ends[:, :, 3:4], ALU.add
            ).then_inc(dve_step.sem, dve_step.up())
            by_chunk = flat(gb).rearrange("p (c t) -> p c t", t=CH)
            V.tensor_tensor(flat(kdec).rearrange("p (c t) -> p c t", t=CH),
                            by_chunk[:, :, CH - 1:CH].to_broadcast([P, GH * NCH, CH]), by_chunk, ALU.subtract
            ).then_inc(gb_done.sem, gb_done.up())
            dve.wait_ge(b2_a.sem, 4)
            dve.wait_ge(kdec_e.sem, kdec_e.due(dve))
            V.tensor_tensor(flat(kdec), flat(kdec), flat(gk), ALU.mult).then_inc(dve_step.sem, dve_step.up())
            for c0 in range(3):
                V.tensor_copy(gqh[:, c0, :, c0 * CH:(c0 + 1) * CH], gq[:, :, c0 * CH:(c0 + 1) * CH]
                ).then_inc(dve_step.sem, dve_step.up())
                for c in range(c0 + 1, NCH):
                    f = {(0, 1): 0, (1, 2): 1, (2, 3): 2, (0, 2): 3, (1, 3): 4, (0, 3): 5}[c0, c]
                    V.tensor_tensor(gqh[:, c0, :, c * CH:(c + 1) * CH], gq[:, :, c * CH:(c + 1) * CH],
                                    fl[:, :, f:f + 1].to_broadcast([P, GH, CH]), ALU.mult
                    ).then_inc(dve_step.sem, dve_step.up())
            V.memset(at_g, 0.0).then_inc(gqh_done.sem, gqh_done.up())

            def weights(h):
                dve.wait_ge(ga_ps.sem, ga_ps.due(dve))
                b, x = ps[:, 4 + h % 2, :], at_g[:, h % 2, :]
                V.tensor_copy(x[0:CH, :], b[0:CH, 0:3 * P]).then_inc(dve_step.sem, dve_step.up())
                V.tensor_copy(x[CH:P, CH:T], b[CH:P, CH:T]).then_inc(dve_step.sem, dve_step.up())
                V.tensor_copy(x[CH:P, T + CH:T + P], b[CH:P, T + CH:T + P]).then_inc(ga_at.sem, ga_at.up())

            weights(0)
            for h in range(GH):
                if h + 1 < GH:
                    weights(h + 1)
                dve.wait_ge(go_rs.sem, go_rs.due(dve))
                y = g_tmp.rearrange("p (j t) -> p j t", j=2)
                V.tensor_tensor(y, bank2(6 + h % 2), spread(g_rs[:, h % 2, :]), ALU.mult
                ).then_inc(dve_step.sem, dve_step.up())
                dve.wait_ge(dve_step.sem, dve_step.now())
                for j in range(2):
                    ins = V.scalar_tensor_tensor(out=sg[:, 2 * h + j, :], in0=y[:, j, :], scalar=gt[:, 132 + j:133 + j],
                                                 in1=sg[:, 2 * h + j, :], op0=ALU.mult, op1=ALU.mult)
                ins.then_inc(xt_done.sem, xt_done.up())
                dve.wait_ge(xt_done.sem, xt_done.now())
            for t in range(2):
                for x in range(2):
                    c = GLR + QL2 + KVL2 + x * HR
                    ins = V.tensor_copy(kx[:, t, x, :].rearrange("p (a b) -> p a b", a=4),
                                        tk[:, t, c:c + HR].unsqueeze(1).to_broadcast([P, 4, HR]))
            ins.then_inc(kx_done.sem, kx_done.up())
            def gated(c):
                dve.wait_ge(used, t_gwo + c + 1)
                V.tensor_tensor(two(ya, c), bank2(4 + c), two(gates, c), ALU.mult).then_inc(ya_done.sem, ya_done.up())

            dve.wait_ge(gates_done.sem, 2)
            gated(0)
            gated(1)
            dve.wait_ge(lat_ps.sem, lat_ps.due(dve))
            for m in range(5):
                ins = V.tensor_scalar(lat[:, m, :], ps[:, m // 2, m % 2 * T:(m % 2 + 1) * T], gt[:, 134 + m:135 + m],
                                      None, ALU.mult)
            ins.then_inc(xt_done.sem, xt_done.up())
            gated(2)
            gated(3)

        def mla_pe(pe):
            pe.wait_ge(x_ready.sem, x_ready.due(pe))
            pe.wait_ge(ya_done.sem, ya_done.due(pe, 2))
            four = (0, P, 2 * P, 3 * P)
            tile_a(pe, t_uq, 4, kt=KQ, width=512, m_cols=four)
            pe.wait_ge(ya_done.sem, ya_done.due(pe, 2))
            tile_a(pe, t_uq + 1, 6, kt=KQ, width=512, m_cols=four)
            tile_a(pe, t_uq + 2, 0, kt=KQ, width=512, m_cols=four)
            for j, (kb, vb) in enumerate(((2, 4), (6, 0))):
                n = t_ukv + j
                evacuated = m_d if j == 0 else m_a
                pe.wait_ge(evacuated.sem, evacuated.due(pe))
                tile_a(pe, n, kb, kt=2, width=1024, m_cols=tuple(h * 256 for h in range(4)), x0=3, done=False)

                pe.wait_ge(evacuated.sem, evacuated.due(pe))
                s = ring(n)
                for t in range(2):
                    for k in range(2):
                        x = slice(t * P, (t + 1) * P)
                        w = [y[:, s, k * 1024:(k + 1) * 1024].rearrange("p (h c) -> p h c", h=4)[:, :, MN:MN + MV]
                             for y in (wh, wl)]
                        last = mm3(ps[:, vb + t, :].rearrange("p (h c) -> p h c", h=4),
                                   (xh[:, 3 + k, x], xl[:, 3 + k, x]), w, k == 0, k == 1)
                last.then_inc(used, 1)
            pe.wait_ge(m_a.sem, m_a.due(pe, 2))
            pe.wait_ge(m_d.sem, m_d.due(pe, 3))

            def logits(i):
                for e in range(2):
                    h = 2 * i + e
                    b = 2 * (i % 2) + e
                    for t, (c0, c1) in enumerate(((0, P), (P, 3 * P))):
                        y = slice(t * P, (t + 1) * P)
                        mm(ps[:, b, c0:c1], qn[:, h, y], kn[:, h, 0:c1 - c0], start=True, stop=False)
                        for x in range(2):
                            last = mm(ps[:, b, c0:c1], rr[:, x, h // 4, y], kp[x][:, h % 4, 0:c1 - c0],
                                      start=False, stop=x == 1)
                return last

            def weighted(i, e, pt, _):
                h = 2 * i + e
                o_ = ps[:, 6 + i % 2, e * T:(e + 1) * T]
                val = [vm[:, t, h * MV:(h + 1) * MV] for t in range(2)]
                mm(o_[:, 0:P], val[0], pt[:, 0:P], start=True, stop=True)
                mm(o_[:, P:T], val[0], pt[:, P:2 * P], start=True, stop=False)
                return mm(o_[:, P:T], val[1], pt[:, 2 * P:3 * P], start=False, stop=True)

            attend_pe(pe, MH // 2, logits, weighted)
            out_pe(pe, t_mwo)
            out_pe(pe, t_out, moving=4)

        def mla_act(act):
            for i, (c0, c1) in enumerate(((GLR, GLR + QL2), (GLR + QL2, GLR + QL2 + KVL2))):
                for t in range(2):
                    nc.scalar.activation(flat(lat)[:, 0:c1 - c0], tk[:, t, c0:c1], ACT.Square,
                                         accum_out=small[:, 2 * i + t:2 * i + t + 1]
                    ).then_inc(act_step.sem, act_step.up())
                    act.wait_ge(act_step.sem, act_step.now())
                nc.scalar.activation(small[:, 4 + 2 * i:6 + 2 * i], small[:, 2 * i:2 * i + 2], ACT.Ln,
                                     scale=1.0 / (c1 - c0), bias=eps[:, 1:2]).then_inc(act_step.sem, act_step.up())
                act.wait_ge(act_step.sem, act_step.now())
                nc.scalar.activation(small[:, 4 + 2 * i:6 + 2 * i], small[:, 4 + 2 * i:6 + 2 * i], ACT.Exp, scale=-0.5
                ).then_inc(act_step.sem, act_step.up())
                act.wait_ge(act_step.sem, act_step.now())
                for t in range(2):
                    ins = nc.scalar.activation(tk[:, t, c0:c1], tk[:, t, c0:c1], ACT.Copy,
                                               scale=small[:, 4 + 2 * i + t:5 + 2 * i + t])
                    if (i, t) != (1, 1):
                        ins.then_inc(act_step.sem, act_step.up())
            ins.then_inc(lat_scaled.sem, lat_scaled.up())
            hi_until(act, t_gwo + 6)
            act.wait_ge(used, t_gwo + 4)
            act.wait_ge(xt_done.sem, xt_done.due(act))
            nc.scalar.activation(xh[:, 0:5, :], lat, ACT.Copy).then_inc(xh_done.sem, xh_done.up())
            hi_until(act, t_gwo + 7)

            for j, (to, n, b) in enumerate(((qn[:, 0:4, :], t_uq + 1, 6), (qn[:, 4:8, :], t_uq + 2, 0),
                                            (kn[:, 0:4, :], t_ukv, 2), (kn[:, 4:8, :], t_ukv + 1, 6))):
                hi_until(act, n + 3)
                act.wait_ge(used, n + 1)
                nc.scalar.activation(to, ps[:, b:b + 2, :].rearrange("p b (k t) -> p (b k) t", t=T), ACT.Copy
                ).then_inc(m_a.sem, m_a.up())
            hi_until(act, t_mwo + 3)

            def outputs(i):
                nc.scalar.activation(two(xh, i), bank2(6 + i % 2), ACT.Copy).then_inc(oh_done.sem, oh_done.up())

            attend_act(act, MH // 2, (MN + MR) ** -0.5, outputs)
            hi_until(act, t_mwo + 6)
            act.wait_ge(used, t_mwo + 4)
            x_act(act, r)
            hi_until(act, t_mwo + 7)
            def mixed(act, c):
                act.wait_ge(used, t_out + c + 1)
                return bank2(4 + c)
            rms_act(act, mixed, t_out + 3)

        def mla_dve(dve):
            dve.wait_ge(xh_done.sem, xh_done.due(dve))
            V.tensor_tensor(xl[:, 0:5, :], lat, xh[:, 0:5, :].bitcast(F32), ALU.subtract
            ).then_inc(x_ready.sem, x_ready.up())
            cos, sin = trig_t[:, 0, :], trig_t[:, 1, :]
            k1, k2 = ps[:, 3, 0:T], ps[:, 3, T:2 * T]
            for j, (x, y) in enumerate(((k1, cos), (k2, sin), (k2, cos), (k1, sin))):
                V.tensor_tensor(tmp2[:, j, :], x, y, ALU.mult).then_inc(dve_step.sem, dve_step.up())
                dve.wait_ge(dve_step.sem, dve_step.now())
            V.tensor_tensor(tmp2[:, 0, :], tmp2[:, 0, :], tmp2[:, 1, :], ALU.subtract
            ).then_inc(dve_step.sem, dve_step.up())
            dve.wait_ge(dve_step.sem, dve_step.now())
            V.tensor_tensor(tmp2[:, 2, :], tmp2[:, 2, :], tmp2[:, 3, :], ALU.add
            ).then_inc(dve_step.sem, dve_step.up())
            for x in range(2):
                V.memset(kp[x], 0.0).then_inc(dve_step.sem, dve_step.up())
                dve.wait_ge(dve_step.sem, dve_step.now())
                for h in range(4):
                    V.tensor_copy(kp[x][HR * h:HR * (h + 1), h, :], tmp2[HR * h:HR * (h + 1), 2 * x, :]
                    ).then_inc(dve_step.sem, dve_step.up())
            V.tensor_copy(small[:, 80:82], small[:, 60:62]).then_inc(m_d.sem, m_d.up())
            dve.wait_ge(used, t_uq + 1)
            q1, q2 = bank2(4), bank2(5)
            rv = [rp[:, j, :].rearrange("p (k t) -> p k t", k=2) for j in range(2)]
            for x, (y, w, op) in enumerate(((q1, q2, ALU.subtract), (q2, q1, ALU.add))):
                V.tensor_tensor(rv[0], y, spread(cos), ALU.mult).then_inc(dve_step.sem, dve_step.up())
                dve.wait_ge(dve_step.sem, dve_step.now())
                V.tensor_tensor(rv[1], w, spread(sin), ALU.mult).then_inc(dve_step.sem, dve_step.up())
                dve.wait_ge(dve_step.sem, dve_step.now())
                V.tensor_tensor(rr[:, x, :, :], rv[0], rv[1], op).then_inc(dve_step.sem, dve_step.up())
                dve.wait_ge(dve_step.sem, dve_step.now())
            V.tensor_copy(small[:, 80:82], small[:, 60:62]).then_inc(m_d.sem, m_d.up())
            for j, vb in enumerate((4, 0)):
                dve.wait_ge(used, t_ukv + j + 1)
                for t in range(2):
                    ins = V.tensor_copy(vm[:, t, j * 512:(j + 1) * 512], ps[:, vb + t, :])
                    if t == 0:
                        ins.then_inc(dve_step.sem, dve_step.up())
                ins.then_inc(m_d.sem, m_d.up())
            V.tensor_copy(small[:, 80:82], small[:, 60:62]).then_inc(m_d.sem, m_d.up())

            def outputs(i):
                V.tensor_tensor(two(xl, i), bank2(6 + i % 2), two(xh, i).bitcast(F32), ALU.subtract
                ).then_inc(x_ready.sem, x_ready.up())

            attend_dve(dve, MH // 2, (MN + MR) ** -0.5, mbias[:], outputs)
            dve.wait_ge(gates_done.sem, 4)
            for c in range(4):
                dve.wait_ge(used, t_mwo + c + 1)
                V.tensor_tensor(two(r, c), bank2(4 + c), two(gates, 4 + c), ALU.mult
                ).then_inc(dve_step.sem, dve_step.up())
                dve.wait_ge(dve_step.sem, dve_step.now())
                V.tensor_tensor(two(r, c), two(r, c), two(ya, c), ALU.add).then_inc(xt_done.sem, xt_done.up())
            for c in range(4):
                x_lo(dve, c, r)

        def finish_pe(pe):
            stream.skip(pe, 8)
            for c in range(4):
                pe.wait_ge(stream.sem, stream.due(pe))
                for k in (2 * c, 2 * c + 1):
                    for t in range(2):
                        last = nc.tensor.transpose(ps[:, 2 * t + k // 4, k % 4 * P:(k % 4 + 1) * P],
                                                   xt[:, k, t * P:(t + 1) * P], ident[:])
                if c % 2:
                    last.then_inc(out_ps.sem, out_ps.up())

        def half(t, c):
            return out_sb[:, t, c * 512:(c + 1) * 512]

        def finish_act(act):
            for c in range(2):
                act.wait_ge(out_ps.sem, out_ps.due(act))
                nc.scalar.activation(half(0, c), ps[:, c, :], ACT.Copy).then_inc(out_done.sem, out_done.up())

        def finish_dve(dve):
            for c in range(2):
                dve.wait_ge(out_ps.sem, out_ps.due(dve))
                V.tensor_copy(half(1, c), ps[:, 2 + c, :]).then_inc(out_done2.sem, out_done2.up())

        def finish_sp(sp):
            for c in range(2):
                for t, done in ((0, out_done), (1, out_done2)):
                    sp.wait_ge(done.sem, c + 1)
                    sp.dma_start(out[0, t * P:(t + 1) * P, c * 512:(c + 1) * 512], half(t, c)).then_inc(stored, 16)
            sp.wait_ge(stored, 64)

        block = ctx.enter_context(nc.Block())

        @block.sync
        def _(sp):
            sp.dma_start(x_tok, A["x"][0].rearrange("(t p) d -> p t d", p=P)).then_inc(x_in, 16)
            for to, src in ((pos_i, A["positions"][0].rearrange("(t p) -> p t", p=P)),
                            (pos_t, A["positions_2"][0, :].partition_broadcast(P)),
                            (inv24[:], A["inv24"][0, :].partition_broadcast(P)), (inv_t[:], A["inv_t"])):
                sp.dma_start(to, src, allow_slow_non_contiguous=True).then_inc(pos_in, 16)
            for n in range(3):
                load(sp, n)
            setup_sp(sp)
            n = 3
            while n < len(tiles):
                run = runs.get(n)
                if run is None:
                    load(sp, n)
                    n += 1
                    continue
                count, sources = run
                with sp.Fori(0, count) as i:
                    for j, source in enumerate(sources):
                        load(sp, n + j, i, source)
                n += count * len(sources)
            finish_sp(sp)

        def ffn_y(base):
            def source(act, c):
                if c < 3:
                    act.wait_ge(y_done.sem, y_done.due(act))
                else:
                    act.wait_ge(used, base + NF + NF // 2)
                return bank2(4 + c)
            return source

        @block.scalar
        def _(act):
            hi_until(act, 0)
            x_act(act)
            hi_until(act, 2)
            setup_act2(act)
            hi_until(act, 3)
            dsa_act(act)
            ln_act(act, t_wo + 3)
            ffn_act(act, t_ffn0)
            ln_act(act, t_ffn0 + 32)
            hgrn_act(act)
            ln_act(act, t_hwo + 3, b=4)
            ffn_act(act, t_ffn1)
            ln_act(act, t_ffn1 + 32, more=False)
            rms_act(act, from_x, t_ffn1 + 32)
            x_act(act, r, nh_done)
            gla_act(act)
            mla_act(act)
            rms_act(act, from_x, t_out + 3)
            x_act(act, r, nh_done)
            ffn_act(act, t_ffn2)
            y_done.skip(act, 6)
            nc.scalar.preload_act_table_set("natural_log_exp_and_others")
            rms_act(act, ffn_y(t_ffn2), t_ffn2 + 32)
            finish_act(act)

        @block.gpsimd
        def _(pool):
            setup_pool(pool)
            for n in range(5):
                lo(pool, n)
            dsa_pool(pool)
            for n in range(5, 9):
                lo(pool, n)

            def until(n, m):
                passes = (m - n) // RING
                with pool.Fori(0, passes) as i:
                    for j in range(RING):
                        lo(pool, n + j, i)
                for n in range(n + passes * RING, m):
                    lo(pool, n)

            until(9, t_ffn0 + 4)
            norm_pool(pool)
            until(t_ffn0 + 4, t_ffn0 + NF)
            setup_pool2(pool)
            until(t_ffn0 + NF, t_hi + 4)
            norm_pool(pool)
            until(t_hi + 4, t_hwo)
            hgrn_pool(pool)
            until(t_ffn1, t_ffn1 + 4)
            norm_pool(pool)
            until(t_ffn1 + 4, t_rest + 4)
            norm_pool(pool, r)
            until(t_rest + 4, t_gwo + 3)
            norm_pool(pool, sg)
            until(t_gwo + 3, t_ffn2 + 4)
            norm_pool(pool, r)
            until(t_ffn2 + 4, len(tiles))

        @block.vector
        def _(dve):
            setup_x_dve(dve)
            setup_dve(dve)
            gains_dve(dve)
            dsa_dve(dve)
            ln_dve(dve, 0, 32, out_arrived(t_wo))
            ffn_dve(dve, t_ffn0)
            setup_dve2(dve)
            ln_dve(dve, 8, 40, ffn_arrived(t_ffn0))
            hgrn_dve(dve)
            ln_dve(dve, 16, 48, out_arrived(t_hwo), b=4)
            ffn_dve(dve, t_ffn1)
            ln_dve(dve, 24, 56, ffn_arrived(t_ffn1), more=False)
            pre_dve(dve, 64)
            gla_dve(dve)
            mla_dve(dve)
            post_dve(dve, 72)
            pre_dve(dve, 80)
            ffn_dve(dve, t_ffn2)
            post_dve(dve, 88)
            finish_dve(dve)

        @block.tensor
        def _(pe):
            setup_pe(pe)
            dsa_pe(pe)
            ln_pe(pe)
            ffn_pe(pe, t_ffn0)
            ln_pe(pe)
            hgrn_pe(pe)
            ln_pe(pe, b=4)
            ffn_pe(pe, t_ffn1)
            ln_pe(pe)
            for c in range(4):
                square_pe(pe, c)
            gla_pe(pe)
            mla_pe(pe)
            for c in (*range(4), *range(4)):
                square_pe(pe, c)
            ffn_pe(pe, t_ffn2)
            for c in range(4):
                square_pe(pe, c)
            finish_pe(pe)


def kernel(**inputs):
    import concourse.bacc as bacc
    from concourse.bass_utils import run_bass_kernel_spmd

    def frequencies(theta, pairs):
        return np.float32(theta) ** (-np.arange(pairs, dtype=np.float32) / np.float32(pairs))

    arrays = dict(inputs)
    arrays["inv24"] = np.concatenate([frequencies(500000.0, ROT), frequencies(500000.0, IROT)])[None, :]
    arrays["inv_t"] = np.tile(np.float32(1) / np.float32(10000.0) ** (
        np.arange(MR // 2, dtype=np.float32) / np.float32(MR // 2)), 4)[:, None]
    nc = bacc.Bacc("TRN2", target_bir_lowering=False, num_devices=1)
    given, aps = {}, {}
    for name, x in arrays.items():
        x = np.ascontiguousarray(x)
        given[f"in_{name}"] = x
        aps[name] = nc.dram_tensor(f"in_{name}", x.shape, mybir.dt.from_np(x.dtype), kind="ExternalInput").ap()
    out = nc.dram_tensor("out", (1, T, D), F32, kind="ExternalOutput").ap()
    build(nc, aps, out)
    return run_bass_kernel_spmd(nc, [given], core_ids=[0]).results[0]["out"]
```
